# Optimizing a Trainium2 kernel written in Bass

```python
import math
import jax, jax.numpy as jnp
from jax import lax
import numpy as np

D_MODEL = 1024
BATCH = 1
SEQ = 256
DEPTH = 1

ATTN_HEADS = 8
ATTN_HEAD_DIM = D_MODEL // ATTN_HEADS
ATTN_WIDTH = ATTN_HEADS * ATTN_HEAD_DIM
MOBA_BLOCK = 256
MOBA_TOPK = 3
MOBA_Q_CHUNK = 32
REL_BUCKETS = 32
REL_MAX_DIST = 1024
SSM_INNER = 2 * D_MODEL
SSM_HEAD_DIM = 64
SSM_HEADS = SSM_INNER // SSM_HEAD_DIM
SSM_GROUPS = 4
SSM_HEADS_PER_GROUP = SSM_HEADS // SSM_GROUPS
SSM_STATE = 128
SSM_CONV = 4
SSM_CHUNK = 256
SSM_CONV_DIM = SSM_INNER + 2 * SSM_GROUPS * SSM_STATE
MEM_LEN = 256
MEM_HEADS = 4
MEM_HEAD_DIM = D_MODEL // MEM_HEADS
MEM_WIDTH = MEM_HEADS * MEM_HEAD_DIM
N_BRANCHES = 3
FFN_HIDDEN = ((8 * D_MODEL // 3 + 255) // 256) * 256
FFN_CONV = 3
NORM_EPS = 1e-6
IN_SIZES = (ATTN_WIDTH, ATTN_WIDTH, ATTN_WIDTH, SSM_INNER, SSM_CONV_DIM, SSM_HEADS, MEM_WIDTH, N_BRANCHES * D_MODEL)
IN_WIDTH = ATTN_WIDTH * 3 + SSM_INNER + SSM_CONV_DIM + SSM_HEADS + MEM_WIDTH + N_BRANCHES * D_MODEL

kernel_name = 'hybrid_moba_ssd_memory_gated_block'

def rms_norm(x, g):
    xf = x.astype(jnp.float32)
    y = xf * lax.rsqrt(jnp.mean(xf * xf, axis=-1, keepdims=True) + NORM_EPS)
    return (y * g.astype(jnp.float32)).astype(x.dtype)

def gated_group_rms_norm(y, z, g):
    v = y.astype(jnp.float32) * jax.nn.silu(z.astype(jnp.float32))
    shp = v.shape
    v = v.reshape(shp[:-1] + (SSM_GROUPS, shp[-1] // SSM_GROUPS))
    v = v * lax.rsqrt(jnp.mean(v * v, axis=-1, keepdims=True) + NORM_EPS)
    return (v.reshape(shp) * g.astype(jnp.float32)).astype(z.dtype)

def causal_dwconv(x, w, b):
    k_w, c = w.shape
    y = lax.conv_general_dilated(x, w[:, None, :].astype(x.dtype), window_strides=(1,),
                                 padding=[(k_w - 1, 0)], dimension_numbers=('NWC', 'WIO', 'NWC'),
                                 feature_group_count=c)
    return y + b.astype(x.dtype)

def t5_bucket(dist):
    n = jnp.maximum(dist, 0)
    max_exact = REL_BUCKETS // 2
    nf = jnp.maximum(n, max_exact).astype(jnp.float32)
    large = max_exact + (jnp.log(nf / max_exact) / math.log(REL_MAX_DIST / max_exact)
                         * (REL_BUCKETS - max_exact)).astype(jnp.int32)
    large = jnp.minimum(large, REL_BUCKETS - 1)
    return jnp.where(n < max_exact, n, large)

def moba_attention(q, k, v, rel_bias):
    bsz, s_len, n_h, d_h = q.shape
    nb = -(-s_len // MOBA_BLOCK)
    s_pad = nb * MOBA_BLOCK
    pad = s_pad - s_len
    q, k, v = [jnp.pad(t, ((0, 0), (0, pad), (0, 0), (0, 0))).transpose(0, 2, 1, 3) for t in (q, k, v)]
    kb = k.reshape(bsz, n_h, nb, MOBA_BLOCK, d_h)
    vb = v.reshape(bsz, n_h, nb, MOBA_BLOCK, d_h)
    k_mean = jnp.mean(kb.astype(jnp.float32), axis=3)
    q_blk = jnp.arange(s_pad) // MOBA_BLOCK
    gate = jnp.einsum('bhsd,bhnd->bhsn', q.astype(jnp.float32), k_mean)
    fully_past = jnp.arange(nb)[None, :] < q_blk[:, None]
    gate = jnp.where(fully_past, gate, -jnp.inf)
    topk = min(MOBA_TOPK, nb)
    _, sel = lax.top_k(gate, topk)
    scale = d_h ** -0.5
    bias_tab = rel_bias.T
    b_idx = jnp.arange(bsz)[:, None, None]
    h_idx = jnp.arange(n_h)[None, :, None]
    j = jnp.arange(MOBA_BLOCK)

    def one_chunk(ci):
        start = ci * MOBA_Q_CHUNK
        q_c = lax.dynamic_slice_in_dim(q, start, MOBA_Q_CHUNK, axis=2).astype(jnp.float32) * scale
        sel_c = lax.dynamic_slice_in_dim(sel, start, MOBA_Q_CHUNK, axis=2)
        qpos = start + jnp.arange(MOBA_Q_CHUNK)
        own = start // MOBA_BLOCK
        valid = jnp.arange(topk) < own
        sel_flat = sel_c.reshape(bsz, n_h, MOBA_Q_CHUNK * topk)
        k_sel = kb[b_idx, h_idx, sel_flat].reshape(bsz, n_h, MOBA_Q_CHUNK, topk, MOBA_BLOCK, d_h)
        v_sel = vb[b_idx, h_idx, sel_flat].reshape(bsz, n_h, MOBA_Q_CHUNK, topk, MOBA_BLOCK, d_h)
        k_own = lax.dynamic_index_in_dim(kb, own, axis=2, keepdims=False)
        v_own = lax.dynamic_index_in_dim(vb, own, axis=2, keepdims=False)
        dist_sel = qpos[:, None, None] - (sel_c[..., None] * MOBA_BLOCK + j)
        bias_sel = bias_tab[h_idx[..., None, None], t5_bucket(dist_sel)]
        s_sel = jnp.einsum('bhqd,bhqkjd->bhqkj', q_c, k_sel.astype(jnp.float32)) + bias_sel
        s_sel = jnp.where(valid[:, None], s_sel, -jnp.inf)
        dist_own = qpos[:, None] - (own * MOBA_BLOCK + j)[None, :]
        s_own = jnp.einsum('bhqd,bhjd->bhqj', q_c, k_own.astype(jnp.float32)) + bias_tab[:, t5_bucket(dist_own)]
        s_own = jnp.where(dist_own >= 0, s_own, -jnp.inf)
        s_all = jnp.concatenate([s_sel.reshape(bsz, n_h, MOBA_Q_CHUNK, topk * MOBA_BLOCK), s_own], axis=-1)
        p = jax.nn.softmax(s_all, axis=-1)
        p_sel = p[..., :topk * MOBA_BLOCK].reshape(bsz, n_h, MOBA_Q_CHUNK, topk, MOBA_BLOCK)
        p_own = p[..., topk * MOBA_BLOCK:]
        o = (jnp.einsum('bhqkj,bhqkjd->bhqd', p_sel, v_sel.astype(jnp.float32))
             + jnp.einsum('bhqj,bhjd->bhqd', p_own, v_own.astype(jnp.float32)))
        return o.astype(v.dtype)

    out = lax.map(one_chunk, jnp.arange(s_pad // MOBA_Q_CHUNK))
    out = out.transpose(1, 0, 3, 2, 4).reshape(bsz, s_pad, n_h * d_h)
    return out[:, :s_len]

def ssd_chunked_scan(xh, dt, a_neg, bm, cm, d_skip):
    bsz, s_len = xh.shape[:2]
    L = SSM_CHUNK
    nc = -(-s_len // L)
    pad = nc * L - s_len
    xf = xh.astype(jnp.float32)

    def chunks(t, tail):
        t = jnp.pad(t, [(0, 0), (0, pad)] + [(0, 0)] * (t.ndim - 2))
        return jnp.moveaxis(t.reshape((bsz, nc, L) + tail), 1, 0)

    x_c = chunks(xf * dt[..., None], (SSM_GROUPS, SSM_HEADS_PER_GROUP, SSM_HEAD_DIM))
    a_c = chunks(dt * a_neg, (SSM_GROUPS, SSM_HEADS_PER_GROUP))
    b_c = chunks(bm.astype(jnp.float32), (SSM_GROUPS, SSM_STATE))
    c_c = chunks(cm.astype(jnp.float32), (SSM_GROUPS, SSM_STATE))
    causal = jnp.tril(jnp.ones((L, L), dtype=bool))

    def step(state, inp):
        xc, ac, bc, cc = inp
        acs = jnp.cumsum(ac, axis=1)
        seg = acs[:, :, None] - acs[:, None, :]
        decay = jnp.exp(jnp.where(causal[None, :, :, None, None], seg, -jnp.inf))
        cb = jnp.einsum('blgn,bsgn->blsg', cc, bc)
        y_diag = jnp.einsum('blsg,blsgh,bsghp->blghp', cb, decay, xc)
        y_off = jnp.einsum('blgn,bghpn->blghp', cc, state) * jnp.exp(acs)[..., None]
        decay_end = jnp.exp(acs[:, -1:] - acs)
        new_state = (state * jnp.exp(acs[:, -1])[..., None, None]
                     + jnp.einsum('bsgn,bsgh,bsghp->bghpn', bc, decay_end, xc))
        return new_state, y_diag + y_off

    state0 = jnp.zeros((bsz, SSM_GROUPS, SSM_HEADS_PER_GROUP, SSM_HEAD_DIM, SSM_STATE), jnp.float32)
    _, ys = lax.scan(step, state0, (x_c, a_c, b_c, c_c))
    y = jnp.moveaxis(ys, 0, 1).reshape(bsz, nc * L, SSM_HEADS, SSM_HEAD_DIM)[:, :s_len]
    return y + d_skip.astype(jnp.float32)[:, None] * xf

def memory_cross_attention(qm, mem, mem_norm_g, w_mem_kv):
    bsz, s_len = qm.shape[:2]
    kv = rms_norm(mem, mem_norm_g) @ w_mem_kv
    km, vm = jnp.split(kv, 2, axis=-1)
    km = km.reshape(bsz, -1, MEM_HEADS, MEM_HEAD_DIM).astype(jnp.float32)
    vm = vm.reshape(bsz, -1, MEM_HEADS, MEM_HEAD_DIM).astype(jnp.float32)
    s = jnp.einsum('bshd,bmhd->bhsm', qm.astype(jnp.float32) * MEM_HEAD_DIM ** -0.5, km)
    p = jax.nn.softmax(s, axis=-1)
    o = jnp.einsum('bhsm,bmhd->bshd', p, vm)
    return o.reshape(bsz, s_len, MEM_WIDTH).astype(qm.dtype)

def hybrid_layer(h, mem, rel_bias, mix_norm_g, w_in, b_gate, ssm_conv_w, ssm_conv_b, ssm_dt_bias,
                 ssm_A_log, ssm_D, ssm_norm_g, mem_norm_g, w_mem_kv, w_br_attn, w_br_ssm, w_br_mem,
                 w_out, ffn_norm_g, w_ffn_up, ffn_conv_w, ffn_conv_b, w_ffn_down):
    bsz, s_len, _ = h.shape
    u = rms_norm(h, mix_norm_g)
    proj = u @ w_in
    split_points = []
    acc = 0
    for sz in IN_SIZES[:-1]:
        acc += sz
        split_points.append(acc)
    q, k, v, z, xbc, dt_raw, qm, gate_logits = jnp.split(proj, split_points, axis=-1)

    hs = (bsz, s_len, ATTN_HEADS, ATTN_HEAD_DIM)
    o_attn = moba_attention(q.reshape(hs), k.reshape(hs), v.reshape(hs), rel_bias)

    xbc = jax.nn.silu(causal_dwconv(xbc, ssm_conv_w, ssm_conv_b))
    xs, bm, cm = jnp.split(xbc, [SSM_INNER, SSM_INNER + SSM_GROUPS * SSM_STATE], axis=-1)
    dt = jax.nn.softplus(dt_raw.astype(jnp.float32) + ssm_dt_bias.astype(jnp.float32))
    a_neg = -jnp.exp(ssm_A_log.astype(jnp.float32))
    y = ssd_chunked_scan(xs.reshape(bsz, s_len, SSM_HEADS, SSM_HEAD_DIM), dt, a_neg,
                         bm.reshape(bsz, s_len, SSM_GROUPS, SSM_STATE),
                         cm.reshape(bsz, s_len, SSM_GROUPS, SSM_STATE), ssm_D)
    o_ssm = gated_group_rms_norm(y.reshape(bsz, s_len, SSM_INNER), z, ssm_norm_g)

    o_mem = memory_cross_attention(qm.reshape(bsz, s_len, MEM_HEADS, MEM_HEAD_DIM), mem, mem_norm_g, w_mem_kv)

    gates = jax.nn.sigmoid((gate_logits + b_gate).reshape(bsz, s_len, N_BRANCHES, D_MODEL))
    merged = (gates[:, :, 0] * (o_attn @ w_br_attn) + gates[:, :, 1] * (o_ssm @ w_br_ssm)
              + gates[:, :, 2] * (o_mem @ w_br_mem))
    h = h + merged @ w_out

    hid = causal_dwconv(rms_norm(h, ffn_norm_g) @ w_ffn_up, ffn_conv_w, ffn_conv_b)
    g_ff, up = jnp.split(hid, 2, axis=-1)
    return h + (jax.nn.silu(g_ff) * up) @ w_ffn_down

def setup_inputs(seed: int = 0) -> dict:
    key = jax.random.key(seed)
    ks = jax.random.split(key, 24)
    f32 = jnp.float32

    def nrm(k, shape, scale):
        return jax.random.normal(k, shape, f32) * scale

    L = DEPTH
    D = D_MODEL
    F2 = 2 * FFN_HIDDEN
    dt0 = jnp.exp(jax.random.uniform(ks[8], (L, SSM_HEADS), f32, math.log(1e-3), math.log(1e-1)))
    return {
        'x': nrm(ks[0], (BATCH, SEQ, D), 1.0),
        'mem': nrm(ks[1], (BATCH, MEM_LEN, D), 1.0),
        'rel_bias': nrm(ks[2], (REL_BUCKETS, ATTN_HEADS), 0.3),
        'mix_norm_g': 1.0 + nrm(ks[3], (L, D), 0.05),
        'w_in': nrm(ks[4], (L, D, IN_WIDTH), D ** -0.5),
        'b_gate': nrm(ks[5], (L, N_BRANCHES * D), 0.1),
        'ssm_conv_w': nrm(ks[6], (L, SSM_CONV, SSM_CONV_DIM), SSM_CONV ** -0.5),
        'ssm_conv_b': nrm(ks[7], (L, SSM_CONV_DIM), 0.02),
        'ssm_dt_bias': dt0 + jnp.log(-jnp.expm1(-dt0)),
        'ssm_A_log': jnp.log(jax.random.uniform(ks[9], (L, SSM_HEADS), f32, 1.0, 16.0)),
        'ssm_D': 1.0 + nrm(ks[10], (L, SSM_HEADS), 0.1),
        'ssm_norm_g': 1.0 + nrm(ks[11], (L, SSM_INNER), 0.05),
        'mem_norm_g': 1.0 + nrm(ks[12], (L, D), 0.05),
        'w_mem_kv': nrm(ks[13], (L, D, 2 * MEM_WIDTH), D ** -0.5),
        'w_br_attn': nrm(ks[14], (L, ATTN_WIDTH, D), ATTN_WIDTH ** -0.5),
        'w_br_ssm': nrm(ks[15], (L, SSM_INNER, D), SSM_INNER ** -0.5),
        'w_br_mem': nrm(ks[16], (L, MEM_WIDTH, D), MEM_WIDTH ** -0.5),
        'w_out': nrm(ks[17], (L, D, D), D ** -0.5),
        'ffn_norm_g': 1.0 + nrm(ks[18], (L, D), 0.05),
        'w_ffn_up': nrm(ks[19], (L, D, F2), D ** -0.5),
        'ffn_conv_w': nrm(ks[20], (L, FFN_CONV, F2), FFN_CONV ** -0.5),
        'ffn_conv_b': nrm(ks[21], (L, F2), 0.02),
        'w_ffn_down': nrm(ks[22], (L, FFN_HIDDEN, D), FFN_HIDDEN ** -0.5),
        'final_norm_g': 1.0 + nrm(ks[23], (D,), 0.05),
    }

def reference(x, mem, rel_bias, mix_norm_g, w_in, b_gate, ssm_conv_w, ssm_conv_b, ssm_dt_bias, ssm_A_log,
              ssm_D, ssm_norm_g, mem_norm_g, w_mem_kv, w_br_attn, w_br_ssm, w_br_mem, w_out, ffn_norm_g,
              w_ffn_up, ffn_conv_w, ffn_conv_b, w_ffn_down, final_norm_g):
    h = x
    for l in range(DEPTH):
        h = hybrid_layer(h, mem, rel_bias, mix_norm_g[l], w_in[l], b_gate[l], ssm_conv_w[l], ssm_conv_b[l],
                         ssm_dt_bias[l], ssm_A_log[l], ssm_D[l], ssm_norm_g[l], mem_norm_g[l], w_mem_kv[l],
                         w_br_attn[l], w_br_ssm[l], w_br_mem[l], w_out[l], ffn_norm_g[l], w_ffn_up[l],
                         ffn_conv_w[l], ffn_conv_b[l], w_ffn_down[l])
    return rms_norm(h, final_norm_g)


_drawn_inputs = setup_inputs


def setup_inputs(seed=0):
    import zlib

    import numpy as np

    out = dict(_drawn_inputs(seed))
    spreads = {}
    factors = {'b_gate': 2.681,
     'ssm_conv_b': 12.764,
     'mem_norm_g': 8.0,
     'ffn_conv_b': 11.756,
     'rel_bias': 7.014,
     'ssm_D': 4.634,
     'ssm_norm_g': 7.461,
     'ffn_norm_g': 4.865}
    for name, (base, spread) in spreads.items():
        noise = np.random.default_rng([zlib.crc32(name.encode()), seed]).standard_normal(out[name].shape)
        drawn = base * np.exp(spread * noise) if base else spread * noise
        out[name] = __import__('jax').numpy.asarray(drawn.astype(out[name].dtype))
    for name, factor in factors.items():
        out[name] = (out[name] * factor).astype(out[name].dtype)
    return out
```

```python
import numpy as np

import concourse.bass as bass
from concourse import mybir

F32 = mybir.dt.float32
F32R = mybir.dt.float32r
ALU = mybir.AluOpType
ACT = mybir.ActivationFunctionType
AX = mybir.AxisListType.X

P = 128
KB = 1024
EPS = 1e-6
MASKED = -1e30

D = 1024
T = 256
NT = T // P
KT = D // P
HEADS, DH = 8, 128
BUCKETS, MAX_DIST = 32, 1024
SSM = 2 * D
SHD = 64
SHEADS = SSM // SHD
GROUPS, STATE = 4, 128
HPG = SHEADS // GROUPS
GC = SSM // GROUPS
GT = GC // P
TAPS = 4
CONV_T = (SSM + 2 * GROUPS * STATE) // P
MHEADS, MDH = 4, 256
FFN = 2816
FTAPS = 3
FT = FFN // P
F_STEPS = FFN // 256
QC, KC, VC = 0, D, 2 * D
ZC = 3 * D
XC = ZC + SSM
BC = XC + SSM
CC = BC + GROUPS * STATE
DTC = CC + GROUPS * STATE
QMC = DTC + SHEADS
GATEC = QMC + D

SLOTS = 3
CW = 256
CHUNK = KT * CW
LAG = 2 * P - 1
BIAS_W = 3 * P
RA, RB, RC, RD, RE, RF, RG = 0, 8, 12, 16, 20, 24, 26


def constants():
    p, c = np.arange(P)[:, None], np.arange(P)[None, :]
    upper = (c >= p).astype(np.float32)
    ones = np.ones((P, P), np.float32)
    square = np.concatenate([np.eye(P, dtype=np.float32), upper, ones, upper, ones], axis=1)
    dist = LAG - np.arange(BIAS_W)
    n = np.maximum(dist, 0)
    half = BUCKETS // 2
    far = np.maximum(n, half).astype(np.float32)
    large = half + (np.log(far / np.float32(half)) / np.float32(np.log(MAX_DIST / half))
                    * np.float32(BUCKETS - half)).astype(np.int32)
    bucket = np.where(n < half, n, np.minimum(large, BUCKETS - 1))
    table = np.zeros((BUCKETS + 1, BIAS_W), np.float32)
    table[:BUCKETS] = bucket[None, :] == np.arange(BUCKETS)[:, None]
    table[BUCKETS] = np.where(dist < 0, np.float32(MASKED), np.float32(0))
    return square, table, np.ones((1, HEADS), np.float32)


def build(nc, x, mem, rel_bias, mix_norm_g, w_in, b_gate, ssm_conv_w, ssm_conv_b, ssm_dt_bias, ssm_A_log, ssm_D,
          ssm_norm_g, mem_norm_g, w_mem_kv, w_br_attn, w_br_ssm, w_br_mem, w_out, ffn_norm_g, w_ffn_up, ffn_conv_w,
          ffn_conv_b, w_ffn_down, final_norm_g, square, table, one_row, out):
    base = -(-nc.sbuf_base // 64) * 64

    def place(name, at, shape, dtype=F32):
        return nc.alloc_sbuf_tensor_at(name, [P, *shape], dtype, offset=base + int(at * KB))

    w_raw = place("w_raw", 0, [SLOTS, CHUNK])
    w_hi = place("w_hi", 24, [SLOTS, CHUNK], F32R)
    w_lo = place("w_lo", 48, [SLOTS, CHUNK], F32R)
    tok_hi = place("tok_hi", 72, [KT, T], F32R)
    tok_lo = place("tok_lo", 80, [KT, T], F32R)
    sq = place("square_c", 88, [5 * P])
    ident, tri_wide, ones = sq[:, 0:P], sq[:, P:3 * P], sq[:, 4 * P:5 * P]
    cb_mask = sq[:, P:4 * P]
    table_s = place("table_s", 90.5, [BIAS_W])
    relb = place("relb", 92, [HEADS])
    rows_conv = place("rows_conv", 92.5, [P])
    rows_gate = place("rows_gate", 93, [P])
    rows_skip = place("rows_skip", 93.5, [P])
    rows_up01 = place("rows_up01", 94, [P])
    rows_up2 = place("rows_up2", 94.5, [P])
    n_conv, n_gate, n_skip, n_up01, n_up2 = (TAPS + 1) * CONV_T, 3 * KT + SSM // P, SSM // P, 2 * 2 * FT, 2 * 2 * FT
    cols_conv = place("cols_conv", 95, [TAPS + 1, CONV_T])
    cols_gate = place("cols_gate", 95.5, [n_gate])
    cols_skip = place("cols_skip", 95.75, [n_skip])
    cols_up = place("cols_up", 96, [4, 2 * FT])
    skip2 = place("skip2", 96.75, [2])
    dt_rows = place("dt_rows", 96.875, [2, SHEADS])
    stat = place("stat", 97.25, [NT * 4])
    pow_c = place("pow_c", 97.3125, [NT])
    eps_c = place("eps_c", 97.34375, [1])
    soft = place("soft", 97.375, [4, 4])
    msoft = place("msoft", 97.4375, [4, NT])
    a_neg = place("a_neg", 97.5, [SHEADS])
    dt_s = place("dt_s", 97.75, [NT, SHEADS])
    acs_s = place("acs_s", 98, [NT, SHEADS])
    dt_w = [place(f"dt_w{i}", 98.25 + 0.25 * i, [NT, SHEADS]) for i in range(6)]
    da_s = place("da_s", 99.75, [NT, SHEADS])
    R = 100
    g1 = place("g1", R + 0, [KT, T])
    v_ssm = place("v_ssm", R + 8, [GROUPS * GT, T])
    om_hi = place("om_hi", R + 8, [KT, T], F32R)
    om_lo = place("om_lo", R + 16, [KT, T], F32R)
    os_hi = place("os_hi", R + 24, [2 * KT, T], F32R)
    os_lo = place("os_lo", R + 40, [2 * KT, T], F32R)
    mg_hi = place("mg_hi", R + 24, [KT, T], F32R)
    mg_lo = place("mg_lo", R + 32, [KT, T], F32R)
    oa_hi = place("oa_hi", R + 56, [KT, T], F32R)
    oa_lo = place("oa_lo", R + 64, [KT, T], F32R)
    me_hi = place("me_hi", R + 72, [KT, T], F32R)
    me_lo = place("me_lo", R + 80, [KT, T], F32R)
    merged = place("merged", R + 72, [KT, T])
    g0 = place("g0", R + 80, [KT, T])
    x_nat = place("x_nat", R + 24, [NT, D])
    x_sc = place("x_sc", R + 32, [NT, D])
    gain_mix = place("gain_mix", R + 40, [D])
    wdt_raw = place("wdt_raw", R + 8, [KT, P])
    wdt_hi = place("wdt_hi", R + 12, [KT, P], F32R)
    wdt_lo = place("wdt_lo", R + 16, [KT, P], F32R)
    dt_raw = place("dt_raw", R + 20, [T])
    acs_row = place("acs_row", R + 21, [T])
    bias_row = place("bias_row", R + 22, [BIAS_W])
    acs_b = place("acs_b", R + 24, [SHEADS, T])
    decay = place("decay", R + 56, [HPG, 3 * P])
    pad_x = place("pad_x", R + 68, [SLOTS, 2, TAPS - 1 + T])
    conv_a = place("conv_a", R + 75, [SLOTS, 2, T])
    tanh_a = place("tanh_a", R + 81, [SLOTS, 2, T])
    conv_o = place("conv_o", R + 87, [6, T])
    x_dt = place("x_dt", R + 93, [NT, GC])
    z_act = place("z_act", R + 97, [GT, T])
    y_sum = place("y_sum", R + 101, [GT, T])
    sq_v = place("sq_v", R + 105, [GT, T])
    sq_h = place("sq_h", R + 109, [2, T])
    sq_g = place("sq_g", R + 111, [GROUPS, T])
    cb = place("cb", R + 115, [3 * P])
    junk_m = place("junk_m", R + 112, [NT, D])
    prob = place("prob", R + 72, [2, 3 * P])
    prob_t = place("prob_t", R + 75, [2, 3 * P])
    rstd_g = place("rstd_g", R + 82, [GROUPS, T])
    bias_t = place("bias_t", R + 88, [HEADS, 3 * P])
    mem_nat = place("mem_nat", R + 100, [NT, D])
    gain_mem = place("gain_mem", R + 108, [D])
    o_tmp = place("o_tmp", R + 112, [GT, T])
    k_t = place("k_t", R + 116, [2, T])
    q_t = place("q_t", R + 118, [2, T])
    v_t = place("v_t", R + 120, [NT, 2 * DH])
    qm_t = place("qm_t", R + 88, [2, T])
    km_t = place("km_t", R + 90, [2, T])
    vm_t = place("vm_t", R + 92, [NT, MDH])
    mprob = place("mprob", R + 94, [NT, T])
    mprob_t = place("mprob_t", R + 96, [NT, T])
    tanh_d = place("tanh_d", R + 88, [2, T])
    e_attn = place("e_attn", R + 90, [2, T])
    tanh_e = place("tanh_e", R + 92, [2, T])
    e_gate = place("e_gate", R + 94, [2, T])
    e_mem = place("e_mem", R + 96, [2, T])
    e_sum = place("e_sum", R + 98, [2, T])
    h_nat = place("h_nat", R + 100, [NT, D])
    h_sc = place("h_sc", R + 108, [NT, D])
    gain_ffn = place("gain_ffn", R + 40, [D])
    gain_fin = place("gain_fin", R + 44, [D])
    pad_g = place("pad_g", R + 0, [2, FTAPS - 1 + T])
    pad_u = place("pad_u", R + 2.25, [2, FTAPS - 1 + T])
    conv_g = place("conv_g", R + 4.5, [2, T])
    conv_u = place("conv_u", R + 6.5, [2, T])
    tanh_g = place("tanh_g", R + 8.5, [2, T])
    silu_g = place("silu_g", R + 10.5, [2, T])
    hid = place("hid", R + 12.5, [2, T])
    hid_hi = place("hid_hi", R + 14.5, [2, T], F32R)
    hid_lo = place("hid_lo", R + 16.5, [2, T], F32R)
    zero_s = place("zero_s", R + 18.5, [512])

    ps = nc.alloc_psum_tensor("ps", [P, 8, 512], F32)

    acs_d = nc.dram_tensor("acs_d", (SHEADS, T), F32, kind="Internal").ap()
    bias_d = nc.dram_tensor("bias_d", (HEADS, P, BIAS_W), F32, kind="Internal").ap()


    sem = nc.alloc_semaphore
    loaded, hi_ready, lo_ready, gemm_done, bank_free = (
        [sem(f"{n}{s}") for s in range(SLOTS)] for n in ("loaded", "hi_ready", "lo_ready", "gemm_done", "bank_free"))
    x_in, gain_in, const_in, rows_in, dtw_in, dtp_in, relb_in, skip_in = map(
        sem, ("x_in", "gain_in", "const_in", "rows_in", "dtw_in", "dtp_in", "relb_in", "skip_in"))
    eps_set, pow_set, skip_row = sem("eps_set"), sem("pow_set"), sem("skip_row")
    rows_turned, params_ready = sem("rows_turned"), sem("params_ready")
    x_sumsq, x_var, x_rstd, x_scaled, x_turned, x_hi, x_lo = map(
        sem, ("x_sumsq", "x_var", "x_rstd", "x_scaled", "x_turned", "x_hi", "x_lo"))
    wdt_hi_s, wdt_lo_s, dt_mm, dt_copied, dt_turned, dt_exp, dt_step, a_exp = map(
        sem, ("wdt_hi_s", "wdt_lo_s", "dt_mm", "dt_copied", "dt_turned", "dt_exp", "dt_step", "a_exp"))
    acs_mm, acs_ready, acs_out, acs_in = map(sem, ("acs_mm", "acs_ready", "acs_out", "acs_in"))
    bias_mm, bias_copied, bias_out, bias_in = map(sem, ("bias_mm", "bias_copied", "bias_out", "bias_in"))
    conv_step, conv_tanh, conv_done, seg_ready, seg_clamped, decay_ready, decay_cb = map(
        sem, ("conv_step", "conv_tanh", "conv_done", "seg_ready", "seg_clamped", "decay_ready", "decay_cb"))
    xg_turned, cb_mm, cb_masked, xdt_ready, y_mm, z_tanh, z_ready = map(
        sem, ("xg_turned", "cb_mm", "cb_masked", "xdt_ready", "y_mm", "z_tanh", "z_ready"))
    y_step, v_ready, sq_step, g1_ready = map(sem, ("y_step", "v_ready", "sq_step", "g1_ready"))
    var_mm, var_sqrt, var_ready = map(sem, ("var_mm", "var_sqrt", "var_ready"))
    s_mm, s_biased, s_max, s_neg, p_exp, p_rec, p_norm, p_turned, pt_ready, o_mm, oa_hi_s, oa_lo_s = map(
        sem, ("s_mm", "s_biased", "s_max", "s_neg", "p_exp", "p_rec", "p_norm", "p_turned", "pt_ready", "o_mm",
              "oa_hi_s", "oa_lo_s"))
    norm_step, os_hi_s, os_lo_s = map(sem, ("norm_step", "os_hi_s", "os_lo_s"))
    m_in, m_gain_in, m_sumsq, m_var, m_rstd, m_scaled, m_turned, m_hi, m_lo = map(
        sem, ("m_in", "m_gain_in", "m_sumsq", "m_var", "m_rstd", "m_scaled", "m_turned", "m_hi", "m_lo"))
    ms_mm, ms_max, ms_neg, mp_exp, mp_rec, mp_norm, mp_turned, mpt_ready, mo_mm, om_hi_s, om_lo_s = map(
        sem, ("ms_mm", "ms_max", "ms_neg", "mp_exp", "mp_rec", "mp_norm", "mp_turned", "mpt_ready", "mo_mm",
              "om_hi_s", "om_lo_s"))
    g0_ready, e_step, e_summed, mg_hi_s, mg_lo_s = map(
        sem, ("g0_ready", "e_step", "e_summed", "mg_hi_s", "mg_lo_s"))
    x_again, late_gains, h_sumsq, h_var, h_rstd, h_scaled, h_turned, h_hi, h_lo = map(
        sem, ("x_again", "late_gains", "h_sumsq", "h_var", "h_rstd", "h_scaled", "h_turned", "h_hi", "h_lo"))
    f_zero, f_step, g_tanh, g_silu, hid_done, hid_hi_s, hid_lo_s = map(
        sem, ("f_zero", "f_step", "g_tanh", "g_silu", "hid_done", "hid_hi_s", "hid_lo_s"))
    y_added, y_sumsq, y_var, y_rstd, y_scaled, y_out = map(
        sem, ("y_added", "y_sumsq", "y_var", "y_rstd", "y_scaled", "y_out"))

    def load(sp, r, s, w, col):
        sp.wait_ge(lo_ready[s], r + 1)
        src = w[:, bass.ds(col, CW)].rearrange("(k p) n -> p k n", p=P)
        dst = w_raw[:, s, :].rearrange("p (k n) -> p k n", k=KT)
        for half in (slice(KT // 2, KT), slice(0, KT // 2)):
            sp.dma_start(dst[:, half, :], src[:, half, :]).then_inc(loaded[s], 16)

    def load_bc(sp, r, g):
        sp.wait_ge(lo_ready[0], r + 1)
        dst = w_raw[:, 0, :].rearrange("p (k n) -> p k n", k=KT)
        for j, col in enumerate((BC, CC)):
            src = w_in[0][:, bass.ds(col + STATE * g, STATE)].rearrange("(k p) n -> p k n", p=P)
            sp.dma_start(dst[:, :, j * P:(j + 1) * P], src).then_inc(loaded[0], 16)

    def load_down(sp, r, s, f):
        sp.wait_ge(lo_ready[s], r + 1)
        src = w_ffn_down[0][bass.ds(2 * P * f, 2 * P), :].rearrange("(k p) n -> p k n", p=P)
        dst = w_raw[:, s, :].rearrange("p (k n) -> p k n", k=2)
        for k in range(2):
            sp.dma_start(dst[:, k, :], src[:, k, :]).then_inc(loaded[s], 16)

    def split_hi(act, r, s, first=False):
        act.wait_ge(loaded[s], 32 * (r + 1))
        if not first:
            act.wait_ge(gemm_done[s], r)
        act.activation(w_hi[:, s, :], w_raw[:, s, :], ACT.Copy).then_inc(hi_ready[s], 1)

    def split_lo(dve, r, s):
        dve.wait_ge(hi_ready[s], r + 1)
        dve.tensor_tensor(w_lo[:, s, :], w_raw[:, s, :], w_hi[:, s, :].bitcast(F32),
                          ALU.subtract).then_inc(lo_ready[s], 1)

    def gemm_cols(pe, r, s, hi, lo, k0=0, banks=None, free=None, start=True, stop=True):
        pe.wait_ge(lo_ready[s], r + 2)
        for b in [s] if free is None else free:
            pe.wait_ge(bank_free[b], r + 1)
        for j in range(2):
            o = ps[:, s, j * T:(j + 1) * T] if banks is None else ps[:, banks[j], 0:T]
            for k in range(KT):
                w0 = k * CW + j * P
                wh, wl = w_hi[:, s, w0:w0 + P], w_lo[:, s, w0:w0 + P]
                pe.matmul(o, wh, hi[:, k0 + k, :], start=start and k == 0, stop=False)
                pe.matmul(o, wh, lo[:, k0 + k, :], start=False, stop=False)
                mm = pe.matmul(o, wl, hi[:, k0 + k, :], start=False, stop=stop and k == KT - 1)
        mm.then_inc(gemm_done[s], 1)

    def gemm_rows(pe, r, s, hi, lo):
        pe.wait_ge(lo_ready[s], r + 2)
        pe.wait_ge(bank_free[s], r + 1)
        for t in range(NT):
            o = ps[:, s, t * CW:(t + 1) * CW]
            for k in range(KT):
                ah, al = hi[:, k, t * P:(t + 1) * P], lo[:, k, t * P:(t + 1) * P]
                wh, wl = w_hi[:, s, k * CW:(k + 1) * CW], w_lo[:, s, k * CW:(k + 1) * CW]
                pe.matmul(o, ah, wh, start=k == 0, stop=False)
                pe.matmul(o, ah, wl, start=False, stop=False)
                mm = pe.matmul(o, al, wh, start=False, stop=k == KT - 1)
        mm.then_inc(gemm_done[s], 1)

    def gemm_down(pe, r, s):
        pe.wait_ge(lo_ready[s], r + 2)
        for k in range(2):
            for t in range(NT):
                ah, al = hid_hi[:, k, t * P:(t + 1) * P], hid_lo[:, k, t * P:(t + 1) * P]
                for half in range(2):
                    w0 = k * D + half * 512
                    o = ps[:, 4 + 2 * t + half, :]
                    for a, w in ((ah, w_hi), (ah, w_lo), (al, w_hi)):
                        mm = pe.matmul(o, a, w[:, s, w0:w0 + 512], start=False, stop=False, skip_group_check=True)
        mm.then_inc(gemm_done[s], 1)

    def turn_tokens(pe, src, bank0, done):
        for k in range(KT):
            for t in range(NT):
                o = (k % 2) * T + t * P
                mm = pe.transpose(ps[:, bank0 + k // 2, o:o + P], src[:, t, k * P:(k + 1) * P], ident)
            if k % 2:
                mm.then_inc(done, 1)

    def halves(b):
        return ps[:, b, :].rearrange("p (a n) -> p a n", a=2)

    def on_all(v, n):
        return v.rearrange("(a d) -> a d", a=1).to_broadcast([P, n])

    def rows(v):
        return v.rearrange("(c p) -> c p", p=P)

    def conv_tile(s, j, g):
        return GROUPS * GT + GROUPS * j + g if s == 0 else GT * g + 2 * (s - 1) + j

    def gate_tanh(act, dst, s, col):
        for j in range(2):
            a = act.activation(dst[:, j, :], ps[:, s, j * T:(j + 1) * T], ACT.Tanh,
                               bias=cols_gate[:, bass.ds(col + j, 1)], scale=0.5)
        a.then_inc(bank_free[s], 1)

    with nc.Block() as block:
        @block.sync
        def _(sp):
            wi = w_in[0]
            sp.dma_start(x_nat[:], x[0].rearrange("(t p) d -> p t d", p=P)).then_inc(x_in, 16)
            sp.dma_start(gain_mix[:], on_all(mix_norm_g[0], D)).then_inc(gain_in, 16)
            sp.dma_start(sq[:], square).then_inc(const_in, 16)
            sp.dma_start(wdt_raw[:], wi[:, DTC:DTC + P].rearrange("(k p) n -> p k n", p=P)).then_inc(dtw_in, 16)
            with sp.Fori(0, GROUPS) as g:
                r = 2 * g
                load_bc(sp, r, g)
                load(sp, r, 1, wi, XC + GC * g)
                load(sp, r, 2, wi, XC + CW + GC * g)
                load(sp, r + 1, 0, wi, ZC + GC * g)
                load(sp, r + 1, 1, wi, ZC + CW + GC * g)
                load(sp, r + 1, 2, wi, GATEC + D + CW * g)
            with sp.Fori(0, 4) as i:
                load(sp, RB + i, 0, wi, KC + CW * i)
                load(sp, RB + i, 1, wi, QC + CW * i)
                load(sp, RB + i, 2, wi, VC + CW * i)
            with sp.Fori(0, 4) as i:
                load(sp, RC + i, 0, wi, QMC + CW * i)
                load(sp, RC + i, 1, w_mem_kv[0], CW * i)
                load(sp, RC + i, 2, w_mem_kv[0], D + CW * i)
            with sp.Fori(0, 4) as i:
                load(sp, RD + i, 0, w_br_ssm[0, 0:D], CW * i)
                load(sp, RD + i, 1, w_br_ssm[0, D:2 * D], CW * i)
                load(sp, RD + i, 2, wi, GATEC + CW * i)
            sp.wait_ge(m_scaled, NT)
            sp.dma_start(h_nat[:], x[0].rearrange("(t p) d -> p t d", p=P)).then_inc(x_again, 16)
            with sp.Fori(0, 4) as i:
                load(sp, RE + i, 0, w_br_attn[0], CW * i)
                load(sp, RE + i, 1, wi, GATEC + 2 * D + CW * i)
                load(sp, RE + i, 2, w_br_mem[0], CW * i)
            for c in range(3):
                load(sp, RF, c, w_out[0], CW * c)
            sp.wait_ge(gemm_done[1], RE)
            sp.dma_start(gain_ffn[:], on_all(ffn_norm_g[0], D)).then_inc(late_gains, 16)
            sp.dma_start(gain_fin[:], on_all(final_norm_g, D)).then_inc(late_gains, 16)
            load(sp, RF + 1, 0, w_out[0], CW * 3)
            load(sp, RF + 1, 1, w_ffn_up[0], 0)
            load(sp, RF + 1, 2, w_ffn_up[0], FFN)
            with sp.Fori(1, F_STEPS) as f:
                r = f + (RG - 1)
                load(sp, r, 0, w_ffn_up[0], CW * f)
                load(sp, r, 1, w_ffn_up[0], FFN + CW * f)
                load_down(sp, r, 2, f - 1)
            load_down(sp, RG + F_STEPS - 1, 0, F_STEPS - 1)
            for t in range(NT):
                sp.wait_ge(y_scaled, t + 1)
                sp.dma_start(out[0, t * P:(t + 1) * P, :], h_sc[:, t, :]).then_inc(y_out, 16)
            sp.wait_ge(y_out, 16 * NT)

        @block.tensor
        def _(pe):
            pe.wait_ge(const_in, 16)
            pe.wait_ge(rows_in, 16 * 7)
            pe.wait_ge(skip_row, 1)
            at = 0
            for src, n in ((rows_conv, n_conv), (rows_gate, n_gate), (rows_skip, n_skip), (rows_up01, n_up01),
                           (rows_up2, n_up2)):
                mm = pe.transpose(ps[:, 3, at:at + n], src[0:n, :], ident[0:n, 0:n])
                at += n
            mm.then_inc(rows_turned, 1)
            pe.wait_ge(x_scaled, NT)
            turn_tokens(pe, x_sc, 4, x_turned)
            pe.wait_ge(relb_in, 48)
            pe.matmul(ps[0:HEADS, 0, 0:BIAS_W], relb[0:BUCKETS + 1, :], table_s[0:BUCKETS + 1, :],
                      start=True, stop=True).then_inc(bias_mm, 1)
            pe.wait_ge(x_lo, KT // 2)
            pe.wait_ge(wdt_lo_s, 1)
            for k in range(KT):
                for n, (w, a) in enumerate(((wdt_hi, tok_hi), (wdt_hi, tok_lo), (wdt_lo, tok_hi))):
                    mm = pe.matmul(ps[:, 1, 0:T], w[:, k, :], a[:, k, :], start=k == 0 and n == 0,
                                   stop=k == KT - 1 and n == 2)
            mm.then_inc(dt_mm, 1)
            pe.wait_ge(dt_copied, 1)
            for t in range(NT):
                mm = pe.transpose(ps[:, 2, t * SHEADS:(t + 1) * SHEADS], dt_raw[0:SHEADS, t * P:(t + 1) * P],
                                  ident[0:SHEADS, 0:SHEADS])
            mm.then_inc(dt_turned, 1)
            pe.wait_ge(dt_step, 19)
            pe.matmul(ps[:, 4, 0:SHEADS], tri_wide[:, 0:P], da_s[:, 0, :], start=True, stop=True)
            pe.matmul(ps[:, 4, SHEADS:2 * SHEADS], tri_wide[:, P:2 * P], da_s[:, 0, :], start=True, stop=False)
            pe.matmul(ps[:, 4, SHEADS:2 * SHEADS], tri_wide[:, 0:P], da_s[:, 1, :], start=False, stop=True)
            pe.matmul(ps[0:SHEADS, 5, 0:T], da_s[:, 0, :], tri_wide[:, 0:T], start=True, stop=False)
            pe.matmul(ps[0:SHEADS, 5, P:T], da_s[:, 1, :], tri_wide[:, 0:P], start=False,
                      stop=True).then_inc(acs_mm, 1)

            with pe.Fori(0, GROUPS) as g:
                r = 2 * g
                for s in range(SLOTS):
                    gemm_cols(pe, r, s, tok_hi, tok_lo)
                gemm_cols(pe, r + 1, 0, tok_hi, tok_lo)
                pe.wait_ge(conv_done, 3 * g + 3)
                for t in range(NT):
                    for c in range(GT):
                        mm = pe.transpose(ps[:, 3 + t, c * P:(c + 1) * P], conv_o[:, 2 + c, t * P:(t + 1) * P], ident)
                mm.then_inc(xg_turned, 1)
                pe.matmul(ps[:, 5, 0:T], conv_o[:, 0, 0:P], conv_o[:, 1, :], start=True, stop=True)
                pe.matmul(ps[:, 5, T:T + P], conv_o[:, 0, P:T], conv_o[:, 1, P:T], start=True,
                          stop=True).then_inc(cb_mm, 1)
                gemm_cols(pe, r + 1, 1, tok_hi, tok_lo)
                pe.wait_ge(xdt_ready, 2 * g + 2)
                pe.wait_ge(decay_cb, g + 1)
                for h in range(HPG):
                    half, n = SHD * (h % 2), h // 2
                    o = ps[half:half + SHD, 6 + n // 2, (n % 2) * T:(n % 2 + 1) * T]
                    pe.matmul(o, x_dt[:, 0, h * SHD:(h + 1) * SHD], decay[:, h, 0:T], start=True, stop=False)
                    mm = pe.matmul(o[:, P:T], x_dt[:, 1, h * SHD:(h + 1) * SHD], decay[:, h, T:T + P], start=False,
                                   stop=True)
                mm.then_inc(y_mm, 1)
                gemm_cols(pe, r + 1, 2, tok_hi, tok_lo)
            pe.wait_ge(sq_step, 3 * GROUPS)
            for j in range(2):
                mm = pe.matmul(ps[:, 3 + j, :], ones, sq_g[:, 2 * j:2 * j + 2, :].rearrange("p a n -> p (a n)"),
                               start=True, stop=True)
            mm.then_inc(var_mm, 1)

            with pe.Fori(0, 4) as i:
                r = RB + i
                gemm_cols(pe, r, 0, tok_hi, tok_lo)
                gemm_cols(pe, r, 1, tok_hi, tok_lo)
                pe.wait_ge(bank_free[0], r + 2)
                pe.wait_ge(bank_free[1], r + 2)
                for a in range(2):
                    pe.matmul(ps[:, 3 + a, 0:P], q_t[:, a, 0:P], k_t[:, a, 0:P], start=True, stop=True)
                    mm = pe.matmul(ps[:, 3 + a, P:3 * P], q_t[:, a, P:T], k_t[:, a, :], start=True, stop=True)
                mm.then_inc(s_mm, 1)
                gemm_rows(pe, r, 2, tok_hi, tok_lo)
                pe.wait_ge(p_norm, 4 * i + 4)
                for a in range(2):
                    for n in range(3):
                        mm = pe.transpose(ps[:, 5 + a, n * P:(n + 1) * P], prob[:, a, n * P:(n + 1) * P], ident)
                    mm.then_inc(p_turned, 1)
                pe.wait_ge(bank_free[2], r + 2)
                pe.wait_ge(pt_ready, 2 * i + 2)
                for a in range(2):
                    pe.matmul(ps[:, 7, a * T:(a + 1) * T], v_t[:, 0, a * DH:(a + 1) * DH], prob_t[:, a, 0:T],
                              start=True, stop=False)
                    mm = pe.matmul(ps[:, 7, a * T + P:(a + 1) * T], v_t[:, 1, a * DH:(a + 1) * DH],
                                   prob_t[:, a, T:T + P], start=False, stop=True)
                mm.then_inc(o_mm, 1)
            pe.wait_ge(m_scaled, NT)
            turn_tokens(pe, mem_nat, 3, m_turned)

            with pe.Fori(0, 4) as i:
                r = RC + i
                gemm_cols(pe, r, 0, tok_hi, tok_lo)
                pe.wait_ge(m_lo, KT // 2)
                gemm_cols(pe, r, 1, me_hi, me_lo)
                pe.wait_ge(bank_free[0], r + 2)
                pe.wait_ge(bank_free[1], r + 2)
                for t in range(NT):
                    for d in range(2):
                        mm = pe.matmul(ps[:, 3, t * T:(t + 1) * T], qm_t[:, d, t * P:(t + 1) * P], km_t[:, d, :],
                                       start=d == 0, stop=d == 1)
                mm.then_inc(ms_mm, 1)
                gemm_rows(pe, r, 2, me_hi, me_lo)
                pe.wait_ge(mp_norm, 2 * i + 2)
                for m in range(2):
                    for t in range(NT):
                        mm = pe.transpose(ps[:, 4, m * T + t * P:m * T + (t + 1) * P], mprob[:, t, m * P:(m + 1) * P],
                                          ident)
                mm.then_inc(mp_turned, 1)
                pe.wait_ge(bank_free[2], r + 2)
                pe.wait_ge(mpt_ready, i + 1)
                for d in range(2):
                    for m in range(2):
                        mm = pe.matmul(ps[:, 5, d * T:(d + 1) * T], vm_t[:, m, d * P:(d + 1) * P], mprob_t[:, m, :],
                                       start=m == 0, stop=m == 1)
                mm.then_inc(mo_mm, 1)

            pe.wait_ge(os_lo_s, GROUPS)
            with pe.Fori(0, 4) as i:
                r = RD + i
                gemm_cols(pe, r, 0, os_hi, os_lo, 0, (0, 1), (0, 1), stop=False)
                gemm_cols(pe, r, 1, os_hi, os_lo, KT, (0, 1), (), start=False)
                gemm_cols(pe, r, 2, tok_hi, tok_lo)

            pe.wait_ge(oa_lo_s, 4)
            pe.wait_ge(om_lo_s, 4)
            with pe.Fori(0, 4) as i:
                r = RE + i
                gemm_cols(pe, r, 0, oa_hi, oa_lo)
                gemm_cols(pe, r, 1, tok_hi, tok_lo)
                gemm_cols(pe, r, 2, om_hi, om_lo)

            pe.wait_ge(mg_lo_s, 4)
            for c in range(4):
                gemm_rows(pe, RF + c // SLOTS, c % SLOTS, mg_hi, mg_lo)
            pe.wait_ge(h_scaled, NT)
            turn_tokens(pe, h_sc, 4, h_turned)

            pe.wait_ge(h_lo, KT // 2)
            pe.wait_ge(f_zero, 1)
            zeros = zero_s[:].bitcast(mybir.dt.bfloat16)
            for b in range(4, 8):
                pe.matmul(ps[:, b, :], zeros[:, 0:P], zeros[:, 0:512], start=True, stop=False, skip_group_check=True)
            gemm_cols(pe, RF + 1, 1, tok_hi, tok_lo)
            gemm_cols(pe, RF + 1, 2, tok_hi, tok_lo)
            with pe.Fori(1, F_STEPS) as f:
                r = f + (RG - 1)
                gemm_cols(pe, r, 0, tok_hi, tok_lo)
                gemm_cols(pe, r, 1, tok_hi, tok_lo)
                pe.wait_ge(hid_lo_s, f)
                gemm_down(pe, r, 2)
            pe.wait_ge(hid_lo_s, F_STEPS)
            gemm_down(pe, RG + F_STEPS - 1, 0)

        @block.scalar
        def _(act):
            def up_rows(v):
                return v.rearrange("j (c p) -> (j c) p", p=P)

            n = TAPS * CONV_T
            act.dma_start(rows_conv[0:n, :], up_rows(ssm_conv_w[0])).then_inc(rows_in, 16)
            act.dma_start(rows_conv[n:n_conv, :], rows(ssm_conv_b[0])).then_inc(rows_in, 16)
            act.dma_start(rows_gate[0:3 * KT, :], rows(b_gate[0])).then_inc(rows_in, 16)
            act.dma_start(rows_gate[3 * KT:n_gate, :], rows(ssm_norm_g[0])).then_inc(rows_in, 16)
            act.dma_start(rows_up01[0:n_up01, :], up_rows(ffn_conv_w[0, 0:2])).then_inc(rows_in, 16)
            act.dma_start(rows_up2[0:2 * FT, :], up_rows(ffn_conv_w[0, 2:3])).then_inc(rows_in, 16)
            act.dma_start(rows_up2[2 * FT:n_up2, :], rows(ffn_conv_b[0])).then_inc(rows_in, 16)
            act.dma_start(skip2[0:n_skip, :], ssm_D[0].rearrange("(c j) -> c j", j=2)).then_inc(skip_in, 16)
            act.dma_start(dt_rows[:, 0, :], on_all(ssm_dt_bias[0], SHEADS)).then_inc(dtp_in, 16)
            act.dma_start(dt_rows[:, 1, :], on_all(ssm_A_log[0], SHEADS)).then_inc(dtp_in, 16)
            act.dma_start(table_s[0:BUCKETS + 1, :], table).then_inc(relb_in, 16)
            act.dma_start(relb[0:BUCKETS, :], rel_bias).then_inc(relb_in, 16)
            act.dma_start(relb[BUCKETS:BUCKETS + 1, :], one_row).then_inc(relb_in, 16)

            act.wait_ge(x_in, 16)
            for t in range(NT):
                act.activation(x_sc[:, t, :], x_nat[:, t, :], ACT.Square,
                               accum_out=stat[:, t:t + 1]).then_inc(x_sumsq, 1)
            act.wait_ge(dtp_in, 32)
            act.activation(a_neg[:], dt_rows[:, 1, :], ACT.Exp).then_inc(a_exp, 1)
            act.wait_ge(dtw_in, 16)
            act.activation(wdt_hi[:], wdt_raw[:], ACT.Copy).then_inc(wdt_hi_s, 1)
            for j in range(KT // 2):
                act.wait_ge(x_turned, j + 1)
                act.activation(tok_hi[:, 2 * j:2 * j + 2, :], halves(4 + j), ACT.Copy).then_inc(x_hi, 1)
            for s in range(SLOTS):
                split_hi(act, 0, s, first=True)
            act.wait_ge(dt_step, 2)
            act.activation(dt_w[2][:], dt_w[1][:], ACT.Exp).then_inc(dt_exp, 1)
            act.wait_ge(bias_copied, 1)
            act.dma_start(bias_d, bias_row[0:HEADS, :].unsqueeze(1).to_broadcast([HEADS, P, BIAS_W])
                          ).then_inc(bias_out, 16)
            act.wait_ge(acs_ready, 2)
            act.dma_start(acs_d, acs_row[0:SHEADS, :]).then_inc(acs_out, 16)
            act.wait_ge(acs_out, 16)
            act.dma_start(acs_b[:].rearrange("p h t -> p (h t)"), on_all(acs_d.rearrange("h t -> (h t)"), SHEADS * T)
                          ).then_inc(acs_in, 16)

            with act.Fori(0, GROUPS) as g:
                r = 2 * g
                for s in range(SLOTS):
                    act.wait_ge(gemm_done[s], r + 1)
                    for j in range(2):
                        c = conv_tile(s, j, g)
                        act.activation(conv_a[:, s, j, :], ps[:, s, j * T:(j + 1) * T], ACT.Identity,
                                       bias=cols_conv[:, TAPS, bass.ds(c, 1)],
                                       scale=cols_conv[:, TAPS - 1, bass.ds(c, 1)])
                    act.activation(pad_x[:, s, :, TAPS - 1:], halves(s), ACT.Copy).then_inc(bank_free[s], 1)
                    split_hi(act, r + 1, s)
                    if s == 2:
                        act.wait_ge(seg_clamped, 2 * g + 2)
                        act.activation(decay[:], decay[:], ACT.Exp).then_inc(decay_ready, 1)
                    act.wait_ge(conv_step, 18 * g + 6 * s + 6)
                    act.activation(tanh_a[:, s], conv_a[:, s], ACT.Tanh).then_inc(conv_tanh, 1)
                for s in range(2):
                    act.wait_ge(gemm_done[s], r + 2)
                    act.wait_ge(conv_done, 3 * g + s + 1)
                    act.activation(tanh_a[:, s], halves(s), ACT.Tanh, scale=0.5).then_inc(z_tanh, 1)
                    split_hi(act, r + 2, s)
                act.wait_ge(gemm_done[2], r + 2)
                act.wait_ge(conv_done, 3 * g + 3)
                gate_tanh(act, tanh_a[:, 2], 2, KT + 2 * g)
                split_hi(act, r + 2, 2)
            act.wait_ge(eps_set, 1)
            act.wait_ge(g1_ready, 4)
            act.wait_ge(var_mm, 1)
            act.activation(rstd_g[:].rearrange("p a n -> p (a n)"), ps[:, 3:5, :].rearrange("p a n -> p (a n)"),
                           ACT.Sqrt, bias=eps_c[:, 0:1], scale=1.0 / GC).then_inc(var_sqrt, 1)
            act.wait_ge(bias_out, 16)
            for c0, at, n in ((0, LAG - P + P, P), (P, LAG - P, T)):
                src = bass.AP(tensor=bias_d.tensor, offset=at, ap=[[BIAS_W - 1, P], [P * BIAS_W, HEADS], [1, n]])
                act.dma_start(bias_t[:, :, c0:c0 + n], src).then_inc(bias_in, 16)
            act.dma_start(mem_nat[:], mem[0].rearrange("(t p) d -> p t d", p=P)).then_inc(m_in, 16)
            act.dma_start(gain_mem[:], on_all(mem_norm_g[0], D)).then_inc(m_gain_in, 16)
            act.wait_ge(m_in, 16)
            act.wait_ge(m_gain_in, 16)
            for t in range(NT):
                act.activation(junk_m[:, t, :], mem_nat[:, t, :], ACT.Square,
                               accum_out=stat[:, 2 + t:3 + t]).then_inc(m_sumsq, 1)
            act.wait_ge(m_sumsq, NT)

            with act.Fori(0, 4) as i:
                r = RB + i
                split_hi(act, r + 1, 0)
                act.wait_ge(gemm_done[1], r + 1)
                act.activation(q_t[:], halves(1), ACT.Copy, scale=DH ** -0.5).then_inc(bank_free[1], 1)
                split_hi(act, r + 1, 1)
                act.wait_ge(norm_step, 4 * i + 4)
                act.activation(os_hi[:, bass.ds(GT * i, GT), :], o_tmp[:], ACT.Copy).then_inc(os_hi_s, 1)
                act.wait_ge(s_neg, i + 1)
                for a in range(2):
                    for t in range(NT):
                        part = prob[:, a, 0:P] if t == 0 else prob[:, a, P:3 * P]
                        n = 2 * t + a
                        act.activation(part, part, ACT.Exp, bias=soft[:, 1, n:n + 1],
                                       accum_out=soft[:, 2, n:n + 1]).then_inc(p_exp, 1)
                act.wait_ge(gemm_done[2], r + 1)
                act.activation(v_t[:], halves(2), ACT.Copy).then_inc(bank_free[2], 1)
                act.wait_ge(p_turned, 2 * i + 1)
                act.activation(prob_t[:, 0, :], ps[:, 5, 0:3 * P], ACT.Copy).then_inc(pt_ready, 1)
                split_hi(act, r + 1, 2)
                act.wait_ge(o_mm, i + 1)
                act.activation(oa_hi[:, bass.ds(2 * i, 2), :], halves(7), ACT.Copy).then_inc(oa_hi_s, 1)
            for j in range(KT // 2):
                act.wait_ge(m_turned, j + 1)
                act.activation(me_hi[:, 2 * j:2 * j + 2, :], halves(3 + j), ACT.Copy).then_inc(m_hi, 1)

            with act.Fori(0, 4) as i:
                r = RC + i
                act.wait_ge(gemm_done[0], r + 1)
                act.activation(qm_t[:], halves(0), ACT.Copy).then_inc(bank_free[0], 1)
                split_hi(act, r + 1, 0)
                act.wait_ge(gemm_done[1], r + 1)
                act.activation(km_t[:], halves(1), ACT.Copy).then_inc(bank_free[1], 1)
                split_hi(act, r + 1, 1)
                act.wait_ge(ms_neg, i + 1)
                for t in range(NT):
                    act.activation(mprob[:, t, :], ps[:, 3, t * T:(t + 1) * T], ACT.Exp, bias=msoft[:, 1, t:t + 1],
                                   scale=MDH ** -0.5, accum_out=msoft[:, 2, t:t + 1]).then_inc(mp_exp, 1)
                act.wait_ge(gemm_done[2], r + 1)
                act.activation(vm_t[:], halves(2), ACT.Copy).then_inc(bank_free[2], 1)
                act.wait_ge(mp_turned, i + 1)
                act.activation(mprob_t[:], halves(4), ACT.Copy).then_inc(mpt_ready, 1)
                split_hi(act, r + 1, 2)
                act.wait_ge(mo_mm, i + 1)
                act.activation(om_hi[:, bass.ds(2 * i, 2), :], halves(5), ACT.Copy).then_inc(om_hi_s, 1)

            with act.Fori(0, 4) as i:
                r = RD + i
                split_hi(act, r + 1, 0)
                split_hi(act, r + 1, 1)
                act.wait_ge(gemm_done[2], r + 1)
                gate_tanh(act, tanh_d, 2, 2 * i)
                split_hi(act, r + 1, 2)

            with act.Fori(0, 4) as i:
                r = RE + i
                split_hi(act, r + 1, 0)
                act.wait_ge(gemm_done[1], r + 1)
                gate_tanh(act, tanh_e, 1, 2 * KT + 2 * i)
                split_hi(act, r + 1, 1)
                split_hi(act, r + 1, 2)
                act.wait_ge(e_summed, i + 1)
                act.activation(mg_hi[:, bass.ds(2 * i, 2), :], e_sum[:], ACT.Copy).then_inc(mg_hi_s, 1)

            for c in range(4):
                split_hi(act, RF + 1 + c // SLOTS, c % SLOTS)
            act.wait_ge(bank_free[0], RF + 3)
            for t in range(NT):
                act.activation(h_sc[:, t, :], h_nat[:, t, :], ACT.Square,
                               accum_out=stat[:, 4 + t:5 + t]).then_inc(h_sumsq, 1)
            for j in range(KT // 2):
                act.wait_ge(h_turned, j + 1)
                act.activation(tok_hi[:, 2 * j:2 * j + 2, :], halves(4 + j), ACT.Copy).then_inc(h_hi, 1)

            def ffn(f, ra, sa, rb, sb, after_gate, after_up, last, peeled=False):
                for n, (r, s, pad, conv, tile) in enumerate(((ra, sa, pad_g, conv_g, 0), (rb, sb, pad_u, conv_u, FT))):
                    act.wait_ge(gemm_done[s], r + 1)
                    if not peeled:
                        act.wait_ge((g_silu, hid_done)[n], f)
                    for j in range(2):
                        c = tile + 2 * f + j
                        act.activation(conv[:, j, :], ps[:, s, j * T:(j + 1) * T], ACT.Identity,
                                       bias=cols_up[:, FTAPS, bass.ds(c, 1)],
                                       scale=cols_up[:, FTAPS - 1, bass.ds(c, 1)])
                    act.activation(pad[:, :, FTAPS - 1:], halves(s), ACT.Copy).then_inc(bank_free[s], 1)
                    for rr, ss in (after_gate, after_up)[n]:
                        split_hi(act, rr, ss)
                    if n == 0:
                        act.wait_ge(f_step, 8 * f + 4)
                        act.activation(tanh_g[:], conv_g[:], ACT.Tanh).then_inc(g_tanh, 1)
                act.wait_ge(hid_done, f + 1)
                if not peeled:
                    act.wait_ge(gemm_done[2], f + RG)
                act.activation(hid_hi[:], hid[:], ACT.Copy).then_inc(hid_hi_s, 1)
                for rr, ss in last:
                    split_hi(act, rr, ss)

            ffn(0, RF + 1, 1, RF + 1, 2, [(RG, 1)], [(RG, 2)], [], peeled=True)
            with act.Fori(1, F_STEPS - 1) as f:
                r = f + (RG - 1)
                ffn(f, r, 0, r, 1, [(r + 1, 0)], [(r + 1, 1)], [(r + 1, 2)])
            r = RG + F_STEPS - 2
            ffn(F_STEPS - 1, r, 0, r, 1, [(r + 1, 0)], [], [])
            for t in range(NT):
                act.wait_ge(y_added, t + 1)
                act.activation(h_sc[:, t, :], h_nat[:, t, :], ACT.Square,
                               accum_out=stat[:, 6 + t:7 + t]).then_inc(y_sumsq, 1)

        @block.vector
        def _(dve):
            def gate(dst, src, done):
                dve.tensor_scalar(dst, src, 0.5, 0.5, ALU.mult, ALU.add).then_inc(done, 1)

            for s in range(SLOTS):
                dve.memset(pad_x[:, s, 0, 0:TAPS - 1], 0.0).then_inc(lo_ready[s], 1)
                dve.memset(pad_x[:, s, 1, 0:TAPS - 1], 0.0).then_inc(bank_free[s], 1)
            dve.memset(eps_c[:], EPS).then_inc(eps_set, 1)
            dve.memset(pow_c[:], -0.5).then_inc(pow_set, 1)
            dve.wait_ge(skip_in, 16)
            dve.tensor_copy(rows_skip[0:n_skip, :].rearrange("p (j n) -> p j n", j=2),
                            skip2[0:n_skip, :].unsqueeze(2).to_broadcast([n_skip, 2, SHD])).then_inc(skip_row, 1)
            dve.wait_ge(gain_in, 16)
            for t in range(NT):
                dve.wait_ge(x_rstd, t + 1)
                dve.scalar_tensor_tensor(x_sc[:, t, :], x_nat[:, t, :], stat[:, t:t + 1], gain_mix[:], ALU.mult,
                                         ALU.mult).then_inc(x_scaled, 1)
            dve.wait_ge(wdt_hi_s, 1)
            dve.tensor_tensor(wdt_lo[:], wdt_raw[:], wdt_hi[:].bitcast(F32), ALU.subtract).then_inc(wdt_lo_s, 1)
            for j in range(KT // 2):
                dve.wait_ge(x_hi, j + 1)
                two = slice(2 * j, 2 * j + 2)
                dve.tensor_tensor(tok_lo[:, two, :], halves(4 + j), tok_hi[:, two, :].bitcast(F32),
                                  ALU.subtract).then_inc(x_lo, 1)
            dve.wait_ge(rows_turned, 1)
            at = [0]

            def take(dst, n, scale):
                dve.tensor_scalar(dst, ps[:, 3, at[0]:at[0] + n], scale, None, ALU.mult).then_inc(params_ready, 1)
                at[0] += n

            take(cols_conv[:].rearrange("p a c -> p (a c)"), n_conv, 0.5)
            take(cols_gate[:, 0:3 * KT], 3 * KT, 0.5)
            take(cols_gate[:, 3 * KT:n_gate], n_gate - 3 * KT, 1.0)
            take(cols_skip[:], n_skip, 1.0)
            for j in range(4):
                take(cols_up[:, j, 0:FT], FT, 0.5)
                take(cols_up[:, j, FT:2 * FT], FT, 1.0)
            dve.wait_ge(bias_mm, 1)
            dve.tensor_copy(bias_row[0:HEADS, :], ps[0:HEADS, 0, 0:BIAS_W]).then_inc(bias_copied, 1)
            dve.wait_ge(dt_mm, 1)
            dve.tensor_copy(dt_raw[0:SHEADS, :], ps[0:SHEADS, 1, 0:T]).then_inc(dt_copied, 1)
            for s in range(SLOTS):
                split_lo(dve, 0, s)
            v, m, e, s_, q, p = dt_w
            steps = [0]

            def step(ins):
                steps[0] += 1
                ins.then_inc(dt_step, 1)
                dve.wait_ge(dt_step, steps[0])

            dve.wait_ge(dtp_in, 32)
            dve.wait_ge(dt_turned, 1)
            step(dve.tensor_tensor(v[:], ps[:, 2, 0:NT * SHEADS].rearrange("p (t h) -> p t h", t=NT),
                                   dt_rows[:, 0:1, :].to_broadcast([P, NT, SHEADS]), ALU.add))
            step(dve.scalar_tensor_tensor(m[:], v[:], -1.0, v[:], ALU.mult, ALU.min))
            dve.wait_ge(dt_exp, 1)
            step(dve.tensor_scalar(m[:], e[:], 2.0, None, ALU.add))
            step(dve.reciprocal(q[:], m[:]))
            step(dve.tensor_tensor(s_[:], e[:], q[:], ALU.mult))
            step(dve.tensor_tensor(q[:], s_[:], s_[:], ALU.mult))
            step(dve.tensor_scalar(p[:], q[:], 1.0 / 17, None, ALU.mult))
            for n in (15, 13, 11, 9, 7, 5, 3):
                step(dve.scalar_tensor_tensor(p[:], p[:], 1.0 / n, q[:], ALU.add, ALU.mult))
            step(dve.scalar_tensor_tensor(p[:], p[:], 1.0, s_[:], ALU.add, ALU.mult))
            step(dve.tensor_scalar(m[:], v[:], 0.0, None, ALU.max))
            step(dve.scalar_tensor_tensor(dt_s[:], p[:], 2.0, m[:], ALU.mult, ALU.add))
            dve.wait_ge(a_exp, 1)
            step(dve.tensor_scalar(a_neg[:], a_neg[:], -1.0, None, ALU.mult))
            step(dve.tensor_tensor(da_s[:], dt_s[:], a_neg[:].unsqueeze(1).to_broadcast([P, NT, SHEADS]), ALU.mult))
            assert steps[0] == 19
            dve.wait_ge(acs_mm, 1)
            dve.tensor_copy(acs_s[:].rearrange("p t h -> p (t h)"), ps[:, 4, 0:NT * SHEADS]).then_inc(acs_ready, 1)
            dve.tensor_copy(acs_row[0:SHEADS, :], ps[0:SHEADS, 5, 0:T]).then_inc(acs_ready, 1)

            with dve.Fori(0, GROUPS) as g:
                r = 2 * g

                def convolve(s):
                    dve.wait_ge(bank_free[s], r + 2)
                    for tap in range(TAPS - 1):
                        for j in range(2):
                            n = 18 * g + 6 * s + 2 * tap + j
                            if tap:
                                dve.wait_ge(conv_step, n - 1)
                            dve.scalar_tensor_tensor(
                                conv_a[:, s, j, :], pad_x[:, s, j, tap:tap + T],
                                cols_conv[:, tap, bass.ds(conv_tile(s, j, g), 1)], conv_a[:, s, j, :], ALU.mult,
                                ALU.add).then_inc(conv_step, 1)

                def activate(s):
                    dve.wait_ge(conv_tanh, 3 * g + s + 1)
                    dve.scalar_tensor_tensor(conv_o[:, 2 * s:2 * s + 2, :], tanh_a[:, s], 1.0, conv_a[:, s], ALU.add,
                                             ALU.mult).then_inc(conv_done, 1)

                convolve(0)
                split_lo(dve, r + 1, 0)
                activate(0)
                convolve(1)
                split_lo(dve, r + 1, 1)
                dve.wait_ge(seg_ready, 2 * g + 2)
                for c in (slice(0, P), slice(T, T + P)):
                    dve.tensor_scalar(decay[:, :, c], decay[:, :, c], 0.0, None, ALU.min).then_inc(seg_clamped, 1)
                activate(1)
                convolve(2)
                split_lo(dve, r + 1, 2)
                activate(2)

                def silu_z(s):
                    dve.wait_ge(z_tanh, 2 * g + s + 1)
                    dve.scalar_tensor_tensor(z_act[:, 2 * s:2 * s + 2, :], tanh_a[:, s], 1.0, halves(s), ALU.add,
                                             ALU.mult).then_inc(bank_free[s], 1)
                    split_lo(dve, r + 2, s)

                silu_z(0)
                dve.wait_ge(xg_turned, g + 1)
                for t in range(NT):
                    dve.tensor_tensor(x_dt[:, t, :].rearrange("p (h n) -> p h n", n=SHD),
                                      ps[:, 3 + t, :].rearrange("p (h n) -> p h n", n=SHD),
                                      dt_s[:, t, bass.ds(HPG * g, HPG)].unsqueeze(2).to_broadcast([P, HPG, SHD]),
                                      ALU.mult).then_inc(xdt_ready, 1)
                dve.wait_ge(cb_mm, g + 1)
                dve.tensor_tensor(cb[:], ps[:, 5, 0:3 * P], cb_mask, ALU.mult).then_inc(cb_masked, 1)
                dve.wait_ge(cb_masked, g + 1)
                dve.wait_ge(decay_ready, g + 1)
                dve.tensor_tensor(decay[:], decay[:], cb[:].unsqueeze(1).to_broadcast([P, HPG, 3 * P]),
                                  ALU.mult).then_inc(decay_cb, 1)
                silu_z(1)
                dve.wait_ge(y_mm, g + 1)
                for c in range(GT):
                    dve.scalar_tensor_tensor(y_sum[:, c, :], conv_o[:, 2 + c, :], cols_skip[:, bass.ds(GT * g + c, 1)],
                                             ps[:, 6 + c // 2, (c % 2) * T:(c % 2 + 1) * T], ALU.mult,
                                             ALU.add).then_inc(y_step, 1)
                dve.wait_ge(y_step, GT * g + GT)
                dve.scalar_tensor_tensor(v_ssm[:, bass.ds(GT * g, GT), :], z_act[:], 0.5, y_sum[:], ALU.mult,
                                         ALU.mult).then_inc(v_ready, 1)
                dve.wait_ge(bank_free[2], r + 3)
                gate(g1[:, bass.ds(2 * g, 2), :], tanh_a[:, 2], g1_ready)
                split_lo(dve, r + 2, 2)
            dve.wait_ge(var_sqrt, 1)
            dve.reciprocal(rstd_g[:], rstd_g[:]).then_inc(var_ready, 1)
            dve.wait_ge(var_ready, 1)
            dve.wait_ge(m_gain_in, 16)
            for t in range(NT):
                dve.wait_ge(m_rstd, t + 1)
                dve.scalar_tensor_tensor(mem_nat[:, t, :], mem_nat[:, t, :], stat[:, 2 + t:3 + t], gain_mem[:],
                                         ALU.mult, ALU.mult).then_inc(m_scaled, 1)
            dve.wait_ge(bias_in, 32)

            with dve.Fori(0, 4) as i:
                r = RB + i
                dve.wait_ge(gemm_done[0], r + 1)
                dve.tensor_copy(k_t[:], halves(0)).then_inc(bank_free[0], 1)
                split_lo(dve, r + 1, 0)
                for c in range(GT):
                    dve.scalar_tensor_tensor(o_tmp[:, c, :], v_ssm[:, bass.ds(GT * i + c, 1), :].squeeze(1),
                                             cols_gate[:, bass.ds(3 * KT + GT * i + c, 1)],
                                             rstd_g[:, bass.ds(i, 1), :].squeeze(1), ALU.mult,
                                             ALU.mult).then_inc(norm_step, 1)
                dve.wait_ge(s_mm, i + 1)
                dve.tensor_tensor(prob[:], ps[:, 3:5, 0:3 * P], bias_t[:, bass.ds(2 * i, 2), :],
                                  ALU.add).then_inc(s_biased, 1)
                dve.wait_ge(s_biased, i + 1)
                dve.tensor_reduce(soft[:, 0, 0:2], prob[:, :, 0:P], AX, ALU.max).then_inc(s_max, 1)
                dve.tensor_reduce(soft[:, 0, 2:4], prob[:, :, P:3 * P], AX, ALU.max).then_inc(s_max, 1)
                dve.wait_ge(s_max, 2 * i + 2)
                dve.tensor_scalar(soft[:, 1, :], soft[:, 0, :], -1.0, None, ALU.mult).then_inc(s_neg, 1)
                split_lo(dve, r + 1, 1)
                dve.wait_ge(p_exp, 4 * i + 4)
                dve.reciprocal(soft[:, 3, :], soft[:, 2, :]).then_inc(p_rec, 1)
                dve.wait_ge(p_rec, i + 1)
                for a in range(2):
                    for t in range(NT):
                        part = prob[:, a, 0:P] if t == 0 else prob[:, a, P:3 * P]
                        dve.tensor_scalar(part, part, soft[:, 3, 2 * t + a:2 * t + a + 1], None,
                                          ALU.mult).then_inc(p_norm, 1)
                dve.wait_ge(os_hi_s, i + 1)
                dve.tensor_tensor(os_lo[:, bass.ds(GT * i, GT), :], o_tmp[:],
                                  os_hi[:, bass.ds(GT * i, GT), :].bitcast(F32), ALU.subtract).then_inc(os_lo_s, 1)
                dve.wait_ge(p_turned, 2 * i + 2)
                dve.tensor_copy(prob_t[:, 1, :], ps[:, 6, 0:3 * P]).then_inc(pt_ready, 1)
                split_lo(dve, r + 1, 2)
                dve.wait_ge(oa_hi_s, i + 1)
                dve.tensor_tensor(oa_lo[:, bass.ds(2 * i, 2), :], halves(7),
                                  oa_hi[:, bass.ds(2 * i, 2), :].bitcast(F32), ALU.subtract).then_inc(oa_lo_s, 1)
            for j in range(KT // 2):
                dve.wait_ge(m_hi, j + 1)
                two = slice(2 * j, 2 * j + 2)
                dve.tensor_tensor(me_lo[:, two, :], halves(3 + j), me_hi[:, two, :].bitcast(F32),
                                  ALU.subtract).then_inc(m_lo, 1)

            with dve.Fori(0, 4) as i:
                r = RC + i
                split_lo(dve, r + 1, 0)
                dve.wait_ge(ms_mm, i + 1)
                dve.tensor_reduce(msoft[:, 0, :], halves(3), AX, ALU.max).then_inc(ms_max, 1)
                dve.wait_ge(ms_max, i + 1)
                dve.tensor_scalar(msoft[:, 1, :], msoft[:, 0, :], -(MDH ** -0.5), None, ALU.mult).then_inc(ms_neg, 1)
                split_lo(dve, r + 1, 1)
                dve.wait_ge(mp_exp, 2 * i + 2)
                dve.reciprocal(msoft[:, 3, :], msoft[:, 2, :]).then_inc(mp_rec, 1)
                dve.wait_ge(mp_rec, i + 1)
                for t in range(NT):
                    dve.tensor_scalar(mprob[:, t, :], mprob[:, t, :], msoft[:, 3, t:t + 1], None,
                                      ALU.mult).then_inc(mp_norm, 1)
                split_lo(dve, r + 1, 2)
                dve.wait_ge(om_hi_s, i + 1)
                dve.tensor_tensor(om_lo[:, bass.ds(2 * i, 2), :], halves(5),
                                  om_hi[:, bass.ds(2 * i, 2), :].bitcast(F32), ALU.subtract).then_inc(om_lo_s, 1)

            with dve.Fori(0, 4) as i:
                r = RD + i
                split_lo(dve, r + 1, 0)
                dve.wait_ge(gemm_done[1], r + 1)
                for j in range(2):
                    tile = bass.ds(2 * i + j, 1)
                    dve.tensor_tensor(merged[:, tile, :], ps[:, j:j + 1, 0:T], g1[:, tile, :],
                                      ALU.mult).then_inc(bank_free[j], 1)
                split_lo(dve, r + 1, 1)
                dve.wait_ge(bank_free[2], r + 2)
                gate(g0[:, bass.ds(2 * i, 2), :], tanh_d[:], g0_ready)
                split_lo(dve, r + 1, 2)

            with dve.Fori(0, 4) as i:
                r = RE + i
                two = bass.ds(2 * i, 2)
                dve.wait_ge(g0_ready, 4)
                dve.wait_ge(gemm_done[0], r + 1)
                dve.tensor_tensor(e_attn[:], halves(0), g0[:, two, :], ALU.mult).then_inc(bank_free[0], 1)
                split_lo(dve, r + 1, 0)
                dve.wait_ge(bank_free[0], r + 2)
                dve.tensor_tensor(e_attn[:], e_attn[:], merged[:, two, :], ALU.add).then_inc(e_step, 1)
                dve.wait_ge(bank_free[1], r + 2)
                gate(e_gate[:], tanh_e[:], e_step)
                split_lo(dve, r + 1, 1)
                dve.wait_ge(e_step, 2 * i + 2)
                dve.wait_ge(gemm_done[2], r + 1)
                dve.tensor_tensor(e_mem[:], halves(2), e_gate[:], ALU.mult).then_inc(bank_free[2], 1)
                dve.wait_ge(bank_free[2], r + 2)
                dve.tensor_tensor(e_sum[:], e_attn[:], e_mem[:], ALU.add).then_inc(e_summed, 1)
                split_lo(dve, r + 1, 2)
                dve.wait_ge(mg_hi_s, i + 1)
                dve.tensor_tensor(mg_lo[:, two, :], e_sum[:], mg_hi[:, two, :].bitcast(F32),
                                  ALU.subtract).then_inc(mg_lo_s, 1)

            dve.memset(zero_s[:], 0.0).then_inc(f_zero, 1)
            dve.memset(pad_g[:, :, 0:FTAPS - 1], 0.0).then_inc(f_zero, 1)
            dve.memset(pad_u[:, :, 0:FTAPS - 1], 0.0).then_inc(f_zero, 1)
            dve.wait_ge(x_again, 16)
            for c in range(4):
                r, s = RF + c // SLOTS, c % SLOTS
                dve.wait_ge(gemm_done[s], r + 1)
                part = h_nat[:, :, c * CW:(c + 1) * CW]
                dve.tensor_tensor(part, halves(s), part, ALU.add).then_inc(bank_free[s], 1)
                split_lo(dve, r + 1, s)
            dve.wait_ge(late_gains, 32)
            for t in range(NT):
                dve.wait_ge(h_rstd, t + 1)
                dve.scalar_tensor_tensor(h_sc[:, t, :], h_nat[:, t, :], stat[:, 4 + t:5 + t], gain_ffn[:], ALU.mult,
                                         ALU.mult).then_inc(h_scaled, 1)
            for j in range(KT // 2):
                dve.wait_ge(h_hi, j + 1)
                two = slice(2 * j, 2 * j + 2)
                dve.tensor_tensor(tok_lo[:, two, :], halves(4 + j), tok_hi[:, two, :].bitcast(F32),
                                  ALU.subtract).then_inc(h_lo, 1)

            def ffn(f, sa, ra, sb, rb, after_gate, after_up, last):
                def convolve(n, s, r, pad, conv, tile):
                    dve.wait_ge(bank_free[s], r + 2)
                    for tap in range(FTAPS - 1):
                        for j in range(2):
                            m = 8 * f + 4 * n + 2 * tap + j
                            if tap:
                                dve.wait_ge(f_step, m - 1)
                            dve.scalar_tensor_tensor(conv[:, j, :], pad[:, j, tap:tap + T],
                                                     cols_up[:, tap, bass.ds(tile + 2 * f + j, 1)], conv[:, j, :],
                                                     ALU.mult, ALU.add).then_inc(f_step, 1)

                convolve(0, sa, ra, pad_g, conv_g, 0)
                for rr, ss in after_gate:
                    split_lo(dve, rr, ss)
                dve.wait_ge(g_tanh, f + 1)
                dve.scalar_tensor_tensor(silu_g[:], tanh_g[:], 1.0, conv_g[:], ALU.add, ALU.mult).then_inc(g_silu, 1)
                convolve(1, sb, rb, pad_u, conv_u, FT)
                dve.wait_ge(g_silu, f + 1)
                dve.wait_ge(f_step, 8 * f + 8)
                dve.tensor_tensor(hid[:], silu_g[:], conv_u[:], ALU.mult).then_inc(hid_done, 1)
                for rr, ss in after_up:
                    split_lo(dve, rr, ss)
                dve.wait_ge(hid_hi_s, f + 1)
                dve.tensor_tensor(hid_lo[:], hid[:], hid_hi[:].bitcast(F32), ALU.subtract).then_inc(hid_lo_s, 1)
                for rr, ss in last:
                    split_lo(dve, rr, ss)

            ffn(0, 1, RF + 1, 2, RF + 1, [(RG, 1)], [(RG, 2)], [])
            with dve.Fori(1, F_STEPS - 1) as f:
                r = f + (RG - 1)
                ffn(f, 0, r, 1, r, [(r + 1, 0)], [(r + 1, 1)], [(r + 1, 2)])
            r = RG + F_STEPS - 2
            ffn(F_STEPS - 1, 0, r, 1, r, [(r + 1, 0)], [], [])
            dve.wait_ge(gemm_done[0], RG + F_STEPS)
            for t in range(NT):
                part = h_nat[:, t, :].rearrange("p (a n) -> p a n", a=2)
                dve.tensor_tensor(part, ps[:, 4 + 2 * t:6 + 2 * t, :], part, ALU.add).then_inc(y_added, 1)
            for t in range(NT):
                dve.wait_ge(y_rstd, t + 1)
                dve.scalar_tensor_tensor(h_sc[:, t, :], h_nat[:, t, :], stat[:, 6 + t:7 + t], gain_fin[:], ALU.mult,
                                         ALU.mult).then_inc(y_scaled, 1)

        @block.gpsimd
        def _(pool):
            def rstd(c, sumsq, var, done):
                for t in range(NT):
                    col = stat[:, c + t:c + t + 1]
                    pool.wait_ge(sumsq, t + 1)
                    pool.tensor_scalar(col, col, 1.0 / D, EPS, ALU.mult, ALU.add).then_inc(var, 1)
                    pool.wait_ge(var, t + 1)
                    pool.tensor_tensor(col, col, pow_c[:, 0:1], ALU.pow).then_inc(done, 1)

            pool.wait_ge(pow_set, 1)
            rstd(0, x_sumsq, x_var, x_rstd)
            pool.wait_ge(acs_ready, 2)
            pool.wait_ge(acs_in, 16)
            with pool.Fori(0, GROUPS) as g:
                heads = bass.ds(HPG * g, HPG)
                for t, c, first in ((0, slice(0, T), 0), (1, slice(T, T + P), P)):
                    pool.tensor_tensor(decay[:, :, c], acs_b[:, heads, first:T],
                                       acs_s[:, t, heads].unsqueeze(2).to_broadcast([P, HPG, T - first]),
                                       ALU.subtract).then_inc(seg_ready, 1)
                v = v_ssm[:, bass.ds(GT * g, GT), :]
                pool.wait_ge(v_ready, g + 1)
                pool.tensor_tensor(sq_v[:], v, v, ALU.mult).then_inc(sq_step, 1)
                pool.wait_ge(sq_step, 3 * g + 1)
                pool.tensor_tensor(sq_h[:], sq_v[:, 0:2, :], sq_v[:, 2:4, :], ALU.add).then_inc(sq_step, 1)
                pool.wait_ge(sq_step, 3 * g + 2)
                pool.tensor_tensor(sq_g[:, bass.ds(g, 1), :], sq_h[:, 0:1, :], sq_h[:, 1:2, :],
                                   ALU.add).then_inc(sq_step, 1)
            rstd(2, m_sumsq, m_var, m_rstd)
            rstd(4, h_sumsq, h_var, h_rstd)
            rstd(6, y_sumsq, y_var, y_rstd)


_INS = ("x", "mem", "rel_bias", "mix_norm_g", "w_in", "b_gate", "ssm_conv_w", "ssm_conv_b", "ssm_dt_bias", "ssm_A_log",
        "ssm_D", "ssm_norm_g", "mem_norm_g", "w_mem_kv", "w_br_attn", "w_br_ssm", "w_br_mem", "w_out", "ffn_norm_g",
        "w_ffn_up", "ffn_conv_w", "ffn_conv_b", "w_ffn_down", "final_norm_g")


def kernel(**inputs):
    import concourse.bacc as bacc
    from concourse.bass_utils import run_bass_kernel_spmd

    nc = bacc.Bacc("TRN2", target_bir_lowering=False, num_devices=1, dynamic_dma_scratch_size=1024)
    arrays = {n: np.ascontiguousarray(inputs[n]) for n in _INS}
    arrays |= dict(zip(("square_table", "bucket_table", "one_row"), constants()))
    aps = [nc.dram_tensor(n, a.shape, mybir.dt.from_np(a.dtype), kind="ExternalInput").ap() for n, a in arrays.items()]
    out = nc.dram_tensor("out", (1, T, D), F32, kind="ExternalOutput").ap()
    build(nc, *aps, out)
    r = run_bass_kernel_spmd(nc, [arrays], core_ids=[0])
    return r.results[0]["out"]
```

```python
import numpy as np

import concourse.bass as bass
from concourse import mybir

F32 = mybir.dt.float32
F32R = mybir.dt.float32r
ALU = mybir.AluOpType
ACT = mybir.ActivationFunctionType
AX = mybir.AxisListType.X

P = 128
KB = 1024
EPS = 1e-6
MASKED = -1e30

D = 1024
T = 256
NT = T // P
KT = D // P
HEADS, DH = 8, 128
BUCKETS, MAX_DIST = 32, 1024
SSM = 2 * D
SHD = 64
SHEADS = SSM // SHD
GROUPS, STATE = 4, 128
HPG = SHEADS // GROUPS
GC = SSM // GROUPS
GT = GC // P
TAPS = 4
CONV_T = (SSM + 2 * GROUPS * STATE) // P
MHEADS, MDH = 4, 256
FFN = 2816
FTAPS = 3
FT = FFN // P
F_STEPS = FFN // 256
QC, KC, VC = 0, D, 2 * D
ZC = 3 * D
XC = ZC + SSM
BC = XC + SSM
CC = BC + GROUPS * STATE
DTC = CC + GROUPS * STATE
QMC = DTC + SHEADS
GATEC = QMC + D

SLOTS = 3
CW = 256
CHUNK = KT * CW
LAG = 2 * P - 1
BIAS_W = 3 * P
RA, RB, RC, RD, RE, RF, RG = 0, 8, 12, 16, 20, 24, 26


def constants():
    p, c = np.arange(P)[:, None], np.arange(P)[None, :]
    upper = (c >= p).astype(np.float32)
    ones = np.ones((P, P), np.float32)
    square = np.concatenate([np.eye(P, dtype=np.float32), upper, ones, upper, ones], axis=1)
    dist = LAG - np.arange(BIAS_W)
    n = np.maximum(dist, 0)
    half = BUCKETS // 2
    far = np.maximum(n, half).astype(np.float32)
    large = half + (np.log(far / np.float32(half)) / np.float32(np.log(MAX_DIST / half))
                    * np.float32(BUCKETS - half)).astype(np.int32)
    bucket = np.where(n < half, n, np.minimum(large, BUCKETS - 1))
    table = np.zeros((BUCKETS + 1, BIAS_W), np.float32)
    table[:BUCKETS] = bucket[None, :] == np.arange(BUCKETS)[:, None]
    table[BUCKETS] = np.where(dist < 0, np.float32(MASKED), np.float32(0))
    return square, table, np.ones((1, HEADS), np.float32)


def build(nc, x, mem, rel_bias, mix_norm_g, w_in, b_gate, ssm_conv_w, ssm_conv_b, ssm_dt_bias, ssm_A_log, ssm_D,
          ssm_norm_g, mem_norm_g, w_mem_kv, w_br_attn, w_br_ssm, w_br_mem, w_out, ffn_norm_g, w_ffn_up, ffn_conv_w,
          ffn_conv_b, w_ffn_down, final_norm_g, square, table, one_row, out):
    base = -(-nc.sbuf_base // 64) * 64

    def place(name, at, shape, dtype=F32):
        return nc.alloc_sbuf_tensor_at(name, [P, *shape], dtype, offset=base + int(at * KB))

    w_raw = place("w_raw", 0, [SLOTS, CHUNK])
    w_hi = place("w_hi", 24, [SLOTS, CHUNK], F32R)
    w_lo = place("w_lo", 48, [SLOTS, CHUNK], F32R)
    tok_hi = place("tok_hi", 72, [KT, T], F32R)
    tok_lo = place("tok_lo", 80, [KT, T], F32R)
    sq = place("square_c", 88, [5 * P])
    ident, tri_wide, ones = sq[:, 0:P], sq[:, P:3 * P], sq[:, 4 * P:5 * P]
    cb_mask = sq[:, P:4 * P]
    table_s = place("table_s", 90.5, [BIAS_W])
    relb = place("relb", 92, [HEADS])
    rows_conv = place("rows_conv", 92.5, [P])
    rows_gate = place("rows_gate", 93, [P])
    rows_skip = place("rows_skip", 93.5, [P])
    rows_up01 = place("rows_up01", 94, [P])
    rows_up2 = place("rows_up2", 94.5, [P])
    n_conv, n_gate, n_skip, n_up01, n_up2 = (TAPS + 1) * CONV_T, 4 * KT + SSM // P, SSM // P, 2 * 2 * FT, 2 * 2 * FT
    cols_conv = place("cols_conv", 95, [TAPS + 1, CONV_T])
    cols_gate = place("cols_gate", 95.5, [n_gate])
    cols_skip = place("cols_skip", 95.75, [n_skip])
    cols_up = place("cols_up", 96, [4, 2 * FT])
    skip2 = place("skip2", 96.75, [2])
    dt_rows = place("dt_rows", 96.875, [2, SHEADS])
    stat = place("stat", 97.25, [NT * 4])
    pow_c = place("pow_c", 97.3125, [NT * GROUPS])
    zero_s = place("zero_s", 99.46875, [P // 2])
    group_rstd = place("group_rstd", 99.71875, [NT * GROUPS])
    soft = place("soft", 97.375, [4, 4])
    msoft = place("msoft", 97.4375, [4, NT])
    R = 100
    a_neg = place("a_neg", 97.5, [SHEADS])
    dt_s = place("dt_s", 97.75, [NT, SHEADS])
    acs_s = place("acs_s", 98, [NT, SHEADS])
    dt_w = [place(f"dt_w{i}", R + 20 + 0.25 * i, [NT, SHEADS]) for i in range(6)]
    da_s = place("da_s", 99.75, [NT, SHEADS])
    g1 = place("g1", R + 0, [KT, T])
    v_ssm = place("v_ssm", R + 8, [GROUPS * GT, T])
    om_hi = place("om_hi", R + 8, [KT, T], F32R)
    om_lo = place("om_lo", R + 108, [KT, T], F32R)
    os_hi = place("os_hi", R + 24, [2 * KT, T], F32R)
    os_lo = place("os_lo", R + 40, [2 * KT, T], F32R)
    mg_hi = place("mg_hi", R + 24, [KT, T], F32R)
    mg_lo = place("mg_lo", R + 32, [KT, T], F32R)
    oa_hi = place("oa_hi", R + 56, [KT, T], F32R)
    oa_lo = place("oa_lo", R + 64, [KT, T], F32R)
    me_hi = place("me_hi", R + 72, [KT, T], F32R)
    me_lo = place("me_lo", R + 80, [KT, T], F32R)
    merged = place("merged", R + 72, [KT, T])
    g0 = place("g0", R + 80, [KT, T])
    x_nat = place("x_nat", R + 24, [NT, D])
    x_sc = place("x_sc", R + 32, [NT, D])
    gain_mix = place("gain_mix", R + 40, [D])
    wdt_raw = place("wdt_raw", R + 8, [KT, P])
    wdt_hi = place("wdt_hi", R + 12, [KT, P], F32R)
    wdt_lo = place("wdt_lo", R + 16, [KT, P], F32R)
    dt_raw = place("dt_raw", 98.25, [T])
    acs_row = place("acs_row", R + 21.5, [T])
    bias_row = place("bias_row", R + 22.5, [BIAS_W])
    acs_b = place("acs_b", R + 24, [SHEADS, T])
    decay = place("decay", R + 56, [HPG, 3 * P])
    pad_x = place("pad_x", R + 68, [SLOTS, 2, TAPS - 1 + T])
    conv_a = place("conv_a", R + 75, [SLOTS, 2, T])
    tanh_a = place("tanh_a", R + 81, [SLOTS, 2, T])
    conv_o = place("conv_o", R + 87, [6, T])
    x_dt = place("x_dt", R + 93, [NT, GC])
    z_act = place("z_act", R + 97, [GT, T])
    y_sum = place("y_sum", R + 101, [GT, T])
    sq_v = place("sq_v", R + 105, [GT, T])
    sq_h = place("sq_h", R + 109, [2, T])
    sq_g = place("sq_g", R + 111, [GROUPS, T])
    cb = place("cb", R + 115, [3 * P])
    bias_t = place("bias_t", R + 24, [HEADS, 3 * P])
    mem_nat = place("mem_nat", R + 36, [NT, D])
    gain_mem = place("gain_mem", R + 44, [D])
    junk_m = place("junk_m", R + 48, [NT, D])
    prob = place("prob", R + 99, [2, 3 * P])
    prob_t = place("prob_t", R + 102, [2, 3 * P])
    k_t = place("k_t", R + 116.5, [2, T])
    q_t = place("q_t", R + 118.5, [2, T])
    v_t = place("v_t", R + 120.5, [NT, 2 * DH])
    qm_t = place("qm_t", R + 88, [2, T])
    km_t = place("km_t", R + 90, [2, T])
    vm_t = place("vm_t", R + 92, [NT, MDH])
    mprob = place("mprob", R + 94, [NT, T])
    mprob_t = place("mprob_t", R + 96, [NT, T])
    rstd_g = place("rstd_g", R + 98, [GROUPS, T])
    o_tmp = place("o_tmp", R + 116.5, [GT, T])
    tanh_d = place("tanh_d", R + 88, [2, T])
    e_attn = place("e_attn", R + 90, [2, T])
    tanh_e = place("tanh_e", R + 92, [2, T])
    e_gate = place("e_gate", R + 94, [2, T])
    e_mem = place("e_mem", R + 96, [2, T])
    e_sum = place("e_sum", R + 98, [2, T])
    h_nat = place("h_nat", R + 100, [NT, D])
    h_sc = place("h_sc", R + 108, [NT, D])
    gain_fin = place("gain_fin", R + 44, [D])
    rstd_b = place("rstd_b", R + 18.5, [T])
    pad_g = place("pad_g", R + 0, [2, FTAPS - 1 + T])
    pad_u = place("pad_u", R + 2.25, [2, FTAPS - 1 + T])
    conv_g = place("conv_g", R + 4.5, [2, T])
    conv_u = place("conv_u", R + 6.5, [2, T])
    tanh_g = place("tanh_g", R + 8.5, [2, T])
    silu_g = place("silu_g", R + 10.5, [2, T])
    hid = place("hid", R + 12.5, [2, T])
    hid_hi = place("hid_hi", R + 14.5, [2, T], F32R)
    hid_lo = place("hid_lo", R + 16.5, [2, T], F32R)

    ps = nc.alloc_psum_tensor("ps", [P, 8, 512], F32)

    acs_d = nc.dram_tensor("acs_d", (SHEADS, T), F32, kind="Internal").ap()
    bias_d = nc.dram_tensor("bias_d", (HEADS, P, BIAS_W), F32, kind="Internal").ap()


    sem = nc.alloc_semaphore
    loaded, hi_ready, lo_ready, gemm_done, bank_free = (
        [sem(f"{n}{s}") for s in range(SLOTS)] for n in ("loaded", "hi_ready", "lo_ready", "gemm_done", "bank_free"))
    x_in = [sem("x_in0"), sem("x_in1")]
    gain_in, const_in, rows_in, dtw_in, dtp_in, relb_in, skip_in = map(
        sem, ("gain_in", "const_in", "rows_in", "dtw_in", "dtp_in", "relb_in", "skip_in"))
    zeros_set, pow_set, skip_row = sem("zeros_set"), sem("pow_set"), sem("skip_row")
    rows_turned, params_ready = sem("rows_turned"), sem("params_ready")
    x_sumsq, x_var, x_rstd, x_scaled, x_turned, x_hi, x_lo = map(
        sem, ("x_sumsq", "x_var", "x_rstd", "x_scaled", "x_turned", "x_hi", "x_lo"))
    wdt_hi_s, wdt_lo_s, dt_mm, dt_copied, dt_turned, dt_exp, dt_step, a_exp = map(
        sem, ("wdt_hi_s", "wdt_lo_s", "dt_mm", "dt_copied", "dt_turned", "dt_exp", "dt_step", "a_exp"))
    acs_mm, acs_ready, acs_out, acs_in = map(sem, ("acs_mm", "acs_ready", "acs_out", "acs_in"))
    bias_mm, bias_copied, bias_out, bias_in = map(sem, ("bias_mm", "bias_copied", "bias_out", "bias_in"))
    conv_step, conv_tanh, conv_done, seg_ready, seg_clamped, decay_ready, decay_cb = map(
        sem, ("conv_step", "conv_tanh", "conv_done", "seg_ready", "seg_clamped", "decay_ready", "decay_cb"))
    xg_turned, cb_mm, cb_masked, xdt_ready, y_mm, z_tanh, z_ready = map(
        sem, ("xg_turned", "cb_mm", "cb_masked", "xdt_ready", "y_mm", "z_tanh", "z_ready"))
    y_step, v_ready, sq_step, g1_ready = map(sem, ("y_step", "v_ready", "sq_step", "g1_ready"))
    group_mm, group_var, group_pow, group_spread, rstd_g_ready = map(
        sem, ("group_mm", "group_var", "group_pow", "group_spread", "rstd_g_ready"))
    s_mm, s_biased, s_max, s_neg, p_exp, p_rec, p_norm, p_turned, pt_ready, o_mm, oa_hi_s, oa_lo_s = map(
        sem, ("s_mm", "s_biased", "s_max", "s_neg", "p_exp", "p_rec", "p_norm", "p_turned", "pt_ready", "o_mm",
              "oa_hi_s", "oa_lo_s"))
    norm_step, os_hi_s, os_lo_s = map(sem, ("norm_step", "os_hi_s", "os_lo_s"))
    m_in, m_gain_in, m_sumsq, m_var, m_rstd, m_scaled, m_turned, m_hi, m_lo = map(
        sem, ("m_in", "m_gain_in", "m_sumsq", "m_var", "m_rstd", "m_scaled", "m_turned", "m_hi", "m_lo"))
    ms_mm, ms_max, ms_neg, mp_exp, mp_rec, mp_norm, mp_turned, mpt_ready, mo_mm, om_hi_s, om_lo_s = map(
        sem, ("ms_mm", "ms_max", "ms_neg", "mp_exp", "mp_rec", "mp_norm", "mp_turned", "mpt_ready", "mo_mm",
              "om_hi_s", "om_lo_s"))
    g0_ready, e_step, e_summed, mg_hi_s, mg_lo_s = map(
        sem, ("g0_ready", "e_step", "e_summed", "mg_hi_s", "mg_lo_s"))
    x_again, late_gain, h_sumsq, h_var, h_rstd, h_spread, rstd_b_ready, h_turned, h_hi, h_lo = map(
        sem, ("x_again", "late_gain", "h_sumsq", "h_var", "h_rstd", "h_spread", "rstd_b_ready", "h_turned", "h_hi",
              "h_lo"))
    pads_zero, conv_begun, f_step, g_tanh, g_silu, hid_done, hid_hi_s, hid_lo_s = map(
        sem, ("pads_zero", "conv_begun", "f_step", "g_tanh", "g_silu", "hid_done", "hid_hi_s", "hid_lo_s"))
    down_done, y_added, y_sumsq, y_var, y_rstd, y_scaled, y_out = map(
        sem, ("down_done", "y_added", "y_sumsq", "y_var", "y_rstd", "y_scaled", "y_out"))

    def load(sp, r, s, w, col):
        sp.wait_ge(lo_ready[s], r + 1)
        src = w[:, bass.ds(col, CW)].rearrange("(k p) n -> p k n", p=P)
        dst = w_raw[:, s, :].rearrange("p (k n) -> p k n", k=KT)
        for half in (slice(KT // 2, KT), slice(0, KT // 2)):
            sp.dma_start(dst[:, half, :], src[:, half, :]).then_inc(loaded[s], 16)

    def load_bc(sp, r, g):
        sp.wait_ge(lo_ready[0], r + 1)
        dst = w_raw[:, 0, :].rearrange("p (k n) -> p k n", k=KT)
        for j, col in enumerate((BC, CC)):
            src = w_in[0][:, bass.ds(col + STATE * g, STATE)].rearrange("(k p) n -> p k n", p=P)
            sp.dma_start(dst[:, :, j * P:(j + 1) * P], src).then_inc(loaded[0], 16)

    def load_down(sp, r, s, f):
        sp.wait_ge(lo_ready[s], r + 1)
        src = w_ffn_down[0][bass.ds(2 * P * f, 2 * P), :].rearrange("(k p) n -> p k n", p=P)
        dst = w_raw[:, s, :].rearrange("p (k n) -> p k n", k=2)
        for k in range(2):
            sp.dma_start(dst[:, k, :], src[:, k, :]).then_inc(loaded[s], 16)

    def split_hi(act, r, s, first=False):
        act.wait_ge(loaded[s], 32 * (r + 1))
        if not first:
            act.wait_ge(gemm_done[s], r)
        act.activation(w_hi[:, s, :], w_raw[:, s, :], ACT.Copy).then_inc(hi_ready[s], 1)

    def split_lo(dve, r, s):
        dve.wait_ge(hi_ready[s], r + 1)
        dve.tensor_tensor(w_lo[:, s, :], w_raw[:, s, :], w_hi[:, s, :].bitcast(F32),
                          ALU.subtract).then_inc(lo_ready[s], 1)

    def gemm_cols(pe, r, s, hi, lo, k0=0, banks=None, free=None, start=True, stop=True):
        pe.wait_ge(lo_ready[s], r + 2)
        for b in [s] if free is None else free:
            pe.wait_ge(bank_free[b], r + 1)
        for j in range(2):
            o = ps[:, s, j * T:(j + 1) * T] if banks is None else ps[:, banks[j], 0:T]
            mm = cols_part(pe, s, j, range(KT), o, hi, lo, k0, start, stop)
        mm.then_inc(gemm_done[s], 1)

    def cols_part(pe, s, j, ks, o, hi, lo, k0=0, start=True, stop=True):
        for k in ks:
            w = slice(k * CW + j * P, k * CW + (j + 1) * P)
            mm = three(pe, o, (w_hi[:, s, w], w_lo[:, s, w]), (hi[:, k0 + k, :], lo[:, k0 + k, :]),
                       start and k == ks[0], stop and k == ks[-1])
        return mm

    def three(pe, o, a, b, start, stop, **kw):
        pe.matmul(o, a[0], b[0], start=start, stop=False, **kw)
        pe.matmul(o, a[0], b[1], start=False, stop=False, **kw)
        return pe.matmul(o, a[1], b[0], start=False, stop=stop, **kw)

    def rows_part(pe, s, t, ks, hi, lo, start, stop, **kw):
        for k in ks:
            cut, w = slice(t * P, (t + 1) * P), slice(k * CW, (k + 1) * CW)
            mm = three(pe, ps[:, s, t * CW:(t + 1) * CW], (hi[:, k, cut], lo[:, k, cut]),
                       (w_hi[:, s, w], w_lo[:, s, w]), start and k == ks[0], stop and k == ks[-1], **kw)
        return mm

    def gemm_rows(pe, r, s, hi, lo):
        pe.wait_ge(lo_ready[s], r + 2)
        pe.wait_ge(bank_free[s], r + 1)
        for t in range(NT):
            mm = rows_part(pe, s, t, range(KT), hi, lo, True, True)
        mm.then_inc(gemm_done[s], 1)

    def down_part(pe, s, t):
        for k in range(2):
            for half in range(2):
                cut, w = slice(t * P, (t + 1) * P), slice(k * D + half * 512, k * D + half * 512 + 512)
                mm = three(pe, ps[:, 4 + 2 * t + half, :], (hid_hi[:, k, cut], hid_lo[:, k, cut]),
                           (w_hi[:, s, w], w_lo[:, s, w]), False, False, skip_group_check=True)
        return mm

    def open_bank(pe, b):
        z = zero_s[:].bitcast(mybir.dt.bfloat16)
        pe.matmul(ps[:, b, :].rearrange("p (a n) -> p a n", n=P), z, z.unsqueeze(1).to_broadcast([P, 4, P]),
                  start=True, stop=False, skip_group_check=True)

    def turn(pe, src, k, t, bank):
        o = (k % 2) * T + t * P
        return pe.transpose(ps[:, bank, o:o + P], src[:, t, k * P:(k + 1) * P], ident)

    def halves(b):
        return ps[:, b, :].rearrange("p (a n) -> p a n", a=2)

    def on_all(v, n):
        return v.rearrange("(a d) -> a d", a=1).to_broadcast([P, n])

    def rows(v):
        return v.rearrange("(c p) -> c p", p=P)

    def conv_tile(s, j, g):
        return GROUPS * GT + GROUPS * j + g if s == 0 else GT * g + 2 * (s - 1) + j

    def gate_tanh(act, dst, s, col):
        for j in range(2):
            a = act.activation(dst[:, j, :], ps[:, s, j * T:(j + 1) * T], ACT.Tanh,
                               bias=cols_gate[:, bass.ds(col + j, 1)], scale=0.5)
        a.then_inc(bank_free[s], 1)

    with nc.Block() as block:
        @block.sync
        def _(sp):
            wi = w_in[0]

            def up_rows(v):
                return v.rearrange("j (c p) -> (j c) p", p=P)

            x_tiles = x[0].rearrange("(t p) d -> p t d", p=P)
            sp.dma_start(x_nat[:, 0, :], x_tiles[:, 0, :]).then_inc(x_in[0], 16)
            sp.dma_start(x_nat[:, 1, :], x_tiles[:, 1, :]).then_inc(x_in[1], 16)
            sp.dma_start(gain_mix[:], on_all(mix_norm_g[0], D)).then_inc(gain_in, 16)
            sp.dma_start(sq[:], square).then_inc(const_in, 16)
            load_bc(sp, 0, 0)
            n = TAPS * CONV_T
            sp.dma_start(rows_conv[0:n, :], up_rows(ssm_conv_w[0])).then_inc(rows_in, 16)
            sp.dma_start(rows_conv[n:n_conv, :], rows(ssm_conv_b[0])).then_inc(rows_in, 16)
            sp.dma_start(rows_gate[0:3 * KT, :], rows(b_gate[0])).then_inc(rows_in, 16)
            sp.dma_start(rows_gate[3 * KT:5 * KT, :], rows(ssm_norm_g[0])).then_inc(rows_in, 16)
            sp.dma_start(rows_gate[5 * KT:n_gate, :], rows(ffn_norm_g[0])).then_inc(rows_in, 16)
            sp.dma_start(rows_up01[0:n_up01, :], up_rows(ffn_conv_w[0, 0:2])).then_inc(rows_in, 16)
            sp.dma_start(rows_up2[0:2 * FT, :], up_rows(ffn_conv_w[0, 2:3])).then_inc(rows_in, 16)
            sp.dma_start(rows_up2[2 * FT:n_up2, :], rows(ffn_conv_b[0])).then_inc(rows_in, 16)
            sp.dma_start(skip2[0:n_skip, :], ssm_D[0].rearrange("(c j) -> c j", j=2)).then_inc(skip_in, 16)
            sp.dma_start(wdt_raw[:], wi[:, DTC:DTC + P].rearrange("(k p) n -> p k n", p=P)).then_inc(dtw_in, 16)
            load(sp, 0, 1, wi, XC)
            load(sp, 0, 2, wi, XC + CW)
            sp.dma_start(dt_rows[:, 0, :], on_all(ssm_dt_bias[0], SHEADS)).then_inc(dtp_in, 16)
            sp.dma_start(dt_rows[:, 1, :], on_all(ssm_A_log[0], SHEADS)).then_inc(dtp_in, 16)
            sp.dma_start(table_s[0:BUCKETS + 1, :], table).then_inc(relb_in, 16)
            sp.dma_start(relb[0:BUCKETS, :], rel_bias).then_inc(relb_in, 16)
            sp.dma_start(relb[BUCKETS:BUCKETS + 1, :], one_row).then_inc(relb_in, 16)

            def load_acs(g):
                sp.dma_start(acs_b[:, bass.ds(HPG * g, HPG), :], acs_d[bass.ds(HPG * g, HPG), :].rearrange(
                    "(a h) t -> a h t", a=1).to_broadcast([P, HPG, T])).then_inc(acs_in, 16)

            load(sp, 1, 0, wi, ZC)
            load(sp, 1, 1, wi, ZC + CW)
            load(sp, 1, 2, wi, GATEC + D)
            sp.wait_ge(acs_ready, 2)
            sp.dma_start(acs_d, acs_row[0:SHEADS, :]).then_inc(acs_out, 16)
            load_bc(sp, 2, 1)
            sp.wait_ge(acs_out, 16)
            load_acs(0)
            load(sp, 2, 1, wi, XC + GC)
            load(sp, 2, 2, wi, XC + CW + GC)
            sp.wait_ge(acs_in, 16)
            load_acs(1)
            load(sp, 3, 0, wi, ZC + GC)
            load(sp, 3, 1, wi, ZC + CW + GC)
            load(sp, 3, 2, wi, GATEC + D + CW)
            sp.wait_ge(bias_copied, 1)
            sp.dma_start(bias_d, bias_row[0:HEADS, :].unsqueeze(1).to_broadcast([HEADS, P, BIAS_W])
                         ).then_inc(bias_out, 16)
            with sp.Fori(2, GROUPS) as g:
                r = 2 * g
                load_bc(sp, r, g)
                load(sp, r, 1, wi, XC + GC * g)
                load(sp, r, 2, wi, XC + CW + GC * g)
                sp.wait_ge(acs_in, 16 * g)
                load_acs(g)
                load(sp, r + 1, 0, wi, ZC + GC * g)
                load(sp, r + 1, 1, wi, ZC + CW + GC * g)
                load(sp, r + 1, 2, wi, GATEC + D + CW * g)
            load(sp, RB, 0, wi, KC)
            load(sp, RB, 1, wi, QC)
            sp.wait_ge(seg_ready, 6)
            sp.wait_ge(bias_out, 16)
            for c0, at, n in ((0, LAG, P), (P, LAG - P, T)):
                src = bass.AP(tensor=bias_d.tensor, offset=at, ap=[[BIAS_W - 1, P], [P * BIAS_W, HEADS], [1, n]])
                sp.dma_start(bias_t[:, :, c0:c0 + n], src).then_inc(bias_in, 16)
            sp.dma_start(mem_nat[:], mem[0].rearrange("(t p) d -> p t d", p=P)).then_inc(m_in, 16)
            sp.dma_start(gain_mem[:], on_all(mem_norm_g[0], D)).then_inc(m_gain_in, 16)
            load(sp, RB, 2, wi, VC)
            with sp.Fori(1, 4) as i:
                load(sp, RB + i, 0, wi, KC + CW * i)
                load(sp, RB + i, 1, wi, QC + CW * i)
                load(sp, RB + i, 2, wi, VC + CW * i)
            with sp.Fori(0, 4) as i:
                load(sp, RC + i, 0, wi, QMC + CW * i)
                load(sp, RC + i, 1, w_mem_kv[0], CW * i)
                load(sp, RC + i, 2, w_mem_kv[0], D + CW * i)
            with sp.Fori(0, 4) as i:
                load(sp, RD + i, 0, w_br_ssm[0, 0:D], CW * i)
                load(sp, RD + i, 1, w_br_ssm[0, D:2 * D], CW * i)
                load(sp, RD + i, 2, wi, GATEC + CW * i)
            sp.wait_ge(os_lo_s, GROUPS)
            sp.wait_ge(oa_lo_s, 4)
            sp.dma_start(h_nat[:], x_tiles).then_inc(x_again, 16)
            with sp.Fori(0, 4) as i:
                load(sp, RE + i, 0, w_br_attn[0], CW * i)
                load(sp, RE + i, 1, wi, GATEC + 2 * D + CW * i)
                load(sp, RE + i, 2, w_br_mem[0], CW * i)
            for c in range(3):
                load(sp, RF, c, w_out[0], CW * c)
            sp.wait_ge(gemm_done[1], RE)
            sp.dma_start(gain_fin[:], on_all(final_norm_g, D)).then_inc(late_gain, 16)
            load(sp, RF + 1, 0, w_out[0], CW * 3)
            load(sp, RF + 1, 1, w_ffn_up[0], 0)
            load(sp, RF + 1, 2, w_ffn_up[0], FFN)
            with sp.Fori(1, F_STEPS) as f:
                r = f + (RG - 1)
                load(sp, r, 0, w_ffn_up[0], CW * f)
                load(sp, r, 1, w_ffn_up[0], FFN + CW * f)
                load_down(sp, r, 2, f - 1)
            load_down(sp, RG + F_STEPS - 1, 0, F_STEPS - 1)
            for t in range(NT):
                sp.wait_ge(y_scaled, t + 1)
                sp.dma_start(out[0, t * P:(t + 1) * P, :], h_sc[:, t, :]).then_inc(y_out, 16)
            sp.wait_ge(y_out, 16 * NT)

        @block.tensor
        def _(pe):
            pe.wait_ge(const_in, 16)
            for t in range(NT):
                pe.wait_ge(x_scaled, t + 1)
                for k in range(KT):
                    mm = turn(pe, x_sc, k, t, 4 + k // 2)
                    if t and k % 2:
                        mm.then_inc(x_turned, 1)
            pe.wait_ge(rows_in, 16 * 8)
            pe.wait_ge(skip_row, 1)
            at = 0
            for src, n in ((rows_conv, n_conv), (rows_gate, n_gate), (rows_skip, n_skip), (rows_up01, n_up01),
                           (rows_up2, n_up2)):
                mm = pe.transpose(ps[:, 3, at:at + n], src[0:n, :], ident[0:n, 0:n])
                at += n
            mm.then_inc(rows_turned, 1)

            pe.wait_ge(x_lo, KT // 2)
            gemm_cols(pe, 0, 0, tok_hi, tok_lo)
            pe.wait_ge(wdt_lo_s, 1)
            for k in range(KT):
                mm = three(pe, ps[:, 4, 0:T], (wdt_hi[:, k, :], wdt_lo[:, k, :]), (tok_hi[:, k, :], tok_lo[:, k, :]),
                           k == 0, k == KT - 1)
            mm.then_inc(dt_mm, 1)
            pe.wait_ge(relb_in, 48)
            pe.matmul(ps[0:HEADS, 5, 0:BIAS_W], relb[0:BUCKETS + 1, :], table_s[0:BUCKETS + 1, :],
                      start=True, stop=True).then_inc(bias_mm, 1)
            pe.wait_ge(dt_copied, 1)
            for t in range(NT):
                mm = pe.transpose(ps[:, 6, t * SHEADS:(t + 1) * SHEADS], dt_raw[0:SHEADS, t * P:(t + 1) * P],
                                  ident[0:SHEADS, 0:SHEADS])
            mm.then_inc(dt_turned, 1)
            gemm_cols(pe, 0, 1, tok_hi, tok_lo)
            pe.wait_ge(dt_step, 19)
            pe.matmul(ps[:, 7, 0:SHEADS], tri_wide[:, 0:P], da_s[:, 0, :], start=True, stop=True)
            pe.matmul(ps[:, 7, SHEADS:2 * SHEADS], tri_wide[:, P:2 * P], da_s[:, 0, :], start=True, stop=False)
            pe.matmul(ps[:, 7, SHEADS:2 * SHEADS], tri_wide[:, 0:P], da_s[:, 1, :], start=False, stop=True)
            pe.matmul(ps[0:SHEADS, 7, T:2 * T], da_s[:, 0, :], tri_wide[:, 0:T], start=True, stop=False)
            pe.matmul(ps[0:SHEADS, 7, T + P:2 * T], da_s[:, 1, :], tri_wide[:, 0:P], start=False,
                      stop=True).then_inc(acs_mm, 1)
            gemm_cols(pe, 0, 2, tok_hi, tok_lo)

            def rest_of_group(g):
                r = 2 * g + 1
                gemm_cols(pe, r, 0, tok_hi, tok_lo)
                gemm_cols(pe, r, 1, tok_hi, tok_lo)
                pe.wait_ge(conv_done, 3 * g + 3)
                for t in range(NT):
                    for c in range(GT):
                        mm = pe.transpose(ps[:, 3 + t, c * P:(c + 1) * P], conv_o[:, 2 + c, t * P:(t + 1) * P], ident)
                mm.then_inc(xg_turned, 1)
                pe.matmul(ps[:, 5, 0:T], conv_o[:, 0, 0:P], conv_o[:, 1, :], start=True, stop=True)
                pe.matmul(ps[:, 5, T:T + P], conv_o[:, 0, P:T], conv_o[:, 1, P:T], start=True,
                          stop=True).then_inc(cb_mm, 1)
                gemm_cols(pe, r, 2, tok_hi, tok_lo)

            def scan(n):
                pe.wait_ge(xdt_ready, 2 * n)
                pe.wait_ge(decay_cb, n)
                for h in range(HPG):
                    half, c = SHD * (h % 2), h // 2
                    o = ps[half:half + SHD, 6 + c // 2, (c % 2) * T:(c % 2 + 1) * T]
                    pe.matmul(o, x_dt[:, 0, h * SHD:(h + 1) * SHD], decay[:, h, 0:T], start=True, stop=False)
                    mm = pe.matmul(o[:, P:T], x_dt[:, 1, h * SHD:(h + 1) * SHD], decay[:, h, T:T + P], start=False,
                                   stop=True)
                mm.then_inc(y_mm, 1)

            rest_of_group(0)
            with pe.Fori(1, GROUPS) as g:
                gemm_cols(pe, 2 * g, 0, tok_hi, tok_lo)
                gemm_cols(pe, 2 * g, 1, tok_hi, tok_lo)
                scan(g)
                gemm_cols(pe, 2 * g, 2, tok_hi, tok_lo)
                rest_of_group(g)

            def scores(i):
                pe.wait_ge(bank_free[0], RB + 2 + i)
                pe.wait_ge(bank_free[1], RB + 2 + i)
                for a in range(2):
                    pe.matmul(ps[:, 3 + a, 0:P], q_t[:, a, 0:P], k_t[:, a, 0:P], start=True, stop=True)
                    mm = pe.matmul(ps[:, 3 + a, P:3 * P], q_t[:, a, P:T], k_t[:, a, :], start=True, stop=True)
                mm.then_inc(s_mm, 1)

            def turn_probs(n):
                pe.wait_ge(m_lo, KT // 2)
                pe.wait_ge(p_norm, 4 * n)
                for a in range(2):
                    for b in range(3):
                        mm = pe.transpose(ps[:, 5 + a, b * P:(b + 1) * P], prob[:, a, b * P:(b + 1) * P], ident)
                    mm.then_inc(p_turned, 1)

            def attend(n):
                pe.wait_ge(bank_free[2], RB + 1 + n)
                pe.wait_ge(pt_ready, 2 * n)
                for a in range(2):
                    pe.matmul(ps[:, 7, a * T:(a + 1) * T], v_t[:, 0, a * DH:(a + 1) * DH], prob_t[:, a, 0:T],
                              start=True, stop=False)
                    mm = pe.matmul(ps[:, 7, a * T + P:(a + 1) * T], v_t[:, 1, a * DH:(a + 1) * DH],
                                   prob_t[:, a, T:T + P], start=False, stop=True)
                mm.then_inc(o_mm, 1)

            gemm_cols(pe, RB, 0, tok_hi, tok_lo)
            gemm_cols(pe, RB, 1, tok_hi, tok_lo)
            scan(GROUPS)
            gemm_rows(pe, RB, 2, tok_hi, tok_lo)
            scores(0)
            pe.wait_ge(m_scaled, NT)
            for j in range(KT // 2):
                if j >= 2:
                    pe.wait_ge(m_lo, j - 1)
                for k in (2 * j, 2 * j + 1):
                    for t in range(NT):
                        mm = turn(pe, mem_nat, k, t, 5 + j % 2)
                mm.then_inc(m_turned, 1)
            with pe.Fori(1, 4) as i:
                gemm_cols(pe, RB + i, 0, tok_hi, tok_lo)
                turn_probs(i)
                gemm_cols(pe, RB + i, 1, tok_hi, tok_lo)
                attend(i)
                gemm_rows(pe, RB + i, 2, tok_hi, tok_lo)
                scores(i)

            def mem_scores(i):
                pe.wait_ge(bank_free[0], RC + 2 + i)
                pe.wait_ge(bank_free[1], RC + 2 + i)
                for t in range(NT):
                    for d in range(2):
                        mm = pe.matmul(ps[:, 3, t * T:(t + 1) * T], qm_t[:, d, t * P:(t + 1) * P], km_t[:, d, :],
                                       start=d == 0, stop=d == 1)
                mm.then_inc(ms_mm, 1)

            def turn_mem_probs(n):
                pe.wait_ge(mp_norm, 2 * n)
                for m in range(2):
                    for t in range(NT):
                        mm = pe.transpose(ps[:, 4, m * T + t * P:m * T + (t + 1) * P], mprob[:, t, m * P:(m + 1) * P],
                                          ident)
                mm.then_inc(mp_turned, 1)

            def mem_attend(n):
                pe.wait_ge(bank_free[2], RC + 1 + n)
                pe.wait_ge(mpt_ready, n)
                for d in range(2):
                    for m in range(2):
                        mm = pe.matmul(ps[:, 5, d * T:(d + 1) * T], vm_t[:, m, d * P:(d + 1) * P], mprob_t[:, m, :],
                                       start=m == 0, stop=m == 1)
                mm.then_inc(mo_mm, 1)

            pe.wait_ge(sq_step, 3 * GROUPS)
            pe.wait_ge(oa_lo_s, 3)
            for t in range(NT):
                for g in range(GROUPS):
                    n = t * GROUPS + g
                    mm = pe.matmul(ps[:, 7, n:n + 1], sq_g[:, g, t * P:(t + 1) * P], ones[:, 0:1], start=True,
                                   stop=True)
            mm.then_inc(group_mm, 1)
            gemm_cols(pe, RC, 0, tok_hi, tok_lo)
            turn_probs(4)
            pe.wait_ge(group_pow, 1)
            for g in range(GROUPS):
                for t in range(NT):
                    n = t * GROUPS + g
                    o = (g % 2) * T + t * P
                    mm = pe.matmul(ps[:, 3 + g // 2, o:o + P], group_rstd[:, n:n + 1].to_broadcast([P, P]), ident,
                                   start=True, stop=True)
            mm.then_inc(group_spread, 1)
            pe.wait_ge(m_lo, KT // 2)
            gemm_cols(pe, RC, 1, me_hi, me_lo)
            attend(4)
            gemm_rows(pe, RC, 2, me_hi, me_lo)
            pe.wait_ge(rstd_g_ready, 1)
            mem_scores(0)
            with pe.Fori(1, 4) as i:
                gemm_cols(pe, RC + i, 0, tok_hi, tok_lo)
                turn_mem_probs(i)
                gemm_cols(pe, RC + i, 1, me_hi, me_lo)
                mem_attend(i)
                gemm_rows(pe, RC + i, 2, me_hi, me_lo)
                mem_scores(i)

            pe.wait_ge(os_lo_s, GROUPS)
            gemm_cols(pe, RD, 0, os_hi, os_lo, 0, (0, 1), (0, 1), stop=False)
            turn_mem_probs(4)
            gemm_cols(pe, RD, 1, os_hi, os_lo, KT, (0, 1), (), start=False)
            mem_attend(4)
            gemm_cols(pe, RD, 2, tok_hi, tok_lo)
            with pe.Fori(1, 4) as i:
                r = RD + i
                gemm_cols(pe, r, 0, os_hi, os_lo, 0, (0, 1), (0, 1), stop=False)
                gemm_cols(pe, r, 1, os_hi, os_lo, KT, (0, 1), (), start=False)
                gemm_cols(pe, r, 2, tok_hi, tok_lo)

            pe.wait_ge(oa_lo_s, 4)
            pe.wait_ge(om_lo_s, 4)
            with pe.Fori(0, 4) as i:
                r = RE + i
                gemm_cols(pe, r, 0, oa_hi, oa_lo)
                gemm_cols(pe, r, 1, tok_hi, tok_lo)
                gemm_cols(pe, r, 2, om_hi, om_lo)

            pe.wait_ge(zeros_set, 1)
            pe.wait_ge(mg_lo_s, 3)
            for c in range(2):
                pe.wait_ge(lo_ready[c], RF + 2)
                pe.wait_ge(bank_free[c], RF + 1)
                open_bank(pe, c)
                for t in range(NT):
                    rows_part(pe, c, t, range(0, 6), mg_hi, mg_lo, False, False, skip_group_check=True)
            pe.wait_ge(mg_lo_s, 4)
            for c in range(2):
                for t in range(NT):
                    mm = rows_part(pe, c, t, range(6, KT), mg_hi, mg_lo, False, False, skip_group_check=True)
                mm.then_inc(gemm_done[c], 1)
            gemm_rows(pe, RF, 2, mg_hi, mg_lo)

            def turn_h(c):
                for k in (2 * c, 2 * c + 1):
                    for t in range(NT):
                        mm = turn(pe, h_nat, k, t, 4 + c)
                mm.then_inc(h_turned, 1)

            pe.wait_ge(bank_free[0], RF + 2)
            turn_h(0)
            pe.wait_ge(bank_free[1], RF + 2)
            turn_h(1)
            pe.wait_ge(lo_ready[0], RF + 3)
            rows_part(pe, 0, 0, range(KT), mg_hi, mg_lo, True, True)
            pe.wait_ge(bank_free[2], RF + 2)
            turn_h(2)
            rows_part(pe, 0, 1, range(KT), mg_hi, mg_lo, True, True).then_inc(gemm_done[0], 1)

            pe.wait_ge(h_lo, 6)
            for s in (1, 2):
                pe.wait_ge(lo_ready[s], RF + 3)
                cols_part(pe, s, 0, range(0, 6), ps[:, s, 0:T], tok_hi, tok_lo, stop=False)
                if s == 1:
                    pe.wait_ge(bank_free[0], RF + 3)
                    turn_h(3)
            pe.wait_ge(h_lo, KT)
            for s in (1, 2):
                cols_part(pe, s, 0, range(6, KT), ps[:, s, 0:T], tok_hi, tok_lo, start=False)
                cols_part(pe, s, 1, range(KT), ps[:, s, T:2 * T], tok_hi, tok_lo).then_inc(gemm_done[s], 1)
                if s == 1:
                    pe.wait_ge(h_rstd, NT)
                    for t in range(NT):
                        mm = pe.matmul(ps[:, 3, t * P:(t + 1) * P], stat[:, 4 + t:5 + t].to_broadcast([P, P]), ident,
                                       start=True, stop=True)
                    mm.then_inc(h_spread, 1)
                    for b in range(4, 8):
                        open_bank(pe, b)
            with pe.Fori(1, F_STEPS) as f:
                r = f + (RG - 1)
                gemm_cols(pe, r, 0, tok_hi, tok_lo)
                gemm_cols(pe, r, 1, tok_hi, tok_lo)
                pe.wait_ge(hid_lo_s, f)
                pe.wait_ge(lo_ready[2], r + 2)
                down_part(pe, 2, 0)
                down_part(pe, 2, 1).then_inc(gemm_done[2], 1)
            pe.wait_ge(hid_lo_s, F_STEPS)
            pe.wait_ge(lo_ready[0], RG + F_STEPS + 1)
            for t in range(NT):
                down_part(pe, 0, t).then_inc(down_done, 1)

        @block.scalar
        def _(act):
            for t in range(NT):
                act.wait_ge(x_in[t], 16)
                act.activation(x_sc[:, t, :], x_nat[:, t, :], ACT.Square,
                               accum_out=stat[:, t:t + 1]).then_inc(x_sumsq, 1)
            split_hi(act, 0, 0, first=True)
            for j in range(KT // 2):
                act.wait_ge(x_turned, j + 1)
                act.activation(tok_hi[:, 2 * j:2 * j + 2, :], halves(4 + j), ACT.Copy).then_inc(x_hi, 1)
            act.wait_ge(dtw_in, 16)
            act.activation(wdt_hi[:], wdt_raw[:], ACT.Copy).then_inc(wdt_hi_s, 1)
            split_hi(act, 0, 1, first=True)
            split_hi(act, 0, 2, first=True)
            act.wait_ge(dtp_in, 32)
            act.activation(a_neg[:], dt_rows[:, 1, :], ACT.Exp).then_inc(a_exp, 1)

            def group(g, first=False):
                r = 2 * g
                for s in range(SLOTS):
                    act.wait_ge(gemm_done[s], r + 1)
                    if first and s == 0:
                        act.wait_ge(params_ready, 12)
                    for j in range(2):
                        c = conv_tile(s, j, g)
                        act.activation(conv_a[:, s, j, :], ps[:, s, j * T:(j + 1) * T], ACT.Identity,
                                       bias=cols_conv[:, TAPS, bass.ds(c, 1)],
                                       scale=cols_conv[:, TAPS - 1, bass.ds(c, 1)])
                    act.activation(pad_x[:, s, :, TAPS - 1:], halves(s), ACT.Copy).then_inc(bank_free[s], 1)
                    split_hi(act, r + 1, s)
                    act.wait_ge(conv_step, 18 * g + 6 * s + 6)
                    act.activation(tanh_a[:, s], conv_a[:, s], ACT.Tanh).then_inc(conv_tanh, 1)
                    if first and s == 0:
                        act.wait_ge(dt_step, 2)
                        act.activation(dt_w[2][:], dt_w[1][:], ACT.Exp).then_inc(dt_exp, 1)
                for s in range(2):
                    act.wait_ge(gemm_done[s], r + 2)
                    act.wait_ge(conv_done, 3 * g + s + 1)
                    act.activation(tanh_a[:, s], halves(s), ACT.Tanh, scale=0.5).then_inc(z_tanh, 1)
                    split_hi(act, r + 2, s)
                act.wait_ge(gemm_done[2], r + 2)
                act.wait_ge(conv_done, 3 * g + 3)
                gate_tanh(act, tanh_a[:, 2], 2, KT + 2 * g)
                split_hi(act, r + 2, 2)
                act.wait_ge(seg_clamped, 2 * g + 2)
                act.activation(decay[:], decay[:], ACT.Exp).then_inc(decay_ready, 1)

            group(0, first=True)
            with act.Fori(1, GROUPS) as g:
                group(g)

            def heads(i, first=False):
                r = RB + i
                split_hi(act, r + 1, 0)
                if not first:
                    act.wait_ge(p_turned, 2 * i - 1)
                    act.activation(prob_t[:, 0, :], ps[:, 5, 0:3 * P], ACT.Copy).then_inc(pt_ready, 1)
                act.wait_ge(gemm_done[1], r + 1)
                act.activation(q_t[:], halves(1), ACT.Copy, scale=DH ** -0.5).then_inc(bank_free[1], 1)
                split_hi(act, r + 1, 1)
                if first:
                    act.wait_ge(m_in, 16)
                    act.wait_ge(seg_ready, 2 * GROUPS)
                    for t in range(NT):
                        act.activation(junk_m[:, t, :], mem_nat[:, t, :], ACT.Square,
                                       accum_out=stat[:, 2 + t:3 + t]).then_inc(m_sumsq, 1)
                else:
                    act.wait_ge(o_mm, i)
                    act.activation(oa_hi[:, bass.ds(2 * (i - 1), 2), :], halves(7), ACT.Copy).then_inc(oa_hi_s, 1)
                act.wait_ge(gemm_done[2], r + 1)
                act.activation(v_t[:], halves(2), ACT.Copy).then_inc(bank_free[2], 1)
                split_hi(act, r + 1, 2)
                act.wait_ge(s_neg, i + 1)
                for a in range(2):
                    for t in range(NT):
                        part = prob[:, a, 0:P] if t == 0 else prob[:, a, P:3 * P]
                        n = 2 * t + a
                        act.activation(part, part, ACT.Exp, bias=soft[:, 1, n:n + 1],
                                       accum_out=soft[:, 2, n:n + 1]).then_inc(p_exp, 1)

            heads(0, first=True)
            for j in range(KT // 2):
                act.wait_ge(m_turned, j + 1)
                act.activation(me_hi[:, 2 * j:2 * j + 2, :], halves(5 + j % 2), ACT.Copy).then_inc(m_hi, 1)
            with act.Fori(1, 4) as i:
                heads(i)

            def mem_head(i, first=False):
                r = RC + i
                act.wait_ge(gemm_done[0], r + 1)
                act.activation(qm_t[:], halves(0), ACT.Copy).then_inc(bank_free[0], 1)
                split_hi(act, r + 1, 0)
                if first:
                    act.wait_ge(p_turned, 7)
                    act.activation(prob_t[:, 0, :], ps[:, 5, 0:3 * P], ACT.Copy).then_inc(pt_ready, 1)
                    act.wait_ge(group_spread, 1)
                    act.activation(rstd_g[:].rearrange("p a n -> p (a n)"), ps[:, 3:5, :].rearrange("p a n -> p (a n)"),
                                   ACT.Copy).then_inc(rstd_g_ready, 1)
                else:
                    act.wait_ge(mp_turned, i)
                    act.activation(mprob_t[:], halves(4), ACT.Copy).then_inc(mpt_ready, 1)
                act.wait_ge(norm_step, GT * i + GT)
                act.activation(os_hi[:, bass.ds(GT * i, GT), :], o_tmp[:], ACT.Copy).then_inc(os_hi_s, 1)
                act.wait_ge(gemm_done[1], r + 1)
                act.activation(km_t[:], halves(1), ACT.Copy).then_inc(bank_free[1], 1)
                split_hi(act, r + 1, 1)
                if first:
                    act.wait_ge(o_mm, 4)
                    act.activation(oa_hi[:, KT - 2:KT, :], halves(7), ACT.Copy).then_inc(oa_hi_s, 1)
                else:
                    act.wait_ge(mo_mm, i)
                    act.activation(om_hi[:, bass.ds(2 * (i - 1), 2), :], halves(5), ACT.Copy).then_inc(om_hi_s, 1)
                act.wait_ge(gemm_done[2], r + 1)
                act.activation(vm_t[:], halves(2), ACT.Copy).then_inc(bank_free[2], 1)
                act.wait_ge(ms_neg, i + 1)
                for t in range(NT):
                    act.activation(mprob[:, t, :], ps[:, 3, t * T:(t + 1) * T], ACT.Exp, bias=msoft[:, 1, t:t + 1],
                                   scale=MDH ** -0.5, accum_out=msoft[:, 2, t:t + 1]).then_inc(mp_exp, 1)
                split_hi(act, r + 1, 2)

            mem_head(0, first=True)
            with act.Fori(1, 4) as i:
                mem_head(i)

            def ssm_columns(i, first=False):
                r = RD + i
                split_hi(act, r + 1, 0)
                if first:
                    act.wait_ge(mp_turned, 4)
                    act.activation(mprob_t[:], halves(4), ACT.Copy).then_inc(mpt_ready, 1)
                split_hi(act, r + 1, 1)
                if first:
                    act.wait_ge(mo_mm, 4)
                    act.activation(om_hi[:, KT - 2:KT, :], halves(5), ACT.Copy).then_inc(om_hi_s, 1)
                act.wait_ge(gemm_done[2], r + 1)
                gate_tanh(act, tanh_d, 2, 2 * i)
                split_hi(act, r + 1, 2)

            ssm_columns(0, first=True)
            with act.Fori(1, 4) as i:
                ssm_columns(i)

            with act.Fori(0, 4) as i:
                r = RE + i
                split_hi(act, r + 1, 0)
                act.wait_ge(gemm_done[1], r + 1)
                gate_tanh(act, tanh_e, 1, 2 * KT + 2 * i)
                split_hi(act, r + 1, 1)
                act.wait_ge(e_summed, i + 1)
                act.activation(mg_hi[:, bass.ds(2 * i, 2), :], e_sum[:], ACT.Copy).then_inc(mg_hi_s, 1)
                split_hi(act, r + 1, 2)

            def h_high(c):
                act.wait_ge(h_turned, c + 1)
                for j in range(2):
                    k = 2 * c + j
                    act.activation(tok_hi[:, k, :], ps[:, 4 + c, j * T:(j + 1) * T], ACT.Copy,
                                   scale=cols_gate[:, 5 * KT + k:5 * KT + k + 1]).then_inc(h_hi, 1)

            split_hi(act, RF + 1, 0)
            split_hi(act, RF + 1, 1)
            h_high(0)
            h_high(1)
            split_hi(act, RF + 1, 2)
            h_high(2)
            h_high(3)
            for t in range(NT):
                act.activation(h_sc[:, t, :], h_nat[:, t, :], ACT.Square,
                               accum_out=stat[:, 4 + t:5 + t]).then_inc(h_sumsq, 1)
            split_hi(act, RG, 0)

            def ffn(f, sa, ra, sb, rb, after_gate, after_up, last, first=False):
                for n, (s, r, pad, conv, tile) in enumerate(((sa, ra, pad_g, conv_g, 0), (sb, rb, pad_u, conv_u, FT))):
                    act.wait_ge(bank_free[s], r + 2)
                    if not first:
                        act.wait_ge((g_silu, hid_done)[n], f)
                    for j in range(2):
                        c = tile + 2 * f + j
                        act.activation(conv[:, j, :], pad[:, j, FTAPS - 1:], ACT.Identity,
                                       bias=cols_up[:, FTAPS, bass.ds(c, 1)],
                                       scale=cols_up[:, FTAPS - 1, bass.ds(c, 1)]).then_inc(conv_begun, 1)
                    for rr, ss in (after_gate, after_up)[n]:
                        split_hi(act, rr, ss)
                    if n == 0:
                        act.wait_ge(f_step, 8 * f + 4)
                        act.activation(tanh_g[:], conv_g[:], ACT.Tanh).then_inc(g_tanh, 1)
                act.wait_ge(hid_done, f + 1)
                if not first:
                    act.wait_ge(gemm_done[2], f + RG)
                act.activation(hid_hi[:], hid[:], ACT.Copy).then_inc(hid_hi_s, 1)
                for rr, ss in last:
                    split_hi(act, rr, ss)

            ffn(0, 1, RF + 1, 2, RF + 1, [(RG, 1)], [(RG, 2)], [], first=True)
            with act.Fori(1, F_STEPS - 1) as f:
                r = f + (RG - 1)
                ffn(f, 0, r, 1, r, [(r + 1, 0)], [(r + 1, 1)], [(r + 1, 2)])
            r = RG + F_STEPS - 2
            ffn(F_STEPS - 1, 0, r, 1, r, [(r + 1, 0)], [], [])
            for t in range(NT):
                act.wait_ge(y_added, t + 1)
                act.activation(h_sc[:, t, :], h_nat[:, t, :], ACT.Square,
                               accum_out=stat[:, 6 + t:7 + t]).then_inc(y_sumsq, 1)

        @block.vector
        def _(dve):
            def gate(dst, src, done):
                dve.tensor_scalar(dst, src, 0.5, 0.5, ALU.mult, ALU.add).then_inc(done, 1)

            for s in range(SLOTS):
                dve.memset(pad_x[:, s, 0, 0:TAPS - 1], 0.0).then_inc(lo_ready[s], 1)
                dve.memset(pad_x[:, s, 1, 0:TAPS - 1], 0.0).then_inc(bank_free[s], 1)
            dve.memset(pow_c[:], -0.5).then_inc(pow_set, 1)
            dve.memset(zero_s[:], 0.0).then_inc(zeros_set, 1)
            dve.wait_ge(gain_in, 16)
            for t in range(NT):
                dve.wait_ge(x_rstd, t + 1)
                dve.scalar_tensor_tensor(x_sc[:, t, :], x_nat[:, t, :], stat[:, t:t + 1], gain_mix[:], ALU.mult,
                                         ALU.mult).then_inc(x_scaled, 1)
            split_lo(dve, 0, 0)
            for j in range(KT // 2):
                dve.wait_ge(x_hi, j + 1)
                two = slice(2 * j, 2 * j + 2)
                dve.tensor_tensor(tok_lo[:, two, :], halves(4 + j), tok_hi[:, two, :].bitcast(F32),
                                  ALU.subtract).then_inc(x_lo, 1)
            dve.wait_ge(skip_in, 16)
            dve.tensor_copy(rows_skip[0:n_skip, :].rearrange("p (j n) -> p j n", j=2),
                            skip2[0:n_skip, :].unsqueeze(2).to_broadcast([n_skip, 2, SHD])).then_inc(skip_row, 1)
            dve.wait_ge(wdt_hi_s, 1)
            dve.tensor_tensor(wdt_lo[:], wdt_raw[:], wdt_hi[:].bitcast(F32), ALU.subtract).then_inc(wdt_lo_s, 1)
            dve.wait_ge(rows_turned, 1)
            at = [0]

            def take(dst, n, scale):
                dve.tensor_scalar(dst, ps[:, 3, at[0]:at[0] + n], scale, None, ALU.mult).then_inc(params_ready, 1)
                at[0] += n

            take(cols_conv[:].rearrange("p a c -> p (a c)"), n_conv, 0.5)
            take(cols_gate[:, 0:3 * KT], 3 * KT, 0.5)
            take(cols_gate[:, 3 * KT:n_gate], n_gate - 3 * KT, 1.0)
            take(cols_skip[:], n_skip, 1.0)
            for j in range(4):
                take(cols_up[:, j, 0:FT], FT, 0.5)
                take(cols_up[:, j, FT:2 * FT], FT, 1.0)
            for s in (1, 2):
                split_lo(dve, 0, s)

            def softplus():
                v, m, e, s_, q, p = dt_w
                steps = [0]

                def step(ins):
                    steps[0] += 1
                    ins.then_inc(dt_step, 1)
                    dve.wait_ge(dt_step, steps[0])

                dve.wait_ge(dt_mm, 1)
                dve.tensor_copy(dt_raw[0:SHEADS, :], ps[0:SHEADS, 4, 0:T]).then_inc(dt_copied, 1)
                dve.wait_ge(bias_mm, 1)
                dve.tensor_copy(bias_row[0:HEADS, :], ps[0:HEADS, 5, 0:BIAS_W]).then_inc(bias_copied, 1)
                dve.wait_ge(dtp_in, 32)
                dve.wait_ge(dt_turned, 1)
                step(dve.tensor_tensor(v[:], ps[:, 6, 0:NT * SHEADS].rearrange("p (t h) -> p t h", t=NT),
                                       dt_rows[:, 0:1, :].to_broadcast([P, NT, SHEADS]), ALU.add))
                step(dve.scalar_tensor_tensor(m[:], v[:], -1.0, v[:], ALU.mult, ALU.min))
                dve.wait_ge(dt_exp, 1)
                step(dve.tensor_scalar(m[:], e[:], 2.0, None, ALU.add))
                step(dve.reciprocal(q[:], m[:]))
                step(dve.tensor_tensor(s_[:], e[:], q[:], ALU.mult))
                step(dve.tensor_tensor(q[:], s_[:], s_[:], ALU.mult))
                step(dve.tensor_scalar(p[:], q[:], 1.0 / 17, None, ALU.mult))
                for n in (15, 13, 11, 9, 7, 5, 3):
                    step(dve.scalar_tensor_tensor(p[:], p[:], 1.0 / n, q[:], ALU.add, ALU.mult))
                step(dve.scalar_tensor_tensor(p[:], p[:], 1.0, s_[:], ALU.add, ALU.mult))
                step(dve.tensor_scalar(m[:], v[:], 0.0, None, ALU.max))
                step(dve.scalar_tensor_tensor(dt_s[:], p[:], 2.0, m[:], ALU.mult, ALU.add))
                dve.wait_ge(a_exp, 1)
                step(dve.tensor_scalar(a_neg[:], a_neg[:], -1.0, None, ALU.mult))
                step(dve.tensor_tensor(da_s[:], dt_s[:], a_neg[:].unsqueeze(1).to_broadcast([P, NT, SHEADS]),
                                       ALU.mult))
                assert steps[0] == 19

            def take_decay_sums():
                dve.wait_ge(acs_mm, 1)
                dve.tensor_copy(acs_s[:].rearrange("p t h -> p (t h)"), ps[:, 7, 0:NT * SHEADS]).then_inc(acs_ready, 1)
                dve.tensor_copy(acs_row[0:SHEADS, :], ps[0:SHEADS, 7, T:2 * T]).then_inc(acs_ready, 1)

            def scan_out(n):
                dve.wait_ge(y_mm, n)
                for c in range(GT):
                    dve.scalar_tensor_tensor(y_sum[:, c, :], conv_o[:, 2 + c, :],
                                             cols_skip[:, bass.ds(GT * n - GT + c, 1)],
                                             ps[:, 6 + c // 2, (c % 2) * T:(c % 2 + 1) * T], ALU.mult,
                                             ALU.add).then_inc(y_step, 1)
                dve.wait_ge(y_step, GT * n)
                dve.scalar_tensor_tensor(v_ssm[:, bass.ds(GT * n - GT, GT), :], z_act[:], 0.5, y_sum[:], ALU.mult,
                                         ALU.mult).then_inc(v_ready, 1)

            def group(g, first=False):
                r = 2 * g

                def convolve(s):
                    dve.wait_ge(bank_free[s], r + 2)
                    for tap in range(TAPS - 1):
                        for j in range(2):
                            n = 18 * g + 6 * s + 2 * tap + j
                            if tap:
                                dve.wait_ge(conv_step, n - 1)
                            dve.scalar_tensor_tensor(
                                conv_a[:, s, j, :], pad_x[:, s, j, tap:tap + T],
                                cols_conv[:, tap, bass.ds(conv_tile(s, j, g), 1)], conv_a[:, s, j, :], ALU.mult,
                                ALU.add).then_inc(conv_step, 1)

                def activate(s):
                    dve.wait_ge(conv_tanh, 3 * g + s + 1)
                    dve.scalar_tensor_tensor(conv_o[:, 2 * s:2 * s + 2, :], tanh_a[:, s], 1.0, conv_a[:, s], ALU.add,
                                             ALU.mult).then_inc(conv_done, 1)

                def silu_z(s):
                    dve.wait_ge(z_tanh, 2 * g + s + 1)
                    dve.scalar_tensor_tensor(z_act[:, 2 * s:2 * s + 2, :], tanh_a[:, s], 1.0, halves(s), ALU.add,
                                             ALU.mult).then_inc(bank_free[s], 1)
                    split_lo(dve, r + 2, s)

                convolve(0)
                split_lo(dve, r + 1, 0)
                activate(0)
                if first:
                    softplus()
                convolve(1)
                split_lo(dve, r + 1, 1)
                if first:
                    take_decay_sums()
                else:
                    scan_out(g)
                activate(1)
                convolve(2)
                split_lo(dve, r + 1, 2)
                activate(2)
                silu_z(0)
                silu_z(1)
                dve.wait_ge(xg_turned, g + 1)
                for t in range(NT):
                    dve.tensor_tensor(x_dt[:, t, :].rearrange("p (h n) -> p h n", n=SHD),
                                      ps[:, 3 + t, :].rearrange("p (h n) -> p h n", n=SHD),
                                      dt_s[:, t, bass.ds(HPG * g, HPG)].unsqueeze(2).to_broadcast([P, HPG, SHD]),
                                      ALU.mult).then_inc(xdt_ready, 1)
                dve.wait_ge(cb_mm, g + 1)
                dve.tensor_tensor(cb[:], ps[:, 5, 0:3 * P], cb_mask, ALU.mult).then_inc(cb_masked, 1)
                dve.wait_ge(seg_ready, 2 * g + 2)
                for c in (slice(0, P), slice(T, T + P)):
                    dve.tensor_scalar(decay[:, :, c], decay[:, :, c], 0.0, None, ALU.min).then_inc(seg_clamped, 1)
                dve.wait_ge(bank_free[2], r + 3)
                gate(g1[:, bass.ds(2 * g, 2), :], tanh_a[:, 2], g1_ready)
                split_lo(dve, r + 2, 2)
                dve.wait_ge(cb_masked, g + 1)
                dve.wait_ge(decay_ready, g + 1)
                dve.tensor_tensor(decay[:], decay[:], cb[:].unsqueeze(1).to_broadcast([P, HPG, 3 * P]),
                                  ALU.mult).then_inc(decay_cb, 1)

            group(0, first=True)
            with dve.Fori(1, GROUPS) as g:
                group(g)

            def heads(i, first=False):
                r = RB + i
                dve.wait_ge(gemm_done[0], r + 1)
                dve.tensor_copy(k_t[:], halves(0)).then_inc(bank_free[0], 1)
                split_lo(dve, r + 1, 0)
                if not first:
                    dve.wait_ge(p_turned, 2 * i)
                    dve.tensor_copy(prob_t[:, 1, :], ps[:, 6, 0:3 * P]).then_inc(pt_ready, 1)
                split_lo(dve, r + 1, 1)
                if first:
                    scan_out(GROUPS)
                    dve.wait_ge(m_gain_in, 16)
                    for t in range(NT):
                        dve.wait_ge(m_rstd, t + 1)
                        dve.scalar_tensor_tensor(mem_nat[:, t, :], mem_nat[:, t, :], stat[:, 2 + t:3 + t],
                                                 gain_mem[:], ALU.mult, ALU.mult).then_inc(m_scaled, 1)
                    dve.wait_ge(bias_in, 32)
                    dve.wait_ge(v_ready, GROUPS)
                else:
                    dve.wait_ge(oa_hi_s, i)
                    last = bass.ds(2 * (i - 1), 2)
                    dve.tensor_tensor(oa_lo[:, last, :], halves(7), oa_hi[:, last, :].bitcast(F32),
                                      ALU.subtract).then_inc(oa_lo_s, 1)
                dve.wait_ge(s_mm, i + 1)
                dve.tensor_tensor(prob[:], ps[:, 3:5, 0:3 * P], bias_t[:, bass.ds(2 * i, 2), :],
                                  ALU.add).then_inc(s_biased, 1)
                dve.wait_ge(s_biased, i + 1)
                dve.tensor_reduce(soft[:, 0, 0:2], prob[:, :, 0:P], AX, ALU.max).then_inc(s_max, 1)
                dve.tensor_reduce(soft[:, 0, 2:4], prob[:, :, P:3 * P], AX, ALU.max).then_inc(s_max, 1)
                dve.wait_ge(s_max, 2 * i + 2)
                dve.tensor_scalar(soft[:, 1, :], soft[:, 0, :], -1.0, None, ALU.mult).then_inc(s_neg, 1)
                dve.wait_ge(p_exp, 4 * i + 4)
                dve.reciprocal(soft[:, 3, :], soft[:, 2, :]).then_inc(p_rec, 1)
                dve.wait_ge(p_rec, i + 1)
                for a in range(2):
                    for t in range(NT):
                        part = prob[:, a, 0:P] if t == 0 else prob[:, a, P:3 * P]
                        dve.tensor_scalar(part, part, soft[:, 3, 2 * t + a:2 * t + a + 1], None,
                                          ALU.mult).then_inc(p_norm, 1)
                split_lo(dve, r + 1, 2)

            heads(0, first=True)
            for j in range(KT // 2):
                dve.wait_ge(m_hi, j + 1)
                two = slice(2 * j, 2 * j + 2)
                dve.tensor_tensor(me_lo[:, two, :], halves(5 + j % 2), me_hi[:, two, :].bitcast(F32),
                                  ALU.subtract).then_inc(m_lo, 1)
            with dve.Fori(1, 4) as i:
                heads(i)
            dve.wait_ge(group_mm, 1)
            dve.tensor_scalar(group_rstd[:], ps[:, 7, 0:NT * GROUPS], 1.0 / GC, EPS, ALU.mult,
                              ALU.add).then_inc(group_var, 1)

            def mem_head(i, first=False):
                r = RC + i
                split_lo(dve, r + 1, 0)
                if first:
                    dve.wait_ge(p_turned, 8)
                    dve.tensor_copy(prob_t[:, 1, :], ps[:, 6, 0:3 * P]).then_inc(pt_ready, 1)
                    dve.wait_ge(rstd_g_ready, 1)
                for c in range(GT):
                    dve.scalar_tensor_tensor(o_tmp[:, c, :], v_ssm[:, bass.ds(GT * i + c, 1), :].squeeze(1),
                                             cols_gate[:, bass.ds(3 * KT + GT * i + c, 1)],
                                             rstd_g[:, bass.ds(i, 1), :].squeeze(1), ALU.mult,
                                             ALU.mult).then_inc(norm_step, 1)
                split_lo(dve, r + 1, 1)
                dve.wait_ge(os_hi_s, i + 1)
                four = bass.ds(GT * i, GT)
                dve.tensor_tensor(os_lo[:, four, :], o_tmp[:], os_hi[:, four, :].bitcast(F32),
                                  ALU.subtract).then_inc(os_lo_s, 1)
                if first:
                    dve.wait_ge(oa_hi_s, 4)
                    dve.tensor_tensor(oa_lo[:, KT - 2:KT, :], halves(7), oa_hi[:, KT - 2:KT, :].bitcast(F32),
                                      ALU.subtract).then_inc(oa_lo_s, 1)
                else:
                    dve.wait_ge(om_hi_s, i)
                    last = bass.ds(2 * (i - 1), 2)
                    dve.tensor_tensor(om_lo[:, last, :], halves(5), om_hi[:, last, :].bitcast(F32),
                                      ALU.subtract).then_inc(om_lo_s, 1)
                dve.wait_ge(ms_mm, i + 1)
                dve.tensor_reduce(msoft[:, 0, :], halves(3), AX, ALU.max).then_inc(ms_max, 1)
                dve.wait_ge(ms_max, i + 1)
                dve.tensor_scalar(msoft[:, 1, :], msoft[:, 0, :], -(MDH ** -0.5), None, ALU.mult).then_inc(ms_neg, 1)
                dve.wait_ge(mp_exp, 2 * i + 2)
                dve.reciprocal(msoft[:, 3, :], msoft[:, 2, :]).then_inc(mp_rec, 1)
                dve.wait_ge(mp_rec, i + 1)
                for t in range(NT):
                    dve.tensor_scalar(mprob[:, t, :], mprob[:, t, :], msoft[:, 3, t:t + 1], None,
                                      ALU.mult).then_inc(mp_norm, 1)
                split_lo(dve, r + 1, 2)

            mem_head(0, first=True)
            with dve.Fori(1, 4) as i:
                mem_head(i)

            def ssm_columns(i, first=False):
                r = RD + i
                split_lo(dve, r + 1, 0)
                dve.wait_ge(gemm_done[1], r + 1)
                for j in range(2):
                    tile = bass.ds(2 * i + j, 1)
                    dve.tensor_tensor(merged[:, tile, :], ps[:, j:j + 1, 0:T], g1[:, tile, :],
                                      ALU.mult).then_inc(bank_free[j], 1)
                split_lo(dve, r + 1, 1)
                if first:
                    dve.wait_ge(om_hi_s, 4)
                    dve.tensor_tensor(om_lo[:, KT - 2:KT, :], halves(5), om_hi[:, KT - 2:KT, :].bitcast(F32),
                                      ALU.subtract).then_inc(om_lo_s, 1)
                dve.wait_ge(bank_free[2], r + 2)
                gate(g0[:, bass.ds(2 * i, 2), :], tanh_d[:], g0_ready)
                split_lo(dve, r + 1, 2)

            ssm_columns(0, first=True)
            with dve.Fori(1, 4) as i:
                ssm_columns(i)

            dve.wait_ge(g0_ready, 4)
            with dve.Fori(0, 4) as i:
                r = RE + i
                two = bass.ds(2 * i, 2)
                dve.wait_ge(gemm_done[0], r + 1)
                dve.tensor_tensor(e_attn[:], halves(0), g0[:, two, :], ALU.mult).then_inc(bank_free[0], 1)
                split_lo(dve, r + 1, 0)
                dve.wait_ge(bank_free[0], r + 2)
                dve.tensor_tensor(e_attn[:], e_attn[:], merged[:, two, :], ALU.add).then_inc(e_step, 1)
                dve.wait_ge(bank_free[1], r + 2)
                gate(e_gate[:], tanh_e[:], e_step)
                split_lo(dve, r + 1, 1)
                dve.wait_ge(e_step, 2 * i + 2)
                dve.wait_ge(gemm_done[2], r + 1)
                dve.tensor_tensor(e_mem[:], halves(2), e_gate[:], ALU.mult).then_inc(bank_free[2], 1)
                dve.wait_ge(bank_free[2], r + 2)
                dve.tensor_tensor(e_sum[:], e_attn[:], e_mem[:], ALU.add).then_inc(e_summed, 1)
                dve.wait_ge(mg_hi_s, i + 1)
                dve.tensor_tensor(mg_lo[:, two, :], e_sum[:], mg_hi[:, two, :].bitcast(F32),
                                  ALU.subtract).then_inc(mg_lo_s, 1)
                split_lo(dve, r + 1, 2)

            def add_h(r, s, c):
                dve.wait_ge(gemm_done[s], r + 1)
                part = h_nat[:, :, c * CW:(c + 1) * CW]
                dve.tensor_tensor(part, halves(s), part, ALU.add).then_inc(bank_free[s], 1)

            def h_low(c):
                dve.wait_ge(h_hi, 2 * c + 2)
                for j in range(2):
                    k = 2 * c + j
                    dve.scalar_tensor_tensor(tok_lo[:, k, :], ps[:, 4 + c, j * T:(j + 1) * T],
                                             cols_gate[:, 5 * KT + k:5 * KT + k + 1], tok_hi[:, k, :].bitcast(F32),
                                             ALU.mult, ALU.subtract).then_inc(h_lo, 1)

            dve.memset(pad_g[:, :, 0:FTAPS - 1], 0.0).then_inc(pads_zero, 1)
            dve.memset(pad_u[:, :, 0:FTAPS - 1], 0.0).then_inc(pads_zero, 1)
            dve.wait_ge(x_again, 16)
            add_h(RF, 0, 0)
            add_h(RF, 1, 1)
            split_lo(dve, RF + 1, 0)
            split_lo(dve, RF + 1, 1)
            add_h(RF, 2, 2)
            h_low(0)
            h_low(1)
            split_lo(dve, RF + 1, 2)
            h_low(2)
            add_h(RF + 1, 0, 3)
            h_low(3)
            split_lo(dve, RG, 0)
            dve.wait_ge(h_spread, 1)
            dve.tensor_copy(rstd_b[:], ps[:, 3, 0:T]).then_inc(rstd_b_ready, 1)
            dve.wait_ge(rstd_b_ready, 1)
            dve.wait_ge(pads_zero, 2)

            def ffn(f, sa, ra, sb, rb, after_gate, after_up, last):
                def convolve(n, s, r, pad, conv, tile):
                    dve.wait_ge(gemm_done[s], r + 1)
                    dve.tensor_tensor(pad[:, :, FTAPS - 1:], halves(s), rstd_b[:].unsqueeze(1).to_broadcast([P, 2, T]),
                                      ALU.mult).then_inc(bank_free[s], 1)
                    dve.wait_ge(conv_begun, 4 * f + 2 * n + 2)
                    for tap in range(FTAPS - 1):
                        for j in range(2):
                            m = 8 * f + 4 * n + 2 * tap + j
                            if tap:
                                dve.wait_ge(f_step, m - 1)
                            dve.scalar_tensor_tensor(conv[:, j, :], pad[:, j, tap:tap + T],
                                                     cols_up[:, tap, bass.ds(tile + 2 * f + j, 1)], conv[:, j, :],
                                                     ALU.mult, ALU.add).then_inc(f_step, 1)

                convolve(0, sa, ra, pad_g, conv_g, 0)
                for rr, ss in after_gate:
                    split_lo(dve, rr, ss)
                dve.wait_ge(g_tanh, f + 1)
                dve.scalar_tensor_tensor(silu_g[:], tanh_g[:], 1.0, conv_g[:], ALU.add, ALU.mult).then_inc(g_silu, 1)
                convolve(1, sb, rb, pad_u, conv_u, FT)
                dve.wait_ge(g_silu, f + 1)
                dve.wait_ge(f_step, 8 * f + 8)
                dve.tensor_tensor(hid[:], silu_g[:], conv_u[:], ALU.mult).then_inc(hid_done, 1)
                for rr, ss in after_up:
                    split_lo(dve, rr, ss)
                dve.wait_ge(hid_hi_s, f + 1)
                dve.tensor_tensor(hid_lo[:], hid[:], hid_hi[:].bitcast(F32), ALU.subtract).then_inc(hid_lo_s, 1)
                for rr, ss in last:
                    split_lo(dve, rr, ss)

            ffn(0, 1, RF + 1, 2, RF + 1, [(RG, 1)], [(RG, 2)], [])
            with dve.Fori(1, F_STEPS - 1) as f:
                r = f + (RG - 1)
                ffn(f, 0, r, 1, r, [(r + 1, 0)], [(r + 1, 1)], [(r + 1, 2)])
            r = RG + F_STEPS - 2
            ffn(F_STEPS - 1, 0, r, 1, r, [(r + 1, 0)], [], [])
            for t in range(NT):
                dve.wait_ge(down_done, t + 1)
                part = h_nat[:, t, :].rearrange("p (a n) -> p a n", a=2)
                dve.tensor_tensor(part, ps[:, 4 + 2 * t:6 + 2 * t, :], part, ALU.add).then_inc(y_added, 1)
            dve.wait_ge(late_gain, 16)
            for t in range(NT):
                dve.wait_ge(y_rstd, t + 1)
                dve.scalar_tensor_tensor(h_sc[:, t, :], h_nat[:, t, :], stat[:, 6 + t:7 + t], gain_fin[:], ALU.mult,
                                         ALU.mult).then_inc(y_scaled, 1)

        @block.gpsimd
        def _(pool):
            def rstd(c, sumsq, var, done):
                for t in range(NT):
                    col = stat[:, c + t:c + t + 1]
                    pool.wait_ge(sumsq, t + 1)
                    pool.tensor_scalar(col, col, 1.0 / D, EPS, ALU.mult, ALU.add).then_inc(var, 1)
                    pool.wait_ge(var, t + 1)
                    pool.tensor_tensor(col, col, pow_c[:, 0:1], ALU.pow).then_inc(done, 1)

            def exponents(g):
                pool.wait_ge(acs_in, 16 * g + 16)
                heads = bass.ds(HPG * g, HPG)
                for t, c, first in ((0, slice(0, T), 0), (1, slice(T, T + P), P)):
                    pool.tensor_tensor(decay[:, :, c], acs_b[:, heads, first:T],
                                       acs_s[:, t, heads].unsqueeze(2).to_broadcast([P, HPG, T - first]),
                                       ALU.subtract).then_inc(seg_ready, 1)

            def squares(n):
                v = v_ssm[:, bass.ds(GT * n - GT, GT), :]
                pool.wait_ge(v_ready, n)
                pool.tensor_tensor(sq_v[:], v, v, ALU.mult).then_inc(sq_step, 1)
                pool.wait_ge(sq_step, 3 * n - 2)
                pool.tensor_tensor(sq_h[:], sq_v[:, 0:2, :], sq_v[:, 2:4, :], ALU.add).then_inc(sq_step, 1)
                pool.wait_ge(sq_step, 3 * n - 1)
                pool.tensor_tensor(sq_g[:, bass.ds(n - 1, 1), :], sq_h[:, 0:1, :], sq_h[:, 1:2, :],
                                   ALU.add).then_inc(sq_step, 1)

            pool.wait_ge(pow_set, 1)
            rstd(0, x_sumsq, x_var, x_rstd)
            pool.wait_ge(acs_ready, 2)
            exponents(0)
            with pool.Fori(1, GROUPS) as g:
                pool.wait_ge(y_mm, g)
                exponents(g)
                squares(g)
            rstd(2, m_sumsq, m_var, m_rstd)
            squares(GROUPS)
            pool.wait_ge(group_var, 1)
            pool.tensor_tensor(group_rstd[:], group_rstd[:], pow_c[:], ALU.pow).then_inc(group_pow, 1)
            rstd(4, h_sumsq, h_var, h_rstd)
            rstd(6, y_sumsq, y_var, y_rstd)


_INS = ("x", "mem", "rel_bias", "mix_norm_g", "w_in", "b_gate", "ssm_conv_w", "ssm_conv_b", "ssm_dt_bias", "ssm_A_log",
        "ssm_D", "ssm_norm_g", "mem_norm_g", "w_mem_kv", "w_br_attn", "w_br_ssm", "w_br_mem", "w_out", "ffn_norm_g",
        "w_ffn_up", "ffn_conv_w", "ffn_conv_b", "w_ffn_down", "final_norm_g")


def kernel(**inputs):
    import concourse.bacc as bacc
    from concourse.bass_utils import run_bass_kernel_spmd

    nc = bacc.Bacc("TRN2", target_bir_lowering=False, num_devices=1, dynamic_dma_scratch_size=1024)
    arrays = {n: np.ascontiguousarray(inputs[n]) for n in _INS}
    arrays |= dict(zip(("square_table", "bucket_table", "one_row"), constants()))
    aps = [nc.dram_tensor(n, a.shape, mybir.dt.from_np(a.dtype), kind="ExternalInput").ap() for n, a in arrays.items()]
    out = nc.dram_tensor("out", (1, T, D), F32, kind="ExternalOutput").ap()
    build(nc, *aps, out)
    r = run_bass_kernel_spmd(nc, [arrays], core_ids=[0])
    return r.results[0]["out"]
```

```python
import numpy as np

import concourse.bass as bass
from concourse import mybir

F32 = mybir.dt.float32
F32R = mybir.dt.float32r
ALU = mybir.AluOpType
ACT = mybir.ActivationFunctionType
AX = mybir.AxisListType.X

P = 128
KB = 1024
EPS = 1e-6
MASKED = -1e30

D = 1024
T = 256
NT = T // P
KT = D // P
HEADS, DH = 8, 128
BUCKETS, MAX_DIST = 32, 1024
SSM = 2 * D
SHD = 64
SHEADS = SSM // SHD
GROUPS, STATE = 4, 128
HPG = SHEADS // GROUPS
GC = SSM // GROUPS
GT = GC // P
TAPS = 4
CONV_T = (SSM + 2 * GROUPS * STATE) // P
MHEADS, MDH = 4, 256
FFN = 2816
FTAPS = 3
FT = FFN // P
F_STEPS = FFN // 256
QC, KC, VC = 0, D, 2 * D
ZC = 3 * D
XC = ZC + SSM
BC = XC + SSM
CC = BC + GROUPS * STATE
DTC = CC + GROUPS * STATE
QMC = DTC + SHEADS
GATEC = QMC + D

SLOTS = 3
CW = 256
CHUNK = KT * CW
LAG = 2 * P - 1
BIAS_W = 3 * P
RA, RB, RC, RD, RE, RF, RG = 0, 8, 12, 16, 20, 24, 26


def constants():
    p, c = np.arange(P)[:, None], np.arange(P)[None, :]
    upper = (c >= p).astype(np.float32)
    ones = np.ones((P, P), np.float32)
    square = np.concatenate([np.eye(P, dtype=np.float32), upper, ones, upper, ones], axis=1)
    dist = LAG - np.arange(BIAS_W)
    n = np.maximum(dist, 0)
    half = BUCKETS // 2
    far = np.maximum(n, half).astype(np.float32)
    large = half + (np.log(far / np.float32(half)) / np.float32(np.log(MAX_DIST / half))
                    * np.float32(BUCKETS - half)).astype(np.int32)
    bucket = np.where(n < half, n, np.minimum(large, BUCKETS - 1))
    table = np.zeros((BUCKETS + 1, BIAS_W), np.float32)
    table[:BUCKETS] = bucket[None, :] == np.arange(BUCKETS)[:, None]
    table[BUCKETS] = np.where(dist < 0, np.float32(MASKED), np.float32(0))
    return square, table, np.ones((1, HEADS), np.float32)


def build(nc, x, mem, rel_bias, mix_norm_g, w_in, b_gate, ssm_conv_w, ssm_conv_b, ssm_dt_bias, ssm_A_log, ssm_D,
          ssm_norm_g, mem_norm_g, w_mem_kv, w_br_attn, w_br_ssm, w_br_mem, w_out, ffn_norm_g, w_ffn_up, ffn_conv_w,
          ffn_conv_b, w_ffn_down, final_norm_g, square, table, one_row, out):
    base = -(-nc.sbuf_base // 64) * 64

    def place(name, at, shape, dtype=F32):
        return nc.alloc_sbuf_tensor_at(name, [P, *shape], dtype, offset=base + int(at * KB))

    w_raw = place("w_raw", 0, [SLOTS, CHUNK])
    w_hi = place("w_hi", 24, [SLOTS, CHUNK], F32R)
    w_lo = place("w_lo", 48, [SLOTS, CHUNK], F32R)
    tok_hi = place("tok_hi", 72, [KT, T], F32R)
    tok_lo = place("tok_lo", 80, [KT, T], F32R)
    sq = place("square_c", 88, [5 * P])
    ident, tri_wide, ones = sq[:, 0:P], sq[:, P:3 * P], sq[:, 4 * P:5 * P]
    cb_mask = sq[:, P:4 * P]
    table_s = place("table_s", 90.5, [BIAS_W])
    relb = place("relb", 92, [HEADS])
    rows_conv = place("rows_conv", 92.5, [P])
    rows_gate = place("rows_gate", 93, [P])
    rows_skip = place("rows_skip", 93.5, [P])
    rows_up01 = place("rows_up01", 94, [P])
    rows_up2 = place("rows_up2", 94.5, [P])
    n_conv, n_gate, n_skip, n_up01, n_up2 = (TAPS + 1) * CONV_T, 4 * KT + SSM // P, SSM // P, 2 * 2 * FT, 2 * 2 * FT
    cols_conv = place("cols_conv", 95, [TAPS + 1, CONV_T])
    cols_gate = place("cols_gate", 95.5, [n_gate])
    cols_skip = place("cols_skip", 95.75, [n_skip])
    cols_up = place("cols_up", 96, [4, 2 * FT])
    skip2 = place("skip2", 96.75, [2])
    dt_rows = place("dt_rows", 96.875, [2, SHEADS])
    stat = place("stat", 97.25, [NT * 5])
    pow_c = place("pow_c", 97.3125, [NT * GROUPS])
    zero_s = place("zero_s", 99.46875, [P // 2])
    group_rstd = place("group_rstd", 99.71875, [NT * GROUPS])
    soft = place("soft", 97.375, [4, 4])
    msoft = place("msoft", 97.4375, [4, NT])
    R = 100
    a_neg = place("a_neg", 97.5, [SHEADS])
    dt_s = place("dt_s", 97.75, [NT, SHEADS])
    acs_s = place("acs_s", 98, [NT, SHEADS])
    dt_w = [place(f"dt_w{i}", R + 20 + 0.25 * i, [NT, SHEADS]) for i in range(6)]
    da_s = place("da_s", 99.75, [NT, SHEADS])
    g1 = place("g1", R + 0, [KT, T])
    v_ssm = place("v_ssm", R + 8, [GROUPS * GT, T])
    om_hi = place("om_hi", R + 8, [KT, T], F32R)
    om_lo = place("om_lo", R + 108, [KT, T], F32R)
    os_hi = place("os_hi", R + 24, [2 * KT, T], F32R)
    os_lo = place("os_lo", R + 40, [2 * KT, T], F32R)
    mg_hi = place("mg_hi", R + 24, [KT, T], F32R)
    mg_lo = place("mg_lo", R + 32, [KT, T], F32R)
    oa_hi = place("oa_hi", R + 56, [KT, T], F32R)
    oa_lo = place("oa_lo", R + 64, [KT, T], F32R)
    me_hi = place("me_hi", R + 72, [KT, T], F32R)
    me_lo = place("me_lo", R + 80, [KT, T], F32R)
    merged = place("merged", R + 72, [KT, T])
    g0 = place("g0", R + 80, [KT, T])
    x_nat = place("x_nat", R + 24, [NT, D])
    x_sc = place("x_sc", R + 32, [NT, D])
    rows_mix = place("rows_mix", R + 40, [P])
    cols_mix = place("cols_mix", R + 41, [KT])
    wdt_raw = place("wdt_raw", R + 8, [KT, P])
    wdt_hi = place("wdt_hi", R + 12, [KT, P], F32R)
    wdt_lo = place("wdt_lo", R + 16, [KT, P], F32R)
    dt_raw = place("dt_raw", 98.25, [T])
    acs_row = place("acs_row", R + 21.5, [T])
    bias_row = place("bias_row", R + 22.5, [BIAS_W])
    acs_b = place("acs_b", R + 24, [SHEADS, T])
    decay = place("decay", R + 56, [HPG, 3 * P])
    pad_x = place("pad_x", R + 68, [SLOTS, 2, TAPS - 1 + T])
    conv_a = place("conv_a", R + 75, [SLOTS, 2, T])
    tanh_a = place("tanh_a", R + 81, [SLOTS, 2, T])
    conv_o = place("conv_o", R + 87, [6, T])
    x_dt = place("x_dt", R + 93, [NT, GC])
    z_act = place("z_act", R + 97, [GT, T])
    y_sum = place("y_sum", R + 101, [GT, T])
    sq_v = place("sq_v", R + 105, [GT, T])
    sq_h = place("sq_h", R + 109, [2, T])
    sq_g = place("sq_g", R + 111, [GROUPS, T])
    cb = place("cb", R + 115, [3 * P])
    bias_t = place("bias_t", R + 24, [HEADS, 3 * P])
    mem_nat = place("mem_nat", R + 36, [NT, D])
    gain_mem = place("gain_mem", R + 44, [D])
    junk_m = place("junk_m", R + 48, [NT, D])
    prob = place("prob", R + 99, [2, 3 * P])
    prob_t = place("prob_t", R + 48, [2, 3 * P])
    k_t = place("k_t", R + 116.5, [2, T])
    q_t = place("q_t", R + 118.5, [2, T])
    v_t = place("v_t", R + 120.5, [NT, 2 * DH])
    qm_hi = place("qm_hi", R + 88, [2, T], F32R)
    qm_lo = place("qm_lo", R + 102, [2, T], F32R)
    km_hi = place("km_hi", R + 90, [2, T], F32R)
    km_lo = place("km_lo", R + 104, [2, T], F32R)
    vm_hi = place("vm_hi", R + 92, [NT, MDH], F32R)
    vm_lo = place("vm_lo", R + 120.5, [NT, MDH], F32R)
    mprob = place("mprob", R + 94, [NT, T])
    mprob_hi = place("mprob_hi", R + 96, [NT, T], F32R)
    mprob_lo = place("mprob_lo", R + 106, [NT, T], F32R)
    rstd_g = place("rstd_g", R + 98, [GROUPS, T])
    o_tmp = place("o_tmp", R + 116.5, [GT, T])
    tanh_d = place("tanh_d", R + 88, [2, T])
    e_attn = place("e_attn", R + 90, [2, T])
    tanh_e = place("tanh_e", R + 92, [2, T])
    e_gate = place("e_gate", R + 94, [2, T])
    e_mem = place("e_mem", R + 96, [2, T])
    e_sum = place("e_sum", R + 98, [2, T])
    h_nat = place("h_nat", R + 100, [NT, D])
    h_sc = place("h_sc", R + 108, [NT, D])
    gain_fin = place("gain_fin", R + 44, [D])
    last_hi = place("last_hi", R + 20, [2, T], F32R)
    last_lo = place("last_lo", R + 22, [2, T], F32R)
    rstd_b = place("rstd_b", R + 18.5, [T])
    pad_g = place("pad_g", R + 0, [2, FTAPS - 1 + T])
    pad_u = place("pad_u", R + 2.25, [2, FTAPS - 1 + T])
    conv_g = place("conv_g", R + 4.5, [2, T])
    conv_u = place("conv_u", R + 6.5, [2, T])
    tanh_g = place("tanh_g", R + 8.5, [2, T])
    silu_g = place("silu_g", R + 10.5, [2, T])
    hid = place("hid", R + 12.5, [2, T])
    hid_hi = place("hid_hi", R + 14.5, [2, T], F32R)
    hid_lo = place("hid_lo", R + 16.5, [2, T], F32R)

    ps = nc.alloc_psum_tensor("ps", [P, 8, 512], F32)

    acs_d = nc.dram_tensor("acs_d", (SHEADS, T), F32, kind="Internal").ap()
    bias_d = nc.dram_tensor("bias_d", (HEADS, P, BIAS_W), F32, kind="Internal").ap()

    sem = nc.alloc_semaphore
    loaded, hi_ready, lo_ready, gemm_done, bank_free = (
        [sem(f"{n}{s}") for s in range(SLOTS)] for n in ("loaded", "hi_ready", "lo_ready", "gemm_done", "bank_free"))
    x_in = [sem("x_in0"), sem("x_in1")]
    first_in, first_hi, first_lo, mix_turned, mix_ready = map(
        sem, ("first_in", "first_hi", "first_lo", "mix_turned", "mix_ready"))
    gain_in, const_in, rows_in, dtw_in, dtp_in, relb_in, skip_in = map(
        sem, ("gain_in", "const_in", "rows_in", "dtw_in", "dtp_in", "relb_in", "skip_in"))
    zeros_set, pow_set, skip_row = sem("zeros_set"), sem("pow_set"), sem("skip_row")
    rows_turned, params_ready = sem("rows_turned"), sem("params_ready")
    x_sumsq, x_var, x_rstd, x_scaled, x_turned, x_hi, x_lo = map(
        sem, ("x_sumsq", "x_var", "x_rstd", "x_scaled", "x_turned", "x_hi", "x_lo"))
    wdt_hi_s, wdt_lo_s, dt_mm, dt_copied, dt_turned, dt_exp, dt_step, a_exp = map(
        sem, ("wdt_hi_s", "wdt_lo_s", "dt_mm", "dt_copied", "dt_turned", "dt_exp", "dt_step", "a_exp"))
    acs_mm, acs_ready, acs_out, acs_in = map(sem, ("acs_mm", "acs_ready", "acs_out", "acs_in"))
    bias_mm, bias_copied, bias_out, bias_in = map(sem, ("bias_mm", "bias_copied", "bias_out", "bias_in"))
    conv_step, conv_tanh, conv_done, seg_ready, seg_clamped, decay_ready, decay_cb = map(
        sem, ("conv_step", "conv_tanh", "conv_done", "seg_ready", "seg_clamped", "decay_ready", "decay_cb"))
    xg_turned, cb_mm, cb_masked, xdt_ready, y_mm, z_tanh = map(
        sem, ("xg_turned", "cb_mm", "cb_masked", "xdt_ready", "y_mm", "z_tanh"))
    y_step, v_ready, sq_step, g1_ready = map(sem, ("y_step", "v_ready", "sq_step", "g1_ready"))
    group_mm, group_var, group_pow, group_spread, rstd_g_ready = map(
        sem, ("group_mm", "group_var", "group_pow", "group_spread", "rstd_g_ready"))
    s_mm, s_biased, s_max, s_neg, p_exp, p_rec, p_norm, p_turned, pt_ready, o_mm, oa_hi_s, oa_lo_s = map(
        sem, ("s_mm", "s_biased", "s_max", "s_neg", "p_exp", "p_rec", "p_norm", "p_turned", "pt_ready", "o_mm",
              "oa_hi_s", "oa_lo_s"))
    norm_step, os_hi_s, os_lo_s = map(sem, ("norm_step", "os_hi_s", "os_lo_s"))
    m_in, m_gain_in, m_sumsq, m_var, m_rstd, m_step, m_scaled, m_turned, m_hi, m_lo = map(
        sem, ("m_in", "m_gain_in", "m_sumsq", "m_var", "m_rstd", "m_step", "m_scaled", "m_turned", "m_hi", "m_lo"))
    ms_mm, ms_max, ms_neg, mp_exp, mp_rec, mp_norm, mp_turned, mo_mm, om_hi_s, om_lo_s = map(
        sem, ("ms_mm", "ms_max", "ms_neg", "mp_exp", "mp_rec", "mp_norm", "mp_turned", "mo_mm", "om_hi_s", "om_lo_s"))
    qm_hi_s, km_hi_s, vm_hi_s, mpt_hi_s, mpt_ready = map(
        sem, ("qm_hi_s", "km_hi_s", "vm_hi_s", "mpt_hi_s", "mpt_ready"))
    g0_ready, e_step, e_summed, mg_hi_s, mg_lo_s = map(
        sem, ("g0_ready", "e_step", "e_summed", "mg_hi_s", "mg_lo_s"))
    x_again, late_gain, h_sumsq, h_var, h_rstd, h_spread, rstd_b_ready, h_turned, h_hi, h_lo = map(
        sem, ("x_again", "late_gain", "h_sumsq", "h_var", "h_rstd", "h_spread", "rstd_b_ready", "h_turned", "h_hi",
              "h_lo"))
    pads_zero, conv_begun, f_step, g_tanh, g_silu, hid_done, hid_hi_s, hid_lo_s = map(
        sem, ("pads_zero", "conv_begun", "f_step", "g_tanh", "g_silu", "hid_done", "hid_hi_s", "hid_lo_s"))
    down_done, y_added, y_sumsq, y_var, y_rstd, y_scaled, y_out = map(
        sem, ("down_done", "y_added", "y_sumsq", "y_var", "y_rstd", "y_scaled", "y_out"))

    def load(sp, r, s, w, col):
        sp.wait_ge(lo_ready[s], r + 1)
        src = w[:, bass.ds(col, CW)].rearrange("(k p) n -> p k n", p=P)
        dst = w_raw[:, s, :].rearrange("p (k n) -> p k n", k=KT)
        for half in (slice(KT // 2, KT), slice(0, KT // 2)):
            sp.dma_start(dst[:, half, :], src[:, half, :]).then_inc(loaded[s], 16)

    def load_bc(sp, r, g):
        sp.wait_ge(lo_ready[0], r + 1)
        dst = w_raw[:, 0, :].rearrange("p (k n) -> p k n", k=KT)
        for j, col in enumerate((BC, CC)):
            src = w_in[0][:, bass.ds(col + STATE * g, STATE)].rearrange("(k p) n -> p k n", p=P)
            sp.dma_start(dst[:, :, j * P:(j + 1) * P], src).then_inc(loaded[0], 16)

    def load_down(sp, r, s, f):
        sp.wait_ge(lo_ready[s], r + 1)
        src = w_ffn_down[0][bass.ds(2 * P * f, 2 * P), :].rearrange("(k p) n -> p k n", p=P)
        dst = w_raw[:, s, :].rearrange("p (k n) -> p k n", k=2)
        for k in range(2):
            sp.dma_start(dst[:, k, :], src[:, k, :]).then_inc(loaded[s], 16)

    def split_hi(act, r, s, first=False):
        act.wait_ge(loaded[s], 32 * (r + 1))
        if not first:
            act.wait_ge(gemm_done[s], r)
        act.activation(w_hi[:, s, :], w_raw[:, s, :], ACT.Copy).then_inc(hi_ready[s], 1)

    def split_lo(dve, r, s):
        dve.wait_ge(hi_ready[s], r + 1)
        dve.tensor_tensor(w_lo[:, s, :], w_raw[:, s, :], w_hi[:, s, :].bitcast(F32),
                          ALU.subtract).then_inc(lo_ready[s], 1)

    def gemm_cols(pe, r, s, hi, lo, k0=0, banks=None, free=None, start=True, stop=True, tiles=None, between=None):
        pe.wait_ge(lo_ready[s], r + 2)
        for b in [s] if free is None else free:
            pe.wait_ge(bank_free[b], r + 1)
        for j in range(2):
            o = ps[:, s, j * T:(j + 1) * T] if banks is None else ps[:, banks[j], 0:T]
            mm = cols_part(pe, s, j, range(KT), o, hi, lo, k0, start, stop, None if j else tiles)
            if between is not None and j == 0:
                between()
        mm.then_inc(gemm_done[s], 1)

    def cols_part(pe, s, j, ks, o, hi, lo, k0=0, start=True, stop=True, tiles=None):
        for k in ks:
            if tiles is not None:
                pe.wait_ge(tiles[0], k // tiles[1] + 1)
            w = slice(k * CW + j * P, k * CW + (j + 1) * P)
            mm = three(pe, o, (w_hi[:, s, w], w_lo[:, s, w]), (hi[:, k0 + k, :], lo[:, k0 + k, :]),
                       start and k == ks[0], stop and k == ks[-1])
        return mm

    def three(pe, o, a, b, start, stop, **kw):
        pe.matmul(o, a[0], b[0], start=start, stop=False, **kw)
        pe.matmul(o, a[0], b[1], start=False, stop=False, **kw)
        return pe.matmul(o, a[1], b[0], start=False, stop=stop, **kw)

    def rows_part(pe, s, t, ks, hi, lo, start, stop, **kw):
        for k in ks:
            cut, w = slice(t * P, (t + 1) * P), slice(k * CW, (k + 1) * CW)
            mm = three(pe, ps[:, s, t * CW:(t + 1) * CW], (hi[:, k, cut], lo[:, k, cut]),
                       (w_hi[:, s, w], w_lo[:, s, w]), start and k == ks[0], stop and k == ks[-1], **kw)
        return mm

    def gemm_rows(pe, r, s, hi, lo):
        pe.wait_ge(lo_ready[s], r + 2)
        pe.wait_ge(bank_free[s], r + 1)
        for t in range(NT):
            mm = rows_part(pe, s, t, range(KT), hi, lo, True, True)
        mm.then_inc(gemm_done[s], 1)

    def down_part(pe, s, t, hi, lo, done=None):
        for half in range(2):
            for k in range(2):
                cut, w = slice(t * P, (t + 1) * P), slice(k * D + half * 512, k * D + half * 512 + 512)
                mm = three(pe, ps[:, 4 + 2 * t + half, :], (hi[:, k, cut], lo[:, k, cut]),
                           (w_hi[:, s, w], w_lo[:, s, w]), False, False, skip_group_check=True)
            if done is not None:
                mm.then_inc(done, 1)
        return mm

    def open_bank(pe, b):
        z = zero_s[:].bitcast(mybir.dt.bfloat16)
        pe.matmul(ps[:, b, :].rearrange("p (a n) -> p a n", n=P), z, z.unsqueeze(1).to_broadcast([P, 4, P]),
                  start=True, stop=False, skip_group_check=True)

    def turn(pe, src, k, t, bank):
        o = (k % 2) * T + t * P
        return pe.transpose(ps[:, bank, o:o + P], src[:, t, k * P:(k + 1) * P], ident)

    def part_of(w, j):
        return w[:, 0, :].rearrange("p (k n) -> p k n", k=KT)[:, :, j * P:(j + 1) * P]

    def halfcols(n):
        return slice(n % 2 * (D // 2), (n % 2 + 1) * (D // 2))

    def mem_bank(j):
        return (5, 6, 7, 7)[j]

    def halves(b):
        return ps[:, b, :].rearrange("p (a n) -> p a n", a=2)

    def on_all(v, n):
        return v.rearrange("(a d) -> a d", a=1).to_broadcast([P, n])

    def rows(v):
        return v.rearrange("(c p) -> c p", p=P)

    def conv_tile(s, j, g):
        return GROUPS * GT + GROUPS * j + g if s == 0 else GT * g + 2 * (s - 1) + j

    def gate_tanh(act, dst, s, col):
        for j in range(2):
            a = act.activation(dst[:, j, :], ps[:, s, j * T:(j + 1) * T], ACT.Tanh,
                               bias=cols_gate[:, bass.ds(col + j, 1)], scale=0.5)
        a.then_inc(bank_free[s], 1)

    with nc.Block() as block:
        @block.sync
        def _(sp):
            wi = w_in[0]

            def up_rows(v):
                return v.rearrange("j (c p) -> (j c) p", p=P)

            x_tiles = x[0].rearrange("(t p) d -> p t d", p=P)
            sp.dma_start(x_nat[:, 0, :], x_tiles[:, 0, :]).then_inc(x_in[0], 16)
            sp.dma_start(x_nat[:, 1, :], x_tiles[:, 1, :]).then_inc(x_in[1], 16)
            sp.dma_start(rows_mix[0:KT, :], rows(mix_norm_g[0])).then_inc(gain_in, 16)
            sp.dma_start(sq[:], square).then_inc(const_in, 16)
            first_b, first_c = (wi[:, col:col + STATE].rearrange("(k p) n -> p k n", p=P) for col in (BC, CC))
            slot = w_raw[:, 0, :].rearrange("p (k n) -> p k n", k=KT)
            sp.dma_start(slot[:, :, 0:P], first_b).then_inc(first_in, 16)
            for ks in (slice(0, KT // 2), slice(KT // 2, KT)):
                sp.dma_start(slot[:, ks, P:CW], first_c[:, ks, :]).then_inc(loaded[0], 16)
            n = TAPS * CONV_T
            sp.dma_start(rows_conv[0:n, :], up_rows(ssm_conv_w[0])).then_inc(rows_in, 16)
            sp.dma_start(rows_conv[n:n_conv, :], rows(ssm_conv_b[0])).then_inc(rows_in, 16)
            sp.dma_start(rows_gate[0:3 * KT, :], rows(b_gate[0])).then_inc(rows_in, 16)
            sp.dma_start(rows_gate[3 * KT:5 * KT, :], rows(ssm_norm_g[0])).then_inc(rows_in, 16)
            sp.dma_start(rows_gate[5 * KT:n_gate, :], rows(ffn_norm_g[0])).then_inc(rows_in, 16)
            sp.dma_start(rows_up01[0:n_up01, :], up_rows(ffn_conv_w[0, 0:2])).then_inc(rows_in, 16)
            sp.dma_start(rows_up2[0:2 * FT, :], up_rows(ffn_conv_w[0, 2:3])).then_inc(rows_in, 16)
            sp.dma_start(rows_up2[2 * FT:n_up2, :], rows(ffn_conv_b[0])).then_inc(rows_in, 16)
            sp.dma_start(skip2[0:n_skip, :], ssm_D[0].rearrange("(c j) -> c j", j=2)).then_inc(skip_in, 16)
            sp.dma_start(wdt_raw[:], wi[:, DTC:DTC + P].rearrange("(k p) n -> p k n", p=P)).then_inc(dtw_in, 16)
            load(sp, 0, 1, wi, XC)
            load(sp, 0, 2, wi, XC + CW)
            sp.dma_start(dt_rows[:, 0, :], on_all(ssm_dt_bias[0], SHEADS)).then_inc(dtp_in, 16)
            sp.dma_start(dt_rows[:, 1, :], on_all(ssm_A_log[0], SHEADS)).then_inc(dtp_in, 16)
            sp.dma_start(table_s[0:BUCKETS + 1, :], table).then_inc(relb_in, 16)
            sp.dma_start(relb[0:BUCKETS, :], rel_bias).then_inc(relb_in, 16)
            sp.dma_start(relb[BUCKETS:BUCKETS + 1, :], one_row).then_inc(relb_in, 16)

            def load_acs(g):
                sp.dma_start(acs_b[:, bass.ds(HPG * g, HPG), :], acs_d[bass.ds(HPG * g, HPG), :].rearrange(
                    "(a h) t -> a h t", a=1).to_broadcast([P, HPG, T])).then_inc(acs_in, 16)

            load(sp, 1, 0, wi, ZC)
            load(sp, 1, 1, wi, ZC + CW)
            load(sp, 1, 2, wi, GATEC + D)
            sp.wait_ge(acs_ready, 2)
            sp.dma_start(acs_d, acs_row[0:SHEADS, :]).then_inc(acs_out, 16)
            load_bc(sp, 2, 1)
            sp.wait_ge(acs_out, 16)
            load_acs(0)
            load(sp, 2, 1, wi, XC + GC)
            load(sp, 2, 2, wi, XC + CW + GC)
            sp.wait_ge(acs_in, 16)
            load_acs(1)
            load(sp, 3, 0, wi, ZC + GC)
            load(sp, 3, 1, wi, ZC + CW + GC)
            load(sp, 3, 2, wi, GATEC + D + CW)
            sp.wait_ge(bias_copied, 1)
            sp.dma_start(bias_d, bias_row[0:HEADS, :].unsqueeze(1).to_broadcast([HEADS, P, BIAS_W])
                         ).then_inc(bias_out, 16)
            with sp.Fori(2, GROUPS) as g:
                r = 2 * g
                load_bc(sp, r, g)
                load(sp, r, 1, wi, XC + GC * g)
                load(sp, r, 2, wi, XC + CW + GC * g)
                sp.wait_ge(acs_in, 16 * g)
                load_acs(g)
                load(sp, r + 1, 0, wi, ZC + GC * g)
                load(sp, r + 1, 1, wi, ZC + CW + GC * g)
                load(sp, r + 1, 2, wi, GATEC + D + CW * g)
            load(sp, RB, 0, wi, KC)
            load(sp, RB, 1, wi, QC)
            sp.wait_ge(seg_ready, 6)
            sp.wait_ge(bias_out, 16)
            for c0, at, n in ((0, LAG, P), (P, LAG - P, T)):
                src = bass.AP(tensor=bias_d.tensor, offset=at, ap=[[BIAS_W - 1, P], [P * BIAS_W, HEADS], [1, n]])
                sp.dma_start(bias_t[:, :, c0:c0 + n], src).then_inc(bias_in, 16)
            sp.dma_start(mem_nat[:], mem[0].rearrange("(t p) d -> p t d", p=P)).then_inc(m_in, 16)
            sp.dma_start(gain_mem[:], on_all(mem_norm_g[0], D)).then_inc(m_gain_in, 16)
            load(sp, RB, 2, wi, VC)
            with sp.Fori(1, 4) as i:
                load(sp, RB + i, 0, wi, KC + CW * i)
                load(sp, RB + i, 1, wi, QC + CW * i)
                load(sp, RB + i, 2, wi, VC + CW * i)
            with sp.Fori(0, 4) as i:
                load(sp, RC + i, 0, wi, QMC + CW * i)
                load(sp, RC + i, 1, w_mem_kv[0], CW * i)
                load(sp, RC + i, 2, w_mem_kv[0], D + CW * i)
            with sp.Fori(0, 4) as i:
                load(sp, RD + i, 0, w_br_ssm[0, 0:D], CW * i)
                load(sp, RD + i, 1, w_br_ssm[0, D:2 * D], CW * i)
                load(sp, RD + i, 2, wi, GATEC + CW * i)
            sp.wait_ge(os_lo_s, GROUPS)
            sp.wait_ge(om_lo_s, 4)
            sp.dma_start(h_nat[:], x_tiles).then_inc(x_again, 16)
            with sp.Fori(0, 4) as i:
                load(sp, RE + i, 0, w_br_attn[0], CW * i)
                load(sp, RE + i, 1, wi, GATEC + 2 * D + CW * i)
                load(sp, RE + i, 2, w_br_mem[0], CW * i)
            for c in range(3):
                load(sp, RF, c, w_out[0], CW * c)
            sp.wait_ge(gemm_done[1], RE)
            sp.dma_start(gain_fin[:], on_all(final_norm_g, D)).then_inc(late_gain, 16)
            load(sp, RF + 1, 0, w_out[0], CW * 3)
            load(sp, RF + 1, 1, w_ffn_up[0], 0)
            load(sp, RF + 1, 2, w_ffn_up[0], FFN)
            with sp.Fori(1, F_STEPS) as f:
                r = f + (RG - 1)
                load(sp, r, 0, w_ffn_up[0], CW * f)
                load(sp, r, 1, w_ffn_up[0], FFN + CW * f)
                load_down(sp, r, 2, f - 1)
            load_down(sp, RG + F_STEPS - 1, 0, F_STEPS - 1)
            for n in range(2 * NT):
                t = n // 2
                sp.wait_ge(y_scaled, n + 1)
                sp.dma_start(out[0, t * P:(t + 1) * P, halfcols(n)], h_sc[:, t, halfcols(n)]).then_inc(y_out, 16)
            sp.wait_ge(y_out, 16 * 2 * NT)

        @block.tensor
        def _(pe):
            pe.wait_ge(const_in, 16)
            pe.wait_ge(gain_in, 16)
            pe.transpose(ps[:, 2, 0:KT], rows_mix[0:KT, :], ident[0:KT, 0:KT]).then_inc(mix_turned, 1)
            for t in range(NT):
                pe.wait_ge(x_scaled, t + 1)
                for k in range(KT):
                    mm = turn(pe, x_sc, k, t, 4 + k // 2)
                    if t and k % 2:
                        mm.then_inc(x_turned, 1)
            pe.wait_ge(first_lo, 1)
            cols_part(pe, 0, 0, range(KT), ps[:, 0, 0:T], tok_hi, tok_lo, tiles=(x_lo, 1))
            pe.wait_ge(lo_ready[0], 2)
            cols_part(pe, 0, 1, range(KT), ps[:, 0, T:2 * T], tok_hi, tok_lo).then_inc(gemm_done[0], 1)
            pe.wait_ge(rows_in, 16 * 8)
            pe.wait_ge(skip_row, 1)
            at = 0
            for src, n in ((rows_conv, n_conv), (rows_gate, n_gate), (rows_skip, n_skip), (rows_up01, n_up01),
                           (rows_up2, n_up2)):
                mm = pe.transpose(ps[:, 3, at:at + n], src[0:n, :], ident[0:n, 0:n])
                at += n
            mm.then_inc(rows_turned, 1)
            pe.wait_ge(wdt_lo_s, 1)
            for k in range(KT):
                mm = three(pe, ps[:, 4, 0:T], (wdt_hi[:, k, :], wdt_lo[:, k, :]), (tok_hi[:, k, :], tok_lo[:, k, :]),
                           k == 0, k == KT - 1)
            mm.then_inc(dt_mm, 1)
            pe.wait_ge(relb_in, 48)
            pe.matmul(ps[0:HEADS, 5, 0:BIAS_W], relb[0:BUCKETS + 1, :], table_s[0:BUCKETS + 1, :],
                      start=True, stop=True).then_inc(bias_mm, 1)
            gemm_cols(pe, 0, 1, tok_hi, tok_lo)
            pe.wait_ge(dt_copied, 1)
            for t in range(NT):
                mm = pe.transpose(ps[:, 6, t * SHEADS:(t + 1) * SHEADS], dt_raw[0:SHEADS, t * P:(t + 1) * P],
                                  ident[0:SHEADS, 0:SHEADS])
            mm.then_inc(dt_turned, 1)
            gemm_cols(pe, 0, 2, tok_hi, tok_lo)
            def decay_sums():
                pe.wait_ge(dt_step, 19)
                pe.matmul(ps[:, 7, 0:SHEADS], tri_wide[:, 0:P], da_s[:, 0, :], start=True, stop=True)
                pe.matmul(ps[:, 7, SHEADS:2 * SHEADS], tri_wide[:, P:2 * P], da_s[:, 0, :], start=True, stop=False)
                pe.matmul(ps[:, 7, SHEADS:2 * SHEADS], tri_wide[:, 0:P], da_s[:, 1, :], start=False, stop=True)
                pe.matmul(ps[0:SHEADS, 7, T:2 * T], da_s[:, 0, :], tri_wide[:, 0:T], start=True, stop=False)
                pe.matmul(ps[0:SHEADS, 7, T + P:2 * T], da_s[:, 1, :], tri_wide[:, 0:P], start=False,
                          stop=True).then_inc(acs_mm, 1)

            def rest_of_group(g, between=None):
                r = 2 * g + 1
                gemm_cols(pe, r, 0, tok_hi, tok_lo, between=between)
                gemm_cols(pe, r, 1, tok_hi, tok_lo)
                pe.wait_ge(conv_done, 3 * g + 3)
                for t in range(NT):
                    for c in range(GT):
                        mm = pe.transpose(ps[:, 3 + t, c * P:(c + 1) * P], conv_o[:, 2 + c, t * P:(t + 1) * P], ident)
                mm.then_inc(xg_turned, 1)
                pe.matmul(ps[:, 5, 0:T], conv_o[:, 0, 0:P], conv_o[:, 1, :], start=True, stop=True)
                pe.matmul(ps[:, 5, T:T + P], conv_o[:, 0, P:T], conv_o[:, 1, P:T], start=True,
                          stop=True).then_inc(cb_mm, 1)
                gemm_cols(pe, r, 2, tok_hi, tok_lo)

            def scan(n):
                pe.wait_ge(xdt_ready, 2 * n)
                pe.wait_ge(decay_cb, n)
                for h in range(HPG):
                    half, c = SHD * (h % 2), h // 2
                    o = ps[half:half + SHD, 6 + c // 2, (c % 2) * T:(c % 2 + 1) * T]
                    pe.matmul(o, x_dt[:, 0, h * SHD:(h + 1) * SHD], decay[:, h, 0:T], start=True, stop=False)
                    mm = pe.matmul(o[:, P:T], x_dt[:, 1, h * SHD:(h + 1) * SHD], decay[:, h, T:T + P], start=False,
                                   stop=True)
                mm.then_inc(y_mm, 1)

            rest_of_group(0, decay_sums)
            with pe.Fori(1, GROUPS) as g:
                gemm_cols(pe, 2 * g, 0, tok_hi, tok_lo)
                gemm_cols(pe, 2 * g, 1, tok_hi, tok_lo)
                scan(g)
                gemm_cols(pe, 2 * g, 2, tok_hi, tok_lo)
                rest_of_group(g)

            def scores(i):
                pe.wait_ge(bank_free[0], RB + 2 + i)
                pe.wait_ge(bank_free[1], RB + 2 + i)
                for a in range(2):
                    pe.matmul(ps[:, 3 + a, 0:P], q_t[:, a, 0:P], k_t[:, a, 0:P], start=True, stop=True)
                    mm = pe.matmul(ps[:, 3 + a, P:3 * P], q_t[:, a, P:T], k_t[:, a, :], start=True, stop=True)
                mm.then_inc(s_mm, 1)

            def turn_probs(n):
                pe.wait_ge(m_lo, 2)
                for a in range(2):
                    pe.wait_ge(p_norm, 4 * n - 2 + 2 * a)
                    for b in range(3):
                        mm = pe.transpose(ps[:, 5 + a, b * P:(b + 1) * P], prob[:, a, b * P:(b + 1) * P], ident)
                    mm.then_inc(p_turned, 1)

            def attend(n):
                pe.wait_ge(bank_free[2], RB + 1 + n)
                pe.wait_ge(pt_ready, 2 * n)
                for a in range(2):
                    pe.matmul(ps[:, 7, a * T:(a + 1) * T], v_t[:, 0, a * DH:(a + 1) * DH], prob_t[:, a, 0:T],
                              start=True, stop=False)
                    mm = pe.matmul(ps[:, 7, a * T + P:(a + 1) * T], v_t[:, 1, a * DH:(a + 1) * DH],
                                   prob_t[:, a, T:T + P], start=False, stop=True)
                mm.then_inc(o_mm, 1)

            gemm_cols(pe, RB, 0, tok_hi, tok_lo)
            gemm_cols(pe, RB, 1, tok_hi, tok_lo)
            scan(GROUPS)
            gemm_rows(pe, RB, 2, tok_hi, tok_lo)
            scores(0)

            def turn_mem(j):
                for k in (2 * j, 2 * j + 1):
                    for t in range(NT):
                        mm = turn(pe, mem_nat, k, t, mem_bank(j))
                mm.then_inc(m_turned, 1)

            pe.wait_ge(v_ready, GROUPS)
            pe.wait_ge(m_scaled, NT)
            turn_mem(0)
            turn_mem(1)
            turn_mem(2)
            with pe.Fori(1, 4) as i:
                gemm_cols(pe, RB + i, 0, tok_hi, tok_lo)
                turn_probs(i)
                gemm_cols(pe, RB + i, 1, tok_hi, tok_lo)
                pe.wait_ge(m_lo, 3)
                attend(i)
                gemm_rows(pe, RB + i, 2, tok_hi, tok_lo)
                scores(i)

            def mem_scores(i):
                pe.wait_ge(bank_free[0], RC + 2 + i)
                pe.wait_ge(bank_free[1], RC + 2 + i)
                for t in range(NT):
                    for d in range(2):
                        cut = slice(t * P, (t + 1) * P)
                        mm = three(pe, ps[:, 3, t * T:(t + 1) * T], (qm_hi[:, d, cut], qm_lo[:, d, cut]),
                                   (km_hi[:, d, :], km_lo[:, d, :]), d == 0, d == 1)
                mm.then_inc(ms_mm, 1)

            def turn_mem_probs(n):
                pe.wait_ge(mp_norm, 2 * n)
                for m in range(2):
                    for t in range(NT):
                        mm = pe.transpose(ps[:, 4, m * T + t * P:m * T + (t + 1) * P], mprob[:, t, m * P:(m + 1) * P],
                                          ident)
                mm.then_inc(mp_turned, 1)

            def mem_attend(n):
                pe.wait_ge(bank_free[2], RC + 1 + n)
                pe.wait_ge(mpt_ready, n)
                for d in range(2):
                    for m in range(2):
                        cut = slice(d * P, (d + 1) * P)
                        mm = three(pe, ps[:, 5, d * T:(d + 1) * T], (vm_hi[:, m, cut], vm_lo[:, m, cut]),
                                   (mprob_hi[:, m, :], mprob_lo[:, m, :]), m == 0, m == 1)
                mm.then_inc(mo_mm, 1)

            pe.wait_ge(oa_lo_s, 3)
            turn_mem(3)
            gemm_cols(pe, RC, 0, tok_hi, tok_lo)
            turn_probs(4)
            pe.wait_ge(sq_step, 3 * GROUPS)
            for t in range(NT):
                for g in range(GROUPS):
                    n = t * GROUPS + g
                    mm = pe.matmul(ps[:, 3, n:n + 1], sq_g[:, g, t * P:(t + 1) * P], ones[:, 0:1], start=True,
                                   stop=True)
            mm.then_inc(group_mm, 1)
            gemm_cols(pe, RC, 1, me_hi, me_lo, tiles=(m_lo, 2))
            attend(4)
            pe.wait_ge(group_pow, 1)
            for g in range(GROUPS):
                for t in range(NT):
                    n = t * GROUPS + g
                    o = (g % 2) * T + t * P
                    mm = pe.matmul(ps[:, 3 + g // 2, o:o + P], group_rstd[:, n:n + 1].to_broadcast([P, P]), ident,
                                   start=True, stop=True)
            mm.then_inc(group_spread, 1)
            gemm_rows(pe, RC, 2, me_hi, me_lo)
            pe.wait_ge(rstd_g_ready, 1)
            mem_scores(0)
            with pe.Fori(1, 4) as i:
                gemm_cols(pe, RC + i, 0, tok_hi, tok_lo)
                turn_mem_probs(i)
                gemm_cols(pe, RC + i, 1, me_hi, me_lo)
                mem_attend(i)
                gemm_rows(pe, RC + i, 2, me_hi, me_lo)
                mem_scores(i)

            pe.wait_ge(os_lo_s, 2)
            gemm_cols(pe, RD, 0, os_hi, os_lo, 0, (0, 1), (0, 1), stop=False)
            turn_mem_probs(4)
            pe.wait_ge(os_lo_s, GROUPS)
            gemm_cols(pe, RD, 1, os_hi, os_lo, KT, (0, 1), (), start=False)
            mem_attend(4)
            gemm_cols(pe, RD, 2, tok_hi, tok_lo)
            with pe.Fori(1, 4) as i:
                r = RD + i
                gemm_cols(pe, r, 0, os_hi, os_lo, 0, (0, 1), (0, 1), stop=False)
                gemm_cols(pe, r, 1, os_hi, os_lo, KT, (0, 1), (), start=False)
                gemm_cols(pe, r, 2, tok_hi, tok_lo)

            pe.wait_ge(oa_lo_s, 4)
            pe.wait_ge(om_lo_s, 4)
            with pe.Fori(0, 4) as i:
                r = RE + i
                gemm_cols(pe, r, 0, oa_hi, oa_lo)
                gemm_cols(pe, r, 1, tok_hi, tok_lo)
                gemm_cols(pe, r, 2, om_hi, om_lo)

            pe.wait_ge(zeros_set, 1)
            pe.wait_ge(mg_lo_s, 3)
            for c in range(2):
                pe.wait_ge(lo_ready[c], RF + 2)
                pe.wait_ge(bank_free[c], RF + 1)
                open_bank(pe, c)
                for t in range(NT):
                    rows_part(pe, c, t, range(0, 6), mg_hi, mg_lo, False, False, skip_group_check=True)
            pe.wait_ge(mg_lo_s, 4)
            for c in range(2):
                for t in range(NT):
                    mm = rows_part(pe, c, t, range(6, KT), mg_hi, mg_lo, False, False, skip_group_check=True)
                mm.then_inc(gemm_done[c], 1)
            gemm_rows(pe, RF, 2, mg_hi, mg_lo)

            def turn_h(c):
                for k in (2 * c, 2 * c + 1):
                    for t in range(NT):
                        mm = turn(pe, h_nat, k, t, 4 + c)
                mm.then_inc(h_turned, 1)

            pe.wait_ge(bank_free[0], RF + 2)
            turn_h(0)
            pe.wait_ge(bank_free[1], RF + 2)
            turn_h(1)
            pe.wait_ge(lo_ready[0], RF + 3)
            rows_part(pe, 0, 0, range(KT), mg_hi, mg_lo, True, True)
            pe.wait_ge(bank_free[2], RF + 2)
            turn_h(2)
            rows_part(pe, 0, 1, range(KT), mg_hi, mg_lo, True, True).then_inc(gemm_done[0], 1)

            pe.wait_ge(h_lo, 6)
            for s in (1, 2):
                pe.wait_ge(lo_ready[s], RF + 3)
                cols_part(pe, s, 0, range(0, 6), ps[:, s, 0:T], tok_hi, tok_lo, stop=False)
                if s == 1:
                    pe.wait_ge(bank_free[0], RF + 3)
                    turn_h(3)
            pe.wait_ge(h_lo, KT)
            for s in (1, 2):
                cols_part(pe, s, 0, range(6, KT), ps[:, s, 0:T], tok_hi, tok_lo, start=False)
                cols_part(pe, s, 1, range(KT), ps[:, s, T:2 * T], tok_hi, tok_lo).then_inc(gemm_done[s], 1)
                if s == 1:
                    pe.wait_ge(h_rstd, NT)
                    for t in range(NT):
                        mm = pe.matmul(ps[:, 3, t * P:(t + 1) * P], stat[:, 4 + t:5 + t].to_broadcast([P, P]), ident,
                                       start=True, stop=True)
                    mm.then_inc(h_spread, 1)
                    for b in range(4, 8):
                        open_bank(pe, b)
            with pe.Fori(1, F_STEPS) as f:
                r = f + (RG - 1)
                gemm_cols(pe, r, 0, tok_hi, tok_lo)
                gemm_cols(pe, r, 1, tok_hi, tok_lo)
                pe.wait_ge(hid_lo_s, f)
                pe.wait_ge(lo_ready[2], r + 2)
                down_part(pe, 2, 0, hid_hi, hid_lo)
                down_part(pe, 2, 1, hid_hi, hid_lo).then_inc(gemm_done[2], 1)
            pe.wait_ge(hid_lo_s, F_STEPS)
            pe.wait_ge(lo_ready[0], RG + F_STEPS + 1)
            for t in range(NT):
                down_part(pe, 0, t, last_hi, last_lo, down_done)

        @block.scalar
        def _(act):
            for t in range(NT):
                act.wait_ge(x_in[t], 16)
                act.activation(x_sc[:, t, :], x_nat[:, t, :], ACT.Square,
                               accum_out=stat[:, t:t + 1]).then_inc(x_sumsq, 1)
            act.wait_ge(first_in, 16)
            act.activation(part_of(w_hi, 0), part_of(w_raw, 0), ACT.Copy).then_inc(first_hi, 1)
            act.wait_ge(mix_ready, 1)
            for j in range(KT // 2):
                act.wait_ge(x_turned, j + 1)
                for k in (2 * j, 2 * j + 1):
                    act.activation(tok_hi[:, k, :], ps[:, 4 + j, (k % 2) * T:(k % 2 + 1) * T], ACT.Copy,
                                   scale=cols_mix[:, k:k + 1]).then_inc(x_hi, 1)
            act.wait_ge(loaded[0], 32)
            act.activation(part_of(w_hi, 1), part_of(w_raw, 1), ACT.Copy).then_inc(hi_ready[0], 1)
            act.wait_ge(dtw_in, 16)
            act.activation(wdt_hi[:], wdt_raw[:], ACT.Copy).then_inc(wdt_hi_s, 1)
            split_hi(act, 0, 1, first=True)
            split_hi(act, 0, 2, first=True)
            act.wait_ge(dtp_in, 32)
            act.activation(a_neg[:], dt_rows[:, 1, :], ACT.Exp).then_inc(a_exp, 1)

            def group(g, first=False):
                r = 2 * g
                for s in range(SLOTS):
                    act.wait_ge(gemm_done[s], r + 1)
                    if first and s == 0:
                        act.wait_ge(params_ready, 12)
                    for j in range(2):
                        c = conv_tile(s, j, g)
                        act.activation(conv_a[:, s, j, :], ps[:, s, j * T:(j + 1) * T], ACT.Identity,
                                       bias=cols_conv[:, TAPS, bass.ds(c, 1)],
                                       scale=cols_conv[:, TAPS - 1, bass.ds(c, 1)])
                    act.activation(pad_x[:, s, :, TAPS - 1:], halves(s), ACT.Copy).then_inc(bank_free[s], 1)
                    if first and s == 1:
                        act.wait_ge(dt_step, 2)
                        act.activation(dt_w[2][:], dt_w[1][:], ACT.Exp).then_inc(dt_exp, 1)
                    split_hi(act, r + 1, s)
                    act.wait_ge(conv_step, 18 * g + 6 * s + 6)
                    act.activation(tanh_a[:, s], conv_a[:, s], ACT.Tanh).then_inc(conv_tanh, 1)
                for s in range(2):
                    act.wait_ge(gemm_done[s], r + 2)
                    act.wait_ge(conv_done, 3 * g + s + 1)
                    act.activation(tanh_a[:, s], halves(s), ACT.Tanh, scale=0.5).then_inc(z_tanh, 1)
                    split_hi(act, r + 2, s)
                act.wait_ge(gemm_done[2], r + 2)
                act.wait_ge(conv_done, 3 * g + 3)
                gate_tanh(act, tanh_a[:, 2], 2, KT + 2 * g)
                split_hi(act, r + 2, 2)
                act.wait_ge(seg_clamped, 2 * g + 2)
                act.activation(decay[:], decay[:], ACT.Exp).then_inc(decay_ready, 1)

            group(0, first=True)
            with act.Fori(1, GROUPS) as g:
                group(g)

            act.wait_ge(m_in, 16)
            act.wait_ge(seg_ready, 2 * GROUPS)
            for t in range(NT):
                act.activation(junk_m[:, t, :], mem_nat[:, t, :], ACT.Square,
                               accum_out=stat[:, 2 + t:3 + t]).then_inc(m_sumsq, 1)

            def heads(i, first=False):
                r = RB + i
                split_hi(act, r + 1, 0)
                if not first:
                    act.wait_ge(p_turned, 2 * i - 1)
                    act.activation(prob_t[:, 0, :], ps[:, 5, 0:3 * P], ACT.Copy).then_inc(pt_ready, 1)
                act.wait_ge(gemm_done[1], r + 1)
                act.activation(q_t[:], halves(1), ACT.Copy, scale=DH ** -0.5).then_inc(bank_free[1], 1)
                split_hi(act, r + 1, 1)
                if not first:
                    act.wait_ge(o_mm, i)
                    act.activation(oa_hi[:, bass.ds(2 * (i - 1), 2), :], halves(7), ACT.Copy).then_inc(oa_hi_s, 1)
                act.wait_ge(gemm_done[2], r + 1)
                act.activation(v_t[:], halves(2), ACT.Copy).then_inc(bank_free[2], 1)
                split_hi(act, r + 1, 2)
                act.wait_ge(s_neg, i + 1)
                for a in range(2):
                    for t in range(NT):
                        part = prob[:, a, 0:P] if t == 0 else prob[:, a, P:3 * P]
                        n = 2 * t + a
                        act.activation(part, part, ACT.Exp, bias=soft[:, 1, n:n + 1],
                                       accum_out=soft[:, 2, n:n + 1]).then_inc(p_exp, 1)

            heads(0, first=True)

            def mem_high(j):
                act.wait_ge(m_turned, j + 1)
                act.activation(me_hi[:, 2 * j:2 * j + 2, :], halves(mem_bank(j)), ACT.Copy).then_inc(m_hi, 1)

            mem_high(0)
            mem_high(1)
            mem_high(2)
            with act.Fori(1, 4) as i:
                heads(i)
            mem_high(3)

            def mem_head(i, first=False):
                r = RC + i
                act.wait_ge(gemm_done[0], r + 1)
                act.activation(qm_hi[:], halves(0), ACT.Copy).then_inc(qm_hi_s, 1)
                if first:
                    act.wait_ge(p_turned, 7)
                    act.activation(prob_t[:, 0, :], ps[:, 5, 0:3 * P], ACT.Copy).then_inc(pt_ready, 1)
                else:
                    act.wait_ge(mp_turned, i)
                    act.activation(mprob_hi[:], halves(4), ACT.Copy).then_inc(mpt_hi_s, 1)
                split_hi(act, r + 1, 0)
                act.wait_ge(gemm_done[1], r + 1)
                act.activation(km_hi[:], halves(1), ACT.Copy).then_inc(km_hi_s, 1)
                split_hi(act, r + 1, 1)
                if first:
                    act.wait_ge(o_mm, 4)
                    act.activation(oa_hi[:, KT - 2:KT, :], halves(7), ACT.Copy).then_inc(oa_hi_s, 1)
                    act.wait_ge(group_spread, 1)
                    act.activation(rstd_g[:].rearrange("p a n -> p (a n)"), ps[:, 3:5, :].rearrange("p a n -> p (a n)"),
                                   ACT.Copy).then_inc(rstd_g_ready, 1)
                else:
                    act.wait_ge(mo_mm, i)
                    act.activation(om_hi[:, bass.ds(2 * (i - 1), 2), :], halves(5), ACT.Copy).then_inc(om_hi_s, 1)
                act.wait_ge(norm_step, GT * i + GT)
                act.activation(os_hi[:, bass.ds(GT * i, GT), :], o_tmp[:], ACT.Copy).then_inc(os_hi_s, 1)
                act.wait_ge(gemm_done[2], r + 1)
                act.activation(vm_hi[:], halves(2), ACT.Copy).then_inc(vm_hi_s, 1)
                act.wait_ge(ms_neg, i + 1)
                for t in range(NT):
                    act.activation(mprob[:, t, :], ps[:, 3, t * T:(t + 1) * T], ACT.Exp, bias=msoft[:, 1, t:t + 1],
                                   scale=MDH ** -0.5, accum_out=msoft[:, 2, t:t + 1]).then_inc(mp_exp, 1)
                split_hi(act, r + 1, 2)

            mem_head(0, first=True)
            with act.Fori(1, 4) as i:
                mem_head(i)

            def ssm_columns(i, first=False):
                r = RD + i
                split_hi(act, r + 1, 0)
                if first:
                    act.wait_ge(mp_turned, 4)
                    act.activation(mprob_hi[:], halves(4), ACT.Copy).then_inc(mpt_hi_s, 1)
                split_hi(act, r + 1, 1)
                if first:
                    act.wait_ge(mo_mm, 4)
                    act.activation(om_hi[:, KT - 2:KT, :], halves(5), ACT.Copy).then_inc(om_hi_s, 1)
                act.wait_ge(gemm_done[2], r + 1)
                gate_tanh(act, tanh_d, 2, 2 * i)
                split_hi(act, r + 1, 2)

            ssm_columns(0, first=True)
            with act.Fori(1, 4) as i:
                ssm_columns(i)

            with act.Fori(0, 4) as i:
                r = RE + i
                split_hi(act, r + 1, 0)
                act.wait_ge(gemm_done[1], r + 1)
                gate_tanh(act, tanh_e, 1, 2 * KT + 2 * i)
                split_hi(act, r + 1, 1)
                act.wait_ge(e_summed, i + 1)
                act.activation(mg_hi[:, bass.ds(2 * i, 2), :], e_sum[:], ACT.Copy).then_inc(mg_hi_s, 1)
                split_hi(act, r + 1, 2)

            def h_high(c):
                act.wait_ge(h_turned, c + 1)
                for j in range(2):
                    k = 2 * c + j
                    act.activation(tok_hi[:, k, :], ps[:, 4 + c, j * T:(j + 1) * T], ACT.Copy,
                                   scale=cols_gate[:, 5 * KT + k:5 * KT + k + 1]).then_inc(h_hi, 1)

            split_hi(act, RF + 1, 0)
            split_hi(act, RF + 1, 1)
            h_high(0)
            h_high(1)
            split_hi(act, RF + 1, 2)
            h_high(2)
            h_high(3)
            for t in range(NT):
                act.activation(h_sc[:, t, :], h_nat[:, t, :], ACT.Square,
                               accum_out=stat[:, 4 + t:5 + t]).then_inc(h_sumsq, 1)
            split_hi(act, RG, 0)

            def ffn(f, sa, ra, sb, rb, after_gate, after_up, last, first=False, final=False):
                for n, (s, r, pad, conv, tile) in enumerate(((sa, ra, pad_g, conv_g, 0), (sb, rb, pad_u, conv_u, FT))):
                    act.wait_ge(bank_free[s], r + 2)
                    if not first:
                        act.wait_ge((g_silu, hid_done)[n], f)
                    for j in range(2):
                        c = tile + 2 * f + j
                        act.activation(conv[:, j, :], pad[:, j, FTAPS - 1:], ACT.Identity,
                                       bias=cols_up[:, FTAPS, bass.ds(c, 1)],
                                       scale=cols_up[:, FTAPS - 1, bass.ds(c, 1)]).then_inc(conv_begun, 1)
                    for rr, ss in (after_gate, after_up)[n]:
                        split_hi(act, rr, ss)
                    if n == 0:
                        act.wait_ge(f_step, 8 * f + 4)
                        act.activation(tanh_g[:], conv_g[:], ACT.Tanh).then_inc(g_tanh, 1)
                act.wait_ge(hid_done, f + 1)
                if not first and not final:
                    act.wait_ge(gemm_done[2], f + RG)
                act.activation((last_hi if final else hid_hi)[:], hid[:], ACT.Copy).then_inc(hid_hi_s, 1)
                for rr, ss in last:
                    split_hi(act, rr, ss)

            ffn(0, 1, RF + 1, 2, RF + 1, [(RG, 1)], [(RG, 2)], [], first=True)
            with act.Fori(1, F_STEPS - 1) as f:
                r = f + (RG - 1)
                ffn(f, 0, r, 1, r, [(r + 1, 0)], [(r + 1, 1)], [(r + 1, 2)])
            r = RG + F_STEPS - 2
            ffn(F_STEPS - 1, 0, r, 1, r, [(r + 1, 0)], [], [], final=True)
            for n in range(2 * NT):
                act.wait_ge(y_added, n + 1)
                act.activation(h_sc[:, n // 2, halfcols(n)], h_nat[:, n // 2, halfcols(n)], ACT.Square,
                               accum_out=stat[:, 6 + n:7 + n]).then_inc(y_sumsq, 1)

        @block.vector
        def _(dve):
            def gate(dst, src, done):
                dve.tensor_scalar(dst, src, 0.5, 0.5, ALU.mult, ALU.add).then_inc(done, 1)

            for s in range(SLOTS):
                dve.memset(pad_x[:, s, 0, 0:TAPS - 1], 0.0).then_inc(lo_ready[s], 1)
                dve.memset(pad_x[:, s, 1, 0:TAPS - 1], 0.0).then_inc(bank_free[s], 1)
            dve.memset(pow_c[:], -0.5).then_inc(pow_set, 1)
            dve.memset(zero_s[:], 0.0).then_inc(zeros_set, 1)
            for t in range(NT):
                dve.wait_ge(x_rstd, t + 1)
                dve.tensor_scalar(x_sc[:, t, :], x_nat[:, t, :], stat[:, t:t + 1], None, ALU.mult).then_inc(x_scaled, 1)
            dve.wait_ge(mix_turned, 1)
            dve.tensor_copy(cols_mix[:], ps[:, 2, 0:KT]).then_inc(mix_ready, 1)
            dve.wait_ge(first_hi, 1)
            dve.tensor_tensor(part_of(w_lo, 0), part_of(w_raw, 0), part_of(w_hi, 0).bitcast(F32),
                              ALU.subtract).then_inc(first_lo, 1)
            dve.wait_ge(mix_ready, 1)
            for k in range(KT):
                dve.wait_ge(x_hi, 2 * (k // 2) + 2)
                dve.scalar_tensor_tensor(tok_lo[:, k, :], ps[:, 4 + k // 2, (k % 2) * T:(k % 2 + 1) * T],
                                         cols_mix[:, k:k + 1], tok_hi[:, k, :].bitcast(F32), ALU.mult,
                                         ALU.subtract).then_inc(x_lo, 1)
            dve.wait_ge(hi_ready[0], 1)
            dve.tensor_tensor(part_of(w_lo, 1), part_of(w_raw, 1), part_of(w_hi, 1).bitcast(F32),
                              ALU.subtract).then_inc(lo_ready[0], 1)
            dve.wait_ge(skip_in, 16)
            dve.tensor_copy(rows_skip[0:n_skip, :].rearrange("p (j n) -> p j n", j=2),
                            skip2[0:n_skip, :].unsqueeze(2).to_broadcast([n_skip, 2, SHD])).then_inc(skip_row, 1)
            dve.wait_ge(rows_turned, 1)
            at = [0]

            def take(dst, n, scale):
                dve.tensor_scalar(dst, ps[:, 3, at[0]:at[0] + n], scale, None, ALU.mult).then_inc(params_ready, 1)
                at[0] += n

            take(cols_conv[:].rearrange("p a c -> p (a c)"), n_conv, 0.5)
            take(cols_gate[:, 0:3 * KT], 3 * KT, 0.5)
            take(cols_gate[:, 3 * KT:n_gate], n_gate - 3 * KT, 1.0)
            take(cols_skip[:], n_skip, 1.0)
            for j in range(4):
                take(cols_up[:, j, 0:FT], FT, 0.5)
                take(cols_up[:, j, FT:2 * FT], FT, 1.0)

            def softplus():
                v, m, e, s_, q, p = dt_w
                steps = [0]

                def step(ins):
                    steps[0] += 1
                    ins.then_inc(dt_step, 1)
                    dve.wait_ge(dt_step, steps[0])

                dve.wait_ge(dtp_in, 32)
                dve.wait_ge(dt_turned, 1)
                step(dve.tensor_tensor(v[:], ps[:, 6, 0:NT * SHEADS].rearrange("p (t h) -> p t h", t=NT),
                                       dt_rows[:, 0:1, :].to_broadcast([P, NT, SHEADS]), ALU.add))
                step(dve.scalar_tensor_tensor(m[:], v[:], -1.0, v[:], ALU.mult, ALU.min))
                dve.wait_ge(dt_exp, 1)
                step(dve.tensor_scalar(m[:], e[:], 2.0, None, ALU.add))
                step(dve.reciprocal(q[:], m[:]))
                step(dve.tensor_tensor(s_[:], e[:], q[:], ALU.mult))
                step(dve.tensor_tensor(q[:], s_[:], s_[:], ALU.mult))
                step(dve.tensor_scalar(p[:], q[:], 1.0 / 17, None, ALU.mult))
                for n in (15, 13, 11, 9, 7, 5, 3):
                    step(dve.scalar_tensor_tensor(p[:], p[:], 1.0 / n, q[:], ALU.add, ALU.mult))
                step(dve.scalar_tensor_tensor(p[:], p[:], 1.0, s_[:], ALU.add, ALU.mult))
                step(dve.tensor_scalar(m[:], v[:], 0.0, None, ALU.max))
                step(dve.scalar_tensor_tensor(dt_s[:], p[:], 2.0, m[:], ALU.mult, ALU.add))
                dve.wait_ge(a_exp, 1)
                step(dve.tensor_scalar(a_neg[:], a_neg[:], -1.0, None, ALU.mult))
                step(dve.tensor_tensor(da_s[:], dt_s[:], a_neg[:].unsqueeze(1).to_broadcast([P, NT, SHEADS]),
                                       ALU.mult))
                assert steps[0] == 19

            def take_decay_sums():
                dve.wait_ge(acs_mm, 1)
                dve.tensor_copy(acs_s[:].rearrange("p t h -> p (t h)"), ps[:, 7, 0:NT * SHEADS]).then_inc(acs_ready, 1)
                dve.tensor_copy(acs_row[0:SHEADS, :], ps[0:SHEADS, 7, T:2 * T]).then_inc(acs_ready, 1)

            def scan_out(n):
                dve.wait_ge(y_mm, n)
                for c in range(GT):
                    dve.scalar_tensor_tensor(y_sum[:, c, :], conv_o[:, 2 + c, :],
                                             cols_skip[:, bass.ds(GT * n - GT + c, 1)],
                                             ps[:, 6 + c // 2, (c % 2) * T:(c % 2 + 1) * T], ALU.mult,
                                             ALU.add).then_inc(y_step, 1)
                dve.wait_ge(y_step, GT * n)
                dve.scalar_tensor_tensor(v_ssm[:, bass.ds(GT * n - GT, GT), :], z_act[:], 0.5, y_sum[:], ALU.mult,
                                         ALU.mult).then_inc(v_ready, 1)

            def group(g, first=False):
                r = 2 * g

                def convolve(s):
                    dve.wait_ge(bank_free[s], r + 2)
                    for tap in range(TAPS - 1):
                        for j in range(2):
                            n = 18 * g + 6 * s + 2 * tap + j
                            if tap:
                                dve.wait_ge(conv_step, n - 1)
                            dve.scalar_tensor_tensor(
                                conv_a[:, s, j, :], pad_x[:, s, j, tap:tap + T],
                                cols_conv[:, tap, bass.ds(conv_tile(s, j, g), 1)], conv_a[:, s, j, :], ALU.mult,
                                ALU.add).then_inc(conv_step, 1)

                def activate(s):
                    dve.wait_ge(conv_tanh, 3 * g + s + 1)
                    dve.scalar_tensor_tensor(conv_o[:, 2 * s:2 * s + 2, :], tanh_a[:, s], 1.0, conv_a[:, s], ALU.add,
                                             ALU.mult).then_inc(conv_done, 1)

                def silu_z(s):
                    dve.wait_ge(z_tanh, 2 * g + s + 1)
                    dve.scalar_tensor_tensor(z_act[:, 2 * s:2 * s + 2, :], tanh_a[:, s], 1.0, halves(s), ALU.add,
                                             ALU.mult).then_inc(bank_free[s], 1)
                    split_lo(dve, r + 2, s)

                convolve(0)
                if not first:
                    split_lo(dve, r + 1, 0)
                activate(0)
                if first:
                    dve.wait_ge(dt_mm, 1)
                    dve.tensor_copy(dt_raw[0:SHEADS, :], ps[0:SHEADS, 4, 0:T]).then_inc(dt_copied, 1)
                    dve.wait_ge(bias_mm, 1)
                    dve.tensor_copy(bias_row[0:HEADS, :], ps[0:HEADS, 5, 0:BIAS_W]).then_inc(bias_copied, 1)
                    softplus()
                convolve(1)
                if not first:
                    split_lo(dve, r + 1, 1)
                    scan_out(g)
                activate(1)
                if first:
                    take_decay_sums()
                convolve(2)
                if not first:
                    split_lo(dve, r + 1, 2)
                activate(2)
                silu_z(0)
                silu_z(1)
                dve.wait_ge(seg_ready, 2 * g + 2)
                for c in (slice(0, P), slice(T, T + P)):
                    dve.tensor_scalar(decay[:, :, c], decay[:, :, c], 0.0, None, ALU.min).then_inc(seg_clamped, 1)
                dve.wait_ge(xg_turned, g + 1)
                for t in range(NT):
                    dve.tensor_tensor(x_dt[:, t, :].rearrange("p (h n) -> p h n", n=SHD),
                                      ps[:, 3 + t, :].rearrange("p (h n) -> p h n", n=SHD),
                                      dt_s[:, t, bass.ds(HPG * g, HPG)].unsqueeze(2).to_broadcast([P, HPG, SHD]),
                                      ALU.mult).then_inc(xdt_ready, 1)
                dve.wait_ge(cb_mm, g + 1)
                dve.tensor_tensor(cb[:], ps[:, 5, 0:3 * P], cb_mask, ALU.mult).then_inc(cb_masked, 1)
                dve.wait_ge(bank_free[2], r + 3)
                gate(g1[:, bass.ds(2 * g, 2), :], tanh_a[:, 2], g1_ready)
                split_lo(dve, r + 2, 2)
                dve.wait_ge(cb_masked, g + 1)
                dve.wait_ge(decay_ready, g + 1)
                dve.tensor_tensor(decay[:], decay[:], cb[:].unsqueeze(1).to_broadcast([P, HPG, 3 * P]),
                                  ALU.mult).then_inc(decay_cb, 1)

            group(0, first=True)
            with dve.Fori(1, GROUPS) as g:
                group(g)

            def mem_low(j):
                dve.wait_ge(m_hi, j + 1)
                two = slice(2 * j, 2 * j + 2)
                dve.tensor_tensor(me_lo[:, two, :], halves(mem_bank(j)), me_hi[:, two, :].bitcast(F32),
                                  ALU.subtract).then_inc(m_lo, 1)

            def heads(i, first=False):
                r = RB + i
                dve.wait_ge(gemm_done[0], r + 1)
                dve.tensor_copy(k_t[:], halves(0)).then_inc(bank_free[0], 1)
                split_lo(dve, r + 1, 0)
                if not first:
                    dve.wait_ge(p_turned, 2 * i)
                    dve.tensor_copy(prob_t[:, 1, :], ps[:, 6, 0:3 * P]).then_inc(pt_ready, 1)
                split_lo(dve, r + 1, 1)
                if first:
                    scan_out(GROUPS)
                    dve.wait_ge(bias_in, 32)
                    dve.wait_ge(v_ready, GROUPS)
                else:
                    dve.wait_ge(oa_hi_s, i)
                    last = bass.ds(2 * (i - 1), 2)
                    dve.tensor_tensor(oa_lo[:, last, :], halves(7), oa_hi[:, last, :].bitcast(F32),
                                      ALU.subtract).then_inc(oa_lo_s, 1)
                dve.wait_ge(s_mm, i + 1)
                dve.tensor_tensor(prob[:], ps[:, 3:5, 0:3 * P], bias_t[:, bass.ds(2 * i, 2), :],
                                  ALU.add).then_inc(s_biased, 1)
                dve.wait_ge(s_biased, i + 1)
                dve.tensor_reduce(soft[:, 0, 0:2], prob[:, :, 0:P], AX, ALU.max).then_inc(s_max, 1)
                dve.tensor_reduce(soft[:, 0, 2:4], prob[:, :, P:3 * P], AX, ALU.max).then_inc(s_max, 1)
                dve.wait_ge(s_max, 2 * i + 2)
                dve.tensor_scalar(soft[:, 1, :], soft[:, 0, :], -1.0, None, ALU.mult).then_inc(s_neg, 1)
                dve.wait_ge(p_exp, 4 * i + 4)
                dve.reciprocal(soft[:, 3, :], soft[:, 2, :]).then_inc(p_rec, 1)
                dve.wait_ge(p_rec, i + 1)
                for a in range(2):
                    for t in range(NT):
                        part = prob[:, a, 0:P] if t == 0 else prob[:, a, P:3 * P]
                        dve.tensor_scalar(part, part, soft[:, 3, 2 * t + a:2 * t + a + 1], None,
                                          ALU.mult).then_inc(p_norm, 1)
                if first:
                    for j in range(3):
                        mem_low(j)
                split_lo(dve, r + 1, 2)

            heads(0, first=True)
            with dve.Fori(1, 4) as i:
                heads(i)
            mem_low(3)

            def low(bank, hi, lo, ready, n, done):
                dve.wait_ge(ready, n)
                dve.tensor_tensor(lo[:], halves(bank), hi[:].bitcast(F32), ALU.subtract).then_inc(done, 1)

            def mem_head(i, first=False):
                r = RC + i
                low(0, qm_hi, qm_lo, qm_hi_s, i + 1, bank_free[0])
                if not first:
                    low(4, mprob_hi, mprob_lo, mpt_hi_s, i, mpt_ready)
                split_lo(dve, r + 1, 0)
                if first:
                    dve.wait_ge(p_turned, 8)
                    dve.tensor_copy(prob_t[:, 1, :], ps[:, 6, 0:3 * P]).then_inc(pt_ready, 1)
                    dve.wait_ge(group_mm, 1)
                    dve.tensor_scalar(group_rstd[:], ps[:, 3, 0:NT * GROUPS], 1.0 / GC, EPS, ALU.mult,
                                      ALU.add).then_inc(group_var, 1)
                low(1, km_hi, km_lo, km_hi_s, i + 1, bank_free[1])
                split_lo(dve, r + 1, 1)
                if first:
                    dve.wait_ge(oa_hi_s, 4)
                    dve.tensor_tensor(oa_lo[:, KT - 2:KT, :], halves(7), oa_hi[:, KT - 2:KT, :].bitcast(F32),
                                      ALU.subtract).then_inc(oa_lo_s, 1)
                    dve.wait_ge(rstd_g_ready, 1)
                else:
                    dve.wait_ge(om_hi_s, i)
                    last = bass.ds(2 * (i - 1), 2)
                    dve.tensor_tensor(om_lo[:, last, :], halves(5), om_hi[:, last, :].bitcast(F32),
                                      ALU.subtract).then_inc(om_lo_s, 1)
                for c in range(GT):
                    dve.scalar_tensor_tensor(o_tmp[:, c, :], v_ssm[:, bass.ds(GT * i + c, 1), :].squeeze(1),
                                             cols_gate[:, bass.ds(3 * KT + GT * i + c, 1)],
                                             rstd_g[:, bass.ds(i, 1), :].squeeze(1), ALU.mult,
                                             ALU.mult).then_inc(norm_step, 1)
                dve.wait_ge(os_hi_s, i + 1)
                four = bass.ds(GT * i, GT)
                dve.tensor_tensor(os_lo[:, four, :], o_tmp[:], os_hi[:, four, :].bitcast(F32),
                                  ALU.subtract).then_inc(os_lo_s, 1)
                low(2, vm_hi, vm_lo, vm_hi_s, i + 1, bank_free[2])
                dve.wait_ge(ms_mm, i + 1)
                dve.tensor_reduce(msoft[:, 0, :], halves(3), AX, ALU.max).then_inc(ms_max, 1)
                dve.wait_ge(ms_max, i + 1)
                dve.tensor_scalar(msoft[:, 1, :], msoft[:, 0, :], -(MDH ** -0.5), None, ALU.mult).then_inc(ms_neg, 1)
                dve.wait_ge(mp_exp, 2 * i + 2)
                dve.reciprocal(msoft[:, 3, :], msoft[:, 2, :]).then_inc(mp_rec, 1)
                dve.wait_ge(mp_rec, i + 1)
                for t in range(NT):
                    dve.tensor_scalar(mprob[:, t, :], mprob[:, t, :], msoft[:, 3, t:t + 1], None,
                                      ALU.mult).then_inc(mp_norm, 1)
                split_lo(dve, r + 1, 2)

            mem_head(0, first=True)
            with dve.Fori(1, 4) as i:
                mem_head(i)

            def ssm_columns(i, first=False):
                r = RD + i
                split_lo(dve, r + 1, 0)
                if first:
                    low(4, mprob_hi, mprob_lo, mpt_hi_s, 4, mpt_ready)
                dve.wait_ge(gemm_done[1], r + 1)
                for j in range(2):
                    tile = bass.ds(2 * i + j, 1)
                    dve.tensor_tensor(merged[:, tile, :], ps[:, j:j + 1, 0:T], g1[:, tile, :],
                                      ALU.mult).then_inc(bank_free[j], 1)
                split_lo(dve, r + 1, 1)
                if first:
                    dve.wait_ge(om_hi_s, 4)
                    dve.tensor_tensor(om_lo[:, KT - 2:KT, :], halves(5), om_hi[:, KT - 2:KT, :].bitcast(F32),
                                      ALU.subtract).then_inc(om_lo_s, 1)
                dve.wait_ge(bank_free[2], r + 2)
                gate(g0[:, bass.ds(2 * i, 2), :], tanh_d[:], g0_ready)
                split_lo(dve, r + 1, 2)

            ssm_columns(0, first=True)
            with dve.Fori(1, 4) as i:
                ssm_columns(i)

            dve.wait_ge(g0_ready, 4)
            with dve.Fori(0, 4) as i:
                r = RE + i
                two = bass.ds(2 * i, 2)
                dve.wait_ge(gemm_done[0], r + 1)
                dve.tensor_tensor(e_attn[:], halves(0), g0[:, two, :], ALU.mult).then_inc(bank_free[0], 1)
                split_lo(dve, r + 1, 0)
                dve.wait_ge(bank_free[0], r + 2)
                dve.tensor_tensor(e_attn[:], e_attn[:], merged[:, two, :], ALU.add).then_inc(e_step, 1)
                dve.wait_ge(bank_free[1], r + 2)
                gate(e_gate[:], tanh_e[:], e_step)
                split_lo(dve, r + 1, 1)
                dve.wait_ge(e_step, 2 * i + 2)
                dve.wait_ge(gemm_done[2], r + 1)
                dve.tensor_tensor(e_mem[:], halves(2), e_gate[:], ALU.mult).then_inc(bank_free[2], 1)
                dve.wait_ge(bank_free[2], r + 2)
                dve.tensor_tensor(e_sum[:], e_attn[:], e_mem[:], ALU.add).then_inc(e_summed, 1)
                dve.wait_ge(mg_hi_s, i + 1)
                dve.tensor_tensor(mg_lo[:, two, :], e_sum[:], mg_hi[:, two, :].bitcast(F32),
                                  ALU.subtract).then_inc(mg_lo_s, 1)
                split_lo(dve, r + 1, 2)

            def add_h(r, s, c):
                dve.wait_ge(gemm_done[s], r + 1)
                part = h_nat[:, :, c * CW:(c + 1) * CW]
                dve.tensor_tensor(part, halves(s), part, ALU.add).then_inc(bank_free[s], 1)

            def h_low(c):
                dve.wait_ge(h_hi, 2 * c + 2)
                for j in range(2):
                    k = 2 * c + j
                    dve.scalar_tensor_tensor(tok_lo[:, k, :], ps[:, 4 + c, j * T:(j + 1) * T],
                                             cols_gate[:, 5 * KT + k:5 * KT + k + 1], tok_hi[:, k, :].bitcast(F32),
                                             ALU.mult, ALU.subtract).then_inc(h_lo, 1)

            dve.memset(pad_g[:, :, 0:FTAPS - 1], 0.0).then_inc(pads_zero, 1)
            dve.memset(pad_u[:, :, 0:FTAPS - 1], 0.0).then_inc(pads_zero, 1)
            dve.wait_ge(x_again, 16)
            add_h(RF, 0, 0)
            add_h(RF, 1, 1)
            split_lo(dve, RF + 1, 0)
            split_lo(dve, RF + 1, 1)
            add_h(RF, 2, 2)
            h_low(0)
            h_low(1)
            h_low(2)
            split_lo(dve, RF + 1, 2)
            add_h(RF + 1, 0, 3)
            h_low(3)
            dve.wait_ge(h_spread, 1)
            dve.tensor_copy(rstd_b[:], ps[:, 3, 0:T]).then_inc(rstd_b_ready, 1)
            dve.wait_ge(rstd_b_ready, 1)
            dve.wait_ge(pads_zero, 2)

            def ffn(f, sa, ra, sb, rb, early, after_gate, after_up, final=False):
                def pad_with(s, r, pad, splits):
                    dve.wait_ge(gemm_done[s], r + 1)
                    dve.tensor_tensor(pad[:, :, FTAPS - 1:], halves(s), rstd_b[:].unsqueeze(1).to_broadcast([P, 2, T]),
                                      ALU.mult).then_inc(bank_free[s], 1)
                    for rr, ss in splits:
                        split_lo(dve, rr, ss)

                def convolve(n, pad, conv, tile):
                    for tap in range(FTAPS - 1):
                        for j in range(2):
                            m = 8 * f + 4 * n + 2 * tap + j
                            if tap:
                                dve.wait_ge(f_step, m - 1)
                            else:
                                dve.wait_ge(conv_begun, 4 * f + 2 * n + j + 1)
                            dve.scalar_tensor_tensor(conv[:, j, :], pad[:, j, tap:tap + T],
                                                     cols_up[:, tap, bass.ds(tile + 2 * f + j, 1)], conv[:, j, :],
                                                     ALU.mult, ALU.add).then_inc(f_step, 1)

                pad_with(sa, ra, pad_g, early)
                convolve(0, pad_g, conv_g, 0)
                pad_with(sb, rb, pad_u, [])
                dve.wait_ge(g_tanh, f + 1)
                dve.scalar_tensor_tensor(silu_g[:], tanh_g[:], 1.0, conv_g[:], ALU.add, ALU.mult).then_inc(g_silu, 1)
                for rr, ss in after_gate:
                    split_lo(dve, rr, ss)
                convolve(1, pad_u, conv_u, FT)
                dve.wait_ge(g_silu, f + 1)
                dve.wait_ge(f_step, 8 * f + 8)
                dve.tensor_tensor(hid[:], silu_g[:], conv_u[:], ALU.mult).then_inc(hid_done, 1)
                for rr, ss in after_up:
                    split_lo(dve, rr, ss)
                dve.wait_ge(hid_hi_s, f + 1)
                hi, lo = (last_hi, last_lo) if final else (hid_hi, hid_lo)
                dve.tensor_tensor(lo[:], hid[:], hi[:].bitcast(F32), ALU.subtract).then_inc(hid_lo_s, 1)

            ffn(0, 1, RF + 1, 2, RF + 1, [(RG, 0)], [(RG, 1)], [])
            with dve.Fori(1, F_STEPS - 1) as f:
                r = f + (RG - 1)
                ffn(f, 0, r, 1, r, [(r, 2)], [(r + 1, 0)], [(r + 1, 1)])
            r = RG + F_STEPS - 2
            ffn(F_STEPS - 1, 0, r, 1, r, [(r, 2)], [], [], final=True)
            for n in range(2 * NT):
                dve.wait_ge(down_done, n + 1)
                part = h_nat[:, n // 2, halfcols(n)]
                dve.tensor_tensor(part, ps[:, 4 + n, :], part, ALU.add).then_inc(y_added, 1)
            dve.wait_ge(late_gain, 16)
            for n in range(2 * NT):
                t = n // 2
                dve.wait_ge(y_rstd, t + 1)
                dve.scalar_tensor_tensor(h_sc[:, t, halfcols(n)], h_nat[:, t, halfcols(n)],
                                         stat[:, 7 + 2 * t:8 + 2 * t], gain_fin[:, halfcols(n)], ALU.mult,
                                         ALU.mult).then_inc(y_scaled, 1)

        @block.gpsimd
        def _(pool):
            def rstd(c, sumsq, var, done):
                for t in range(NT):
                    col = stat[:, c + t:c + t + 1]
                    pool.wait_ge(sumsq, t + 1)
                    pool.tensor_scalar(col, col, 1.0 / D, EPS, ALU.mult, ALU.add).then_inc(var, 1)
                    pool.wait_ge(var, t + 1)
                    pool.tensor_tensor(col, col, pow_c[:, 0:1], ALU.pow).then_inc(done, 1)

            def exponents(g):
                pool.wait_ge(acs_in, 16 * g + 16)
                heads = bass.ds(HPG * g, HPG)
                for t, c, first in ((0, slice(0, T), 0), (1, slice(T, T + P), P)):
                    pool.tensor_tensor(decay[:, :, c], acs_b[:, heads, first:T],
                                       acs_s[:, t, heads].unsqueeze(2).to_broadcast([P, HPG, T - first]),
                                       ALU.subtract).then_inc(seg_ready, 1)

            def squares(n):
                v = v_ssm[:, bass.ds(GT * n - GT, GT), :]
                pool.wait_ge(v_ready, n)
                pool.tensor_tensor(sq_v[:], v, v, ALU.mult).then_inc(sq_step, 1)
                pool.wait_ge(sq_step, 3 * n - 2)
                pool.tensor_tensor(sq_h[:], sq_v[:, 0:2, :], sq_v[:, 2:4, :], ALU.add).then_inc(sq_step, 1)
                pool.wait_ge(sq_step, 3 * n - 1)
                pool.tensor_tensor(sq_g[:, bass.ds(n - 1, 1), :], sq_h[:, 0:1, :], sq_h[:, 1:2, :],
                                   ALU.add).then_inc(sq_step, 1)

            pool.wait_ge(pow_set, 1)
            rstd(0, x_sumsq, x_var, x_rstd)
            pool.wait_ge(wdt_hi_s, 1)
            pool.tensor_tensor(wdt_lo[:], wdt_raw[:], wdt_hi[:].bitcast(F32), ALU.subtract).then_inc(wdt_lo_s, 1)
            split_lo(pool, 0, 1)
            split_lo(pool, 0, 2)
            for s in range(SLOTS):
                split_lo(pool, 1, s)
            pool.wait_ge(acs_ready, 2)
            exponents(0)
            with pool.Fori(1, GROUPS) as g:
                pool.wait_ge(y_mm, g)
                exponents(g)
                squares(g)
            rstd(2, m_sumsq, m_var, m_rstd)
            pool.wait_ge(m_gain_in, 16)
            for t in range(NT):
                row = mem_nat[:, t, :]
                pool.wait_ge(m_rstd, t + 1)
                pool.tensor_scalar(row, row, stat[:, 2 + t:3 + t], None, ALU.mult).then_inc(m_step, 1)
                pool.wait_ge(m_step, t + 1)
                pool.tensor_tensor(row, row, gain_mem[:], ALU.mult).then_inc(m_scaled, 1)
            squares(GROUPS)
            pool.wait_ge(group_var, 1)
            pool.tensor_tensor(group_rstd[:], group_rstd[:], pow_c[:], ALU.pow).then_inc(group_pow, 1)
            rstd(4, h_sumsq, h_var, h_rstd)
            split_lo(pool, RG + F_STEPS - 1, 0)
            for t in range(NT):
                a, b = stat[:, 6 + 2 * t:7 + 2 * t], stat[:, 7 + 2 * t:8 + 2 * t]
                pool.wait_ge(y_sumsq, 2 * t + 1)
                pool.tensor_scalar(a, a, 1.0 / D, EPS, ALU.mult, ALU.add).then_inc(y_var, 1)
                pool.wait_ge(y_sumsq, 2 * t + 2)
                pool.tensor_scalar(b, b, 1.0 / D, None, ALU.mult).then_inc(y_var, 1)
                pool.wait_ge(y_var, 3 * t + 2)
                pool.tensor_tensor(b, a, b, ALU.add).then_inc(y_var, 1)
                pool.wait_ge(y_var, 3 * t + 3)
                pool.tensor_tensor(b, b, pow_c[:, 0:1], ALU.pow).then_inc(y_rstd, 1)


_INS = ("x", "mem", "rel_bias", "mix_norm_g", "w_in", "b_gate", "ssm_conv_w", "ssm_conv_b", "ssm_dt_bias", "ssm_A_log",
        "ssm_D", "ssm_norm_g", "mem_norm_g", "w_mem_kv", "w_br_attn", "w_br_ssm", "w_br_mem", "w_out", "ffn_norm_g",
        "w_ffn_up", "ffn_conv_w", "ffn_conv_b", "w_ffn_down", "final_norm_g")


def kernel(**inputs):
    import concourse.bacc as bacc
    from concourse.bass_utils import run_bass_kernel_spmd

    nc = bacc.Bacc("TRN2", target_bir_lowering=False, num_devices=1, dynamic_dma_scratch_size=1024)
    arrays = {n: np.ascontiguousarray(inputs[n]) for n in _INS}
    arrays |= dict(zip(("square_table", "bucket_table", "one_row"), constants()))
    aps = [nc.dram_tensor(n, a.shape, mybir.dt.from_np(a.dtype), kind="ExternalInput").ap() for n, a in arrays.items()]
    out = nc.dram_tensor("out", (1, T, D), F32, kind="ExternalOutput").ap()
    build(nc, *aps, out)
    r = run_bass_kernel_spmd(nc, [arrays], core_ids=[0])
    return r.results[0]["out"]
```
